# Optimizing a Trainium2 kernel written in Bass

```python
import jax, jax.numpy as jnp
from jax import lax
import numpy as np

D_MODEL = 1024
BATCH = 1
SEQ = 256
DEPTH = 2
DEC_BATCH = 1
DEC_SEQ = 32
PAST_LEN = 256

CHUNK = 64
H_A = 4
DK_A = 128
DV_A = 128
H_B = 4
DK_B = 128
DV_B = 128
H_C = 8
DK_C = 128
DV_C = 128
CONV_W = 4
N_GROUPS = 4
EXP_PER_GROUP = 8
N_EXPERTS = N_GROUPS * EXP_PER_GROUP
TOP_K = 2
D_EXPERT = 512
MOE_BLOCK = 128
RMS_EPS = 1e-6
ROPE_BASE = 10000.0
N_AB = (DEPTH + 1) // 2
N_C = DEPTH // 2

AB_SPLITS = (H_A * DK_A, H_A * DK_A, H_A * DV_A, H_A * DV_A, H_A, H_A,
             H_B * DK_B, H_B * DK_B, H_B * DV_B, H_B * DV_B)
AB_IN = sum(AB_SPLITS)
AB_OUT = H_A * DV_A + H_B * DV_B
C_QKV = 2 * H_C * DK_C + H_C * DV_C
C_SPLITS = (C_QKV, H_C, H_C, H_C * DV_C)
C_IN = sum(C_SPLITS)
C_OUT = H_C * DV_C

kernel_name = "hybrid_mlstm_retention_gdn_hmoe_stream_step"

def split_cols(z, sizes):
    idx = np.cumsum(sizes)[:-1].tolist()
    return jnp.split(z, idx, axis=-1)

def rmsnorm(x, g):
    xf = x.astype(jnp.float32)
    y = xf * lax.rsqrt(jnp.mean(xf * xf, axis=-1, keepdims=True) + RMS_EPS)
    return (y * g.astype(jnp.float32)).astype(x.dtype)

def l2norm(x):
    return x * lax.rsqrt(jnp.sum(x * x, axis=-1, keepdims=True) + RMS_EPS)

def to_heads(z, h):
    b, t, _ = z.shape
    return z.reshape(b, t, h, -1).transpose(0, 2, 1, 3)

def merge_heads(z):
    b, h, t, d = z.shape
    return z.transpose(0, 2, 1, 3).reshape(b, t, h * d)

def to_chunks(a, L):
    b, h, t = a.shape[:3]
    return jnp.moveaxis(a.reshape(b, h, t // L, L, *a.shape[3:]), 2, 0)

def from_chunks(a):
    a = jnp.moveaxis(a, 0, 2)
    return a.reshape(a.shape[0], a.shape[1], -1, a.shape[-1])

def rotary(x, pos):
    half = x.shape[-1] // 2
    inv = ROPE_BASE ** (-jnp.arange(half, dtype=jnp.float32) / half)
    ang = pos.astype(jnp.float32)[:, None] * inv[None, :]
    cos, sin = jnp.cos(ang), jnp.sin(ang)
    x1, x2 = x[..., :half], x[..., half:]
    return jnp.concatenate([x1 * cos - x2 * sin, x1 * sin + x2 * cos], axis=-1)

def mlstm_scan(q, k, v, ig, lf, c0, n0, m0):
    L = min(CHUNK, q.shape[2])
    causal = jnp.tril(jnp.ones((L, L), dtype=bool))

    def step(carry, inp):
        c, n, m = carry
        qc, kc, vc, ic, fc = inp
        b = jnp.cumsum(fc, axis=-1)
        dmat = jnp.where(causal, b[..., :, None] - b[..., None, :] + ic[..., None, :], -jnp.inf)
        inter = b + m[..., None]
        m_t = jnp.maximum(inter, jnp.max(dmat, axis=-1))
        s = jnp.einsum('bhtd,bhsd->bhts', qc, kc) * jnp.exp(dmat - m_t[..., None])
        w_inter = jnp.exp(inter - m_t)
        num = w_inter[..., None] * jnp.einsum('bhtd,bhde->bhte', qc, c) + jnp.einsum('bhts,bhse->bhte', s, vc)
        den = w_inter * jnp.einsum('bhtd,bhd->bht', qc, n) + jnp.sum(s, axis=-1)
        h = num / jnp.maximum(jnp.abs(den), jnp.exp(-m_t))[..., None]
        m_new = m_t[..., -1]
        wk = jnp.exp(b[..., -1:] - b + ic - m_new[..., None])
        dec = jnp.exp(b[..., -1] + m - m_new)
        c_new = dec[..., None, None] * c + jnp.einsum('bhsd,bhse->bhde', kc * wk[..., None], vc)
        n_new = dec[..., None] * n + jnp.einsum('bhs,bhsd->bhd', wk, kc)
        return (c_new, n_new, m_new), h

    xs = tuple(to_chunks(a, L) for a in (q, k, v, ig, lf))
    (c1, n1, m1), h = lax.scan(step, (c0, n0, m0), xs)
    return from_chunks(h), c1, n1, m1

def retention_scan(q, k, v, s0):
    L = min(CHUNK, q.shape[2])
    lg = jnp.log(1.0 - 2.0 ** (-5.0 - jnp.arange(H_B, dtype=jnp.float32)))
    idx = jnp.arange(L, dtype=jnp.float32)
    rel = idx[:, None] - idx[None, :]
    causal = rel >= 0
    dmat = jnp.where(causal, jnp.exp(jnp.where(causal, rel, 0.0) * lg[:, None, None]), 0.0)
    q_dec = jnp.exp((idx + 1.0) * lg[:, None])
    k_dec = jnp.exp((L - 1.0 - idx) * lg[:, None])
    c_dec = jnp.exp(L * lg)

    def step(s, inp):
        qc, kc, vc = inp
        att = jnp.einsum('bhtd,bhsd->bhts', qc, kc) * dmat
        o = jnp.einsum('bhts,bhse->bhte', att, vc) + q_dec[:, :, None] * jnp.einsum('bhtd,bhde->bhte', qc, s)
        s = c_dec[:, None, None] * s + jnp.einsum('bhsd,bhse->bhde', kc * k_dec[:, :, None], vc)
        return s, o

    s1, o = lax.scan(step, s0, tuple(to_chunks(a, L) for a in (q, k, v)))
    return from_chunks(o), s1

def gdn_scan(q, k, v, beta, g, s0):
    L = min(CHUNK, q.shape[2])
    lower = jnp.tril(jnp.ones((L, L), dtype=bool))
    strict = jnp.tril(jnp.ones((L, L), dtype=bool), -1)
    eye = jnp.eye(L, dtype=jnp.float32)

    def step(s, inp):
        qc, kc, vc, bc, gc = inp
        G = jnp.cumsum(gc, axis=-1)
        diff = G[..., :, None] - G[..., None, :]
        gam = jnp.where(lower, jnp.exp(jnp.where(lower, diff, 0.0)), 0.0)
        a = jnp.where(strict, bc[..., :, None] * jnp.einsum('bhid,bhjd->bhij', kc, kc) * gam, 0.0)
        tri = a + eye
        eg = jnp.exp(G)
        u = lax.linalg.triangular_solve(tri, vc * bc[..., None], left_side=True, lower=True, unit_diagonal=True)
        w = lax.linalg.triangular_solve(tri, kc * (bc * eg)[..., None], left_side=True, lower=True, unit_diagonal=True)
        v_new = u - jnp.einsum('bhld,bhde->bhle', w, s)
        o = (jnp.einsum('bhld,bhde->bhle', qc * eg[..., None], s)
             + jnp.einsum('bhij,bhje->bhie', jnp.einsum('bhid,bhjd->bhij', qc, kc) * gam, v_new))
        g_last = G[..., -1]
        s = (jnp.exp(g_last)[..., None, None] * s
             + jnp.einsum('bhld,bhle->bhde', kc * jnp.exp(g_last[..., None] - G)[..., None], v_new))
        return s, o

    s1, o = lax.scan(step, s0, tuple(to_chunks(a, L) for a in (q, k, v, beta, g)))
    return from_chunks(o), s1

def ab_mixer(h, pos, w_in, gate_bias, w_out, norm_a, norm_b, c0, n0, m0, s0):
    f32 = jnp.float32
    qa, ka, va, oa, ia, fa, qb, kb, vb, gb = split_cols(h @ w_in, AB_SPLITS)
    gate_bias = gate_bias.astype(f32)
    qa = to_heads(qa, H_A).astype(f32)
    ka = to_heads(ka, H_A).astype(f32) * DK_A ** -0.5
    va = to_heads(va, H_A).astype(f32)
    ig = (ia.astype(f32) + gate_bias[:H_A]).transpose(0, 2, 1)
    lf = jax.nn.log_sigmoid(fa.astype(f32) + gate_bias[H_A:]).transpose(0, 2, 1)
    ya, c1, n1, m1 = mlstm_scan(qa, ka, va, ig, lf, c0.astype(f32), n0.astype(f32), m0.astype(f32))
    ya = rmsnorm(ya, norm_a) * jax.nn.sigmoid(to_heads(oa, H_A).astype(f32))
    qb = rotary(to_heads(qb, H_B).astype(f32), pos)
    kb = rotary(to_heads(kb, H_B).astype(f32), pos) * DK_B ** -0.5
    yb, s1 = retention_scan(qb, kb, to_heads(vb, H_B).astype(f32), s0.astype(f32))
    yb = rmsnorm(yb, norm_b) * jax.nn.silu(to_heads(gb, H_B).astype(f32))
    y = jnp.concatenate([merge_heads(ya), merge_heads(yb)], axis=-1).astype(h.dtype)
    return y @ w_out, c1, n1, m1, s1

def gdn_mixer(h, conv_buf, w_in, conv_w, a_log, dt_bias, norm_c, w_out, s0):
    f32 = jnp.float32
    qkv, bt, at, gt = split_cols(h @ w_in, C_SPLITS)
    ext = jnp.concatenate([conv_buf.astype(qkv.dtype), qkv], axis=1)
    conv = lax.conv_general_dilated(ext, conv_w[:, None, :].astype(ext.dtype), (1,), 'VALID',
                                    dimension_numbers=('NWC', 'WIO', 'NWC'), feature_group_count=C_QKV)
    q, k, v = split_cols(jax.nn.silu(conv.astype(f32)), (H_C * DK_C, H_C * DK_C, H_C * DV_C))
    q = l2norm(to_heads(q, H_C)) * DK_C ** -0.5
    k = l2norm(to_heads(k, H_C))
    v = to_heads(v, H_C)
    beta = jax.nn.sigmoid(bt.astype(f32)).transpose(0, 2, 1)
    g = (-jnp.exp(a_log.astype(f32)) * jax.nn.softplus(at.astype(f32) + dt_bias.astype(f32))).transpose(0, 2, 1)
    y, s1 = gdn_scan(q, k, v, beta, g, s0.astype(f32))
    y = rmsnorm(y, norm_c) * jax.nn.silu(to_heads(gt, H_C).astype(f32))
    y = merge_heads(y).astype(h.dtype)
    return y @ w_out, s1, ext[:, -(CONV_W - 1):, :]

def hier_moe(x, w_grp, b_grp, w_exp, b_exp, w_gate, w_up, w_down):
    f32 = jnp.float32
    n, d = x.shape
    xf = x.astype(f32)
    p_grp = jax.nn.softmax(xf @ w_grp.astype(f32) + b_grp.astype(f32), axis=-1)
    grp = jnp.argmax(p_grp, axis=-1)
    p_sel = jnp.take_along_axis(p_grp, grp[:, None], axis=-1)
    fine = (xf @ w_exp.astype(f32) + b_exp.astype(f32)).reshape(n, N_GROUPS, EXP_PER_GROUP)
    fine = jnp.take_along_axis(fine, grp[:, None, None], axis=1)[:, 0]
    w_top, e_top = lax.top_k(jax.nn.softmax(fine, axis=-1), TOP_K)
    gate = p_sel * w_top / jnp.sum(w_top, axis=-1, keepdims=True)
    eid = (grp[:, None] * EXP_PER_GROUP + e_top).reshape(-1)
    tok = jnp.repeat(jnp.arange(n), TOP_K)
    gw = gate.reshape(-1)
    order = jnp.argsort(eid)
    eid_s, tok_s, gw_s = eid[order], tok[order], gw[order]
    counts = jnp.bincount(eid, length=N_EXPERTS)
    padded = ((counts + MOE_BLOCK - 1) // MOE_BLOCK) * MOE_BLOCK
    start = jnp.cumsum(counts) - counts
    pend = jnp.cumsum(padded)
    pstart = pend - padded
    dest = pstart[eid_s] + (jnp.arange(n * TOP_K) - start[eid_s])
    n_blocks = -(-(n * TOP_K) // MOE_BLOCK) + N_EXPERTS
    rows = jnp.zeros((n_blocks * MOE_BLOCK, d), x.dtype).at[dest].set(x[tok_s])
    block_exp = jnp.minimum(jnp.searchsorted(pend, jnp.arange(n_blocks) * MOE_BLOCK, side='right'), N_EXPERTS - 1)

    def expert_block(args):
        xb, e = args
        hb = jax.nn.silu(xb @ w_gate[e]) * (xb @ w_up[e])
        return hb @ w_down[e]

    out_rows = lax.map(expert_block, (rows.reshape(n_blocks, MOE_BLOCK, d), block_exp)).reshape(-1, d)
    y = out_rows[dest] * gw_s[:, None].astype(x.dtype)
    return jax.ops.segment_sum(y, tok_s, num_segments=n)

def run_trunk(x, pos, mc, mn, mm, rs, gs, gconv, norm_mix, norm_ffn, norm_final,
              ab_w_in, ab_gate_bias, ab_w_out, ab_norm_a, ab_norm_b,
              c_w_in, c_conv_w, c_a_log, c_dt_bias, c_norm, c_w_out,
              moe_w_grp, moe_b_grp, moe_w_exp, moe_b_exp, moe_w_gate, moe_w_up, moe_w_down):
    b, t, d = x.shape
    c_l, n_l, m_l, r_l, g_l, cv_l = [], [], [], [], [], []
    for layer in range(DEPTH):
        j = layer // 2
        h = rmsnorm(x, norm_mix[layer])
        if layer % 2 == 0:
            out, c1, n1, m1, s1 = ab_mixer(h, pos, ab_w_in[j], ab_gate_bias[j], ab_w_out[j], ab_norm_a[j],
                                           ab_norm_b[j], mc[j], mn[j], mm[j], rs[j])
            c_l.append(c1); n_l.append(n1); m_l.append(m1); r_l.append(s1)
        else:
            out, s1, cv1 = gdn_mixer(h, gconv[j], c_w_in[j], c_conv_w[j], c_a_log[j], c_dt_bias[j],
                                     c_norm[j], c_w_out[j], gs[j])
            g_l.append(s1); cv_l.append(cv1)
        x = x + out
        h = rmsnorm(x, norm_ffn[layer])
        x = x + hier_moe(h.reshape(b * t, d), moe_w_grp[layer], moe_b_grp[layer], moe_w_exp[layer],
                         moe_b_exp[layer], moe_w_gate[layer], moe_w_up[layer], moe_w_down[layer]).reshape(b, t, d)
    y = rmsnorm(x, norm_final)
    return (y, jnp.stack(c_l), jnp.stack(n_l), jnp.stack(m_l), jnp.stack(r_l), jnp.stack(g_l), jnp.stack(cv_l))

def setup_inputs(seed: int = 0) -> dict:
    key = jax.random.key(seed)
    ks = list(jax.random.split(key, 40))
    f32 = jnp.float32

    def nrm(i, shape, scale):
        return scale * jax.random.normal(ks[i], shape, f32)

    dt = jnp.exp(jax.random.uniform(ks[30], (N_C, H_C), f32, np.log(1e-3), np.log(1e-1)))
    return {
        "x_prompt": nrm(0, (BATCH, SEQ, D_MODEL), 1.0),
        "x_sample": nrm(1, (DEC_BATCH, DEC_SEQ, D_MODEL), 1.0),
        "state_mlstm_c": nrm(2, (N_AB, DEC_BATCH, H_A, DK_A, DV_A), 0.2),
        "state_mlstm_n": nrm(3, (N_AB, DEC_BATCH, H_A, DK_A), 0.2),
        "state_mlstm_m": nrm(4, (N_AB, DEC_BATCH, H_A), 1.0),
        "state_ret": nrm(5, (N_AB, DEC_BATCH, H_B, DK_B, DV_B), 0.2),
        "state_gdn": nrm(6, (N_C, DEC_BATCH, H_C, DK_C, DV_C), 0.1),
        "state_gdn_conv": nrm(7, (N_C, DEC_BATCH, CONV_W - 1, C_QKV), 1.0),
        "norm_mix": 1.0 + nrm(8, (DEPTH, D_MODEL), 0.1),
        "norm_ffn": 1.0 + nrm(9, (DEPTH, D_MODEL), 0.1),
        "norm_final": 1.0 + nrm(10, (D_MODEL,), 0.1),
        "ab_w_in": nrm(11, (N_AB, D_MODEL, AB_IN), D_MODEL ** -0.5),
        "ab_gate_bias": jnp.concatenate([nrm(12, (N_AB, H_A), 0.1),
                                         3.0 + 3.0 * jax.random.uniform(ks[13], (N_AB, H_A), f32)], axis=-1),
        "ab_w_out": nrm(14, (N_AB, AB_OUT, D_MODEL), AB_OUT ** -0.5),
        "ab_norm_a": 1.0 + nrm(15, (N_AB, DV_A), 0.1),
        "ab_norm_b": 1.0 + nrm(16, (N_AB, DV_B), 0.1),
        "c_w_in": nrm(17, (N_C, D_MODEL, C_IN), D_MODEL ** -0.5),
        "c_conv_w": nrm(18, (N_C, CONV_W, C_QKV), CONV_W ** -0.5),
        "c_a_log": jnp.log(jax.random.uniform(ks[19], (N_C, H_C), f32, 1.0, 16.0)),
        "c_dt_bias": dt + jnp.log(-jnp.expm1(-dt)),
        "c_norm": 1.0 + nrm(20, (N_C, DV_C), 0.1),
        "c_w_out": nrm(21, (N_C, C_OUT, D_MODEL), C_OUT ** -0.5),
        "moe_w_grp": nrm(22, (DEPTH, D_MODEL, N_GROUPS), D_MODEL ** -0.5),
        "moe_b_grp": nrm(23, (DEPTH, N_GROUPS), 0.01),
        "moe_w_exp": nrm(24, (DEPTH, D_MODEL, N_EXPERTS), D_MODEL ** -0.5),
        "moe_b_exp": nrm(25, (DEPTH, N_EXPERTS), 0.01),
        "moe_w_gate": nrm(26, (DEPTH, N_EXPERTS, D_MODEL, D_EXPERT), D_MODEL ** -0.5),
        "moe_w_up": nrm(27, (DEPTH, N_EXPERTS, D_MODEL, D_EXPERT), D_MODEL ** -0.5),
        "moe_w_down": nrm(28, (DEPTH, N_EXPERTS, D_EXPERT, D_MODEL), D_EXPERT ** -0.5),
    }

def reference(x_prompt, x_sample, state_mlstm_c, state_mlstm_n, state_mlstm_m, state_ret, state_gdn,
              state_gdn_conv, norm_mix, norm_ffn, norm_final, ab_w_in, ab_gate_bias, ab_w_out, ab_norm_a,
              ab_norm_b, c_w_in, c_conv_w, c_a_log, c_dt_bias, c_norm, c_w_out, moe_w_grp, moe_b_grp,
              moe_w_exp, moe_b_exp, moe_w_gate, moe_w_up, moe_w_down):
    f32 = jnp.float32
    bp, tp, _ = x_prompt.shape
    ts = x_sample.shape[1]
    weights = (norm_mix, norm_ffn, norm_final, ab_w_in, ab_gate_bias, ab_w_out, ab_norm_a, ab_norm_b,
               c_w_in, c_conv_w, c_a_log, c_dt_bias, c_norm, c_w_out, moe_w_grp, moe_b_grp, moe_w_exp,
               moe_b_exp, moe_w_gate, moe_w_up, moe_w_down)
    (y_prompt, mlstm_c_prompt, mlstm_n_prompt, mlstm_m_prompt, ret_prompt, gdn_prompt,
     gdn_conv_prompt) = run_trunk(
        x_prompt, jnp.arange(tp),
        jnp.zeros((N_AB, bp, H_A, DK_A, DV_A), f32), jnp.zeros((N_AB, bp, H_A, DK_A), f32),
        jnp.zeros((N_AB, bp, H_A), f32), jnp.zeros((N_AB, bp, H_B, DK_B, DV_B), f32),
        jnp.zeros((N_C, bp, H_C, DK_C, DV_C), f32), jnp.zeros((N_C, bp, CONV_W - 1, C_QKV), x_prompt.dtype),
        *weights)
    (y_sample, mlstm_c_sample, mlstm_n_sample, mlstm_m_sample, ret_sample, gdn_sample,
     gdn_conv_sample) = run_trunk(
        x_sample, PAST_LEN + jnp.arange(ts), state_mlstm_c, state_mlstm_n, state_mlstm_m, state_ret,
        state_gdn, state_gdn_conv, *weights)
    return (y_prompt, y_sample, mlstm_c_prompt, mlstm_n_prompt, mlstm_m_prompt, ret_prompt, gdn_prompt,
            gdn_conv_prompt, mlstm_c_sample, mlstm_n_sample, mlstm_m_sample, ret_sample, gdn_sample,
            gdn_conv_sample)


_drawn_inputs = setup_inputs


def setup_inputs(seed=0):
    import zlib

    import numpy as np

    out = dict(_drawn_inputs(seed))
    spreads = {}
    factors = {}
    for name, (base, spread) in spreads.items():
        noise = np.random.default_rng([zlib.crc32(name.encode()), seed]).standard_normal(out[name].shape)
        drawn = base * np.exp(spread * noise) if base else spread * noise
        out[name] = __import__('jax').numpy.asarray(drawn.astype(out[name].dtype))
    for name, factor in factors.items():
        out[name] = (out[name] * factor).astype(out[name].dtype)
    return out
```

```python
from contextlib import ExitStack

import concourse.bass as bass
from concourse import mybir

F32 = mybir.dt.float32
I32 = mybir.dt.int32
ALU = mybir.AluOpType
ACT = mybir.ActivationFunctionType
X_AXIS = mybir.AxisListType.X

P = 128
D = 1024
KT = D // P
N_TOK = [128, 128, 32]
TILES = 3
PAD = 3
COL = [PAD, PAD + 128, 2 * PAD + 256]
COLS = 2 * PAD + 256 + 32
HEADS = 8
NEXP, NGRP, EPG, F = 32, 4, 8, 512
BLK = 64
MAX_BLOCKS = 44
EPS = 1e-6
BIG = 1e30

_SIZES = [("ident", 128), ("tri_incl", 128), ("tri_strict", 128), ("ones", 128), ("negmask", 128),
          ("strict", 128), ("merge", 7 * 128), ("merge1_t", 128),
          ("ret_decay", 512), ("rot_cos", 3 * 128), ("rot_sin", 3 * 128), ("ret_q", 4), ("ret_k", 8),
          ("ret_c", 8), ("iota_blk", BLK), ("iota_m99", 8), ("valid", 3), ("invalid", 3),
          ("thresh", 5), ("iota_list", MAX_BLOCKS), ("half_neg", 16)]
CONST = {}
_at = 0
for _n, _w in _SIZES:
    CONST[_n] = (_at, _w)
    _at += _w
CONST_COLS = _at


class Event:

    def __init__(self, sem):
        self.sem, self.made, self.seen = sem, 0, {}

    def mark(self, ins, by=1):
        self.made += by
        ins.then_inc(self.sem, by)

    def wait(self, eng, by=1):
        key = id(eng)
        self.seen[key] = self.seen.get(key, 0) + by
        eng.wait_ge(self.sem, self.seen[key])


class InOrder:

    def __init__(self, eng, event):
        self.eng, self.event = eng, event

    def __call__(self, ins, event=None):
        ev = event or self.event
        ev.mark(ins)
        self.eng.wait_ge(ev.sem, ev.made)


class Lane:

    def __init__(self, full, taken, banks):
        self.full, self.taken, self.banks = full, taken, banks
        self.filled = self.opened = 0

    def open(self, pe):
        if self.filled >= 2:
            pe.wait_ge(self.taken.sem, self.filled - 1)
        return self.banks[self.filled % 2]

    def close(self, ins):
        self.filled += 1
        self.full.mark(ins)

    def take(self, eng):
        self.full.wait(eng)
        self.opened += 1
        return self.banks[(self.opened - 1) % 2]


def trunk(nc, a):
    with ExitStack() as ctx:
        def sb(name, shape, dt=F32):
            return ctx.enter_context(nc.sbuf_tensor(name, shape, dt))

        def sem(name):
            return ctx.enter_context(nc.semaphore(name))

        def ev(name):
            return Event(sem(name))

        W = sb("W", [P, 6, 4096])
        const = sb("const", [P, CONST_COLS])
        zT = sb("zT", [P, 32, COLS])
        TM = sb("TM", [P, 32, P])
        X = sb("X", [P, TILES, D])
        HN = sb("HN", [P, TILES, D])
        HT = sb("HT", [P, KT, COLS])
        gain = sb("gain", [P, D])
        state2 = sb("state2", [P, HEADS, P])
        sm = sb("sm", [P, 436])
        small_w = sb("small_w", [P, KT, 36])
        cconv = sb("cconv", [P, 24, 7])
        tails = sb("tails", [P, 24, 6])
        hgain = sb("hgain", [P, 2, P])
        blocks_i = sb("blocks_i", [1, MAX_BLOCKS], I32)
        banks = [ctx.enter_context(nc.psum_tensor(f"bank{i}", [P, 512], F32)) for i in range(8)]

        def cst(name):
            o, w = CONST[name]
            return const[:, o:o + w]

        ident, ones, tri_incl, tri_strict = cst("ident"), cst("ones"), cst("tri_incl"), cst("tri_strict")
        ws = W[:, 4:6, :].rearrange("p s n -> p (s n)")
        hs = HN[:].rearrange("p t n -> p (t n)")
        zf = zT[:].rearrange("p c n -> p (c n)")

        def heads4(ap):
            return ap.rearrange("p (h n) -> p h n", n=P)

        qT = [heads4(ws[:, 512 * i:512 * i + 512]) for i in range(2)]
        kT = [heads4(ws[:, 1024 + 512 * i:1536 + 512 * i]) for i in range(2)]
        AT, TI, UI, YI = [[heads4(ws[:, 2048 + 1024 * j + 512 * i:2560 + 1024 * j + 512 * i])
                           for i in range(2)] for j in range(4)]
        GAM = [heads4(ws[:, 6144 + 512 * i:6656 + 512 * i]) for i in range(2)]
        Yout = ws[:, 7168:8192].rearrange("p (h n) -> p h n", n=P)
        state1 = hs[:, 0:1024].rearrange("p (h n) -> p h n", n=P)
        Sm, ST, kw, tmp = [heads4(hs[:, 1024 + 512 * i:1536 + 512 * i]) for i in range(4)]
        states = [state1, state1, state2[:, :, :]]
        xg = [zf[:, 512 * i:512 * i + 512].rearrange("p (k s) -> p k s", s=BLK) for i in range(2)]
        sg = [zf[:, 1024 + 256 * i:1280 + 256 * i] for i in range(2)]
        hid = [zf[:, 1536 + 256 * i:1792 + 256 * i] for i in range(2)]
        ys = [zf[:, 2048 + 1024 * i:3072 + 1024 * i] for i in range(2)]
        oh = [[zf[:, 4096 + 192 * (2 * i + j):4288 + 192 * (2 * i + j)].rearrange("p (t s) -> p t s", s=BLK)
               for j in range(2)] for i in range(2)]
        route = zf[:, 5000:7400]
        junk = zf[:, 8384:9408]
        convbuf = ws[:, 0:4 * (COLS - PAD)].rearrange("p (c n) -> p c n", c=4)
        rotc = cst("rot_cos").rearrange("p (t j n) -> p t j n", t=3, j=2)
        rots = cst("rot_sin").rearrange("p (t j n) -> p t j n", t=3, j=2)
        merge = cst("merge").rearrange("p (l n) -> p l n", n=P)
        yg = TM[:].rearrange("p c n -> p (c n)").rearrange("p (b k n) -> p b k n", b=2, k=2)

        _sm = [0]

        def small(w):
            _sm[0] += w
            return sm[:, _sm[0] - w:_sm[0]]

        sumsq, rstd = small(3), small(3)
        g16 = small(48)
        gb1, gb2 = small(8), small(8)
        lg = small(24)
        bcum = small(24)
        acol = small(24)
        t24a, t24b, t24c = small(24), small(24), small(24)
        beta = small(24)
        mprev = [small(4), small(4)]
        nstate = [small(4), small(4)]
        gm = small(8)
        gl = small(8)
        negg = small(4)
        ein, eout = small(32), small(32)
        den, den2 = small(4), small(4)
        hss, hrs = small(16), small(16)
        m1 = small(4)
        pw = [small(6)]
        dk = small(6)
        rb = small(36)
        slots_i = small(6).bitcast(I32).rearrange("p (k t) -> p k t", t=TILES)

        order = {e: ev(f"{e}_order") for e in ("dve", "act", "pool")}
        lanes = [Lane(ev("lane_dve_full"), ev("lane_dve_taken"), banks[0:2]),
                 Lane(ev("lane_act_full"), ev("lane_act_taken"), banks[2:4])]
        L0, L1 = lanes
        const_in, x_in = ev("const_in"), [ev(f"x_in{i}") for i in range(3)]
        gain_in, gain_used = ev("gain_in"), ev("gain_used")
        piece_in = [ev(f"piece_in{i}") for i in range(4)]
        piece_done = []
        small_in = [ev(f"small_in{i}") for i in range(4)]
        small_used = ev("small_used")
        x_ready, ss_ready, rs_ready, hn_ready = ev("x_ready"), ev("ss_ready"), ev("rs_ready"), ev("hn_ready")
        ht_dve, ht_act = ev("ht_dve"), ev("ht_act")
        names = ["z_ready", "tm_dve", "tm_act", "gate_exp_in", "gate_exp", "lf_ready", "diag_ready", "gm_ready",
                 "ein_ready", "eout_ready", "rot_ready", "qkT_dve", "qkT_act", "s_ready", "st_ready", "kw_ready",
                 "state_ready", "r_ready", "vn_ready", "am_ready", "p_ready", "a_ready", "at_ready", "tu_ready",
                 "yi_ready", "hss_ready", "hrs_ready", "y_ready", "yT_dve", "yT_act", "gexp_ready", "tile_done",
                 "conv_raw", "conv_in", "conv_done", "logits_exp_in", "logits_exp", "choice_ready", "nb_ready",
                 "nbb_ready", "list_ready", "blocks_ready", "qkn_ready", "state_done", "tails_done",
                 "hn_out", "gexp_ready2", "conv_used", "zero_rows", "rows_clear"]
        E = {n: ev(n) for n in names}
        state_in = ev("state_in")
        out_written, y_written = ev("out_written"), ev("y_written")
        moe = [dict(
            w_in=[sem(f"moe{l}_w_in{s}") for s in range(6)],
            gate_used=sem(f"moe{l}_gate_used"), up_used=sem(f"moe{l}_up_used"), down_used=sem(f"moe{l}_down_used"),
            onehot=sem(f"moe{l}_onehot"), gathered=sem(f"moe{l}_gathered"), xg=sem(f"moe{l}_xg"),
            gu=sem(f"moe{l}_gu"), silu=sem(f"moe{l}_silu"), hidden=sem(f"moe{l}_hidden"),
            down=sem(f"moe{l}_down"), ya=sem(f"moe{l}_ya"), yb=sem(f"moe{l}_yb"),
            step=sem(f"moe{l}_step"),
            stored=[sem(f"moe{l}_stored{u}") for u in range(2)],
            yg_in=[sem(f"moe{l}_yg_in{b}") for b in range(2)], yg_used=sem(f"moe{l}_yg_used"),
        ) for l in range(2)]

        states_out = sem("states_out")

        block = ctx.enter_context(nc.Block())

        def nblk_reg(eng):
            count = eng.value_load(blocks_i[0:1, MAX_BLOCKS - 1:MAX_BLOCKS], min_val=5, max_val=MAX_BLOCKS - 2)
            return eng.snap((count + 1) // 2)

        @block.tensor
        def _(pe):
            def mm(out, lhsT, rhs, start=True, stop=True):
                return nc.tensor.matmul(out, lhsT, rhs, start=start, stop=stop)

            def flip(out, src, n):
                return nc.tensor.transpose(out, src, ident[:n, :n])

            def transpose_tile(src, t, n):
                for g in range(2):
                    bank = lanes[g].open(pe)
                    for j in range(4):
                        last = flip(bank[:, j * P:j * P + n], src(4 * g + j)[:n], n)
                    lanes[g].close(last)

            def norm():
                for t in range(TILES):
                    hn_ready.wait(pe)
                    transpose_tile(lambda c: HN[:, t, c * P:c * P + P], t, N_TOK[t])
                ht_dve.wait(pe, 3)
                ht_act.wait(pe, 3)

            def small_projection(w, which, loads):
                small_in[which].wait(pe, 16 * loads)
                bank = L0.open(pe)
                for t in range(TILES):
                    n, c = N_TOK[t], COL[t]
                    for k in range(KT):
                        last = mm(bank[:n, 64 * t:64 * t + w], HT[:, k, c:c + n], small_w[:, k, 0:w],
                                  k == 0, k == KT - 1)
                L0.close(last)

            def input_projection():
                for p in range(8):
                    piece_in[p % 4].wait(pe, 16)
                    w = W[:, p % 4, :].rearrange("p (k n) -> p k n", k=KT)
                    for j in range(4):
                        bank = L1.open(pe)
                        for k in range(KT):
                            last = mm(bank[:, 0:COLS], w[:, k, j * P:j * P + P], HT[:, k, :], k == 0, k == KT - 1)
                        L1.close(last)
                    piece_done.append((L1.full.sem, L1.full.made))

            def output_projection():
                E["yT_dve"].wait(pe, 3)
                E["yT_act"].wait(pe, 3)
                for p in (8, 9):
                    piece_in[p % 4].wait(pe, 16)
                    w = W[:, p % 4, :].rearrange("p (k n) -> p k n", k=KT)
                    for t in range(TILES):
                        n, c = N_TOK[t], COL[t]
                        bank = L0.open(pe)
                        for k in range(KT):
                            last = mm(bank[:n, :], HT[:, k, c:c + n], w[:, k, :], k == 0, k == KT - 1)
                        L0.close(last)
                    piece_done.append((L0.full.sem, L0.full.made))

            def to_tokens(t, first):
                n, c = N_TOK[t], COL[t]
                for g in range(first, 8):
                    lane = lanes[g % 2]
                    bank = lane.open(pe)
                    for j in range(4):
                        last = flip(bank[:n, j * P:j * P + P], zT[:, 4 * g + j, c:c + n], P)
                    lane.close(last)
                E["tm_dve"].wait(pe)
                E["tm_act"].wait(pe)

            def row_broadcast(n):
                E["diag_ready"].wait(pe)
                bank = L0.open(pe)
                L0.close(mm(heads4(bank[:n, :])[:, :, :n], ones[:n, :n], tmp[:n, :, :n]))

            def last_row(t, w):
                n = N_TOK[t]
                sel = ident[:n, n - 1:n].to_broadcast([n, P])
                bank = L0.open(pe)
                L0.close(mm(bank[:, 0:w], sel, gm[:n, 0:w]))

            def half(t, f, q, k, vchunk, kwise, mlstm=False, delta=False):
                n = N_TOK[t]
                st = states[t]
                bank = L0.open(pe)
                for h in range(4):
                    last = mm(bank[:n, h * P:h * P + n], q(h), k(h))
                L0.close(last)
                if delta:
                    bank = L0.open(pe)
                    for h in range(4):
                        last = mm(bank[:n, h * P:h * P + P], k(h), st[:, 4 * f + h, :])
                    L0.close(last)
                E["s_ready"].wait(pe)
                bank = L1.open(pe)
                for h in range(4):
                    last = flip(bank[:n, h * P:h * P + n], Sm[:n, h, :n], n)
                L1.close(last)
                bank = L0.open(pe)
                for h in range(4):
                    last = mm(bank[:n, h * P:h * P + P], q(h), st[:, 4 * f + h, :])
                L0.close(last)
                if mlstm:
                    bank = L0.open(pe)
                    for h in range(4):
                        last = mm(bank[:n, h:h + 1], q(h), nstate[t // 2][:, h:h + 1])
                    L0.close(last)
                if delta:
                    E["r_ready"].wait(pe)
                    bank = L1.open(pe)
                    for h in range(4):
                        last = mm(bank[:n, h * P:h * P + P], UI[f][:n, h, :n], TM[:n, vchunk + h, :])
                    L1.close(last)
                    E["vn_ready"].wait(pe)
                v = (lambda h: YI[f][:n, h, :]) if delta else (lambda h: TM[:n, vchunk + h, :])
                E["st_ready"].wait(pe)
                bank = L0.open(pe)
                for h in range(4):
                    last = mm(bank[:n, h * P:h * P + P], ST[:n, h, :n], v(h))
                L0.close(last)
                E["kw_ready"].wait(pe)
                bank = L0.open(pe)
                for h in range(4):
                    last = mm(bank[:, h * P:h * P + P], kw[:n, h, :], v(h))
                L0.close(last)
                if mlstm:
                    bank = L0.open(pe)
                    for h in range(4):
                        last = mm(bank[:, h:h + 1], kw[:n, h, :], ones[:n, 0:1])
                    L0.close(last)

            def finish_tile(t):
                E["y_ready"].wait(pe)
                transpose_tile(lambda c: Yout[:, c, :], t, N_TOK[t])

            def cumulate(w):
                E["lf_ready"].wait(pe)
                bank = L0.open(pe)
                L0.close(mm(bank[:, 0:3 * w], tri_incl, lg[:, 0:3 * w]))

            def layer_ab():
                norm()
                small_projection(8, 0, 4)
                cumulate(4)
                input_projection()
                E["z_ready"].wait(pe)
                for t in range(TILES):
                    n, c = N_TOK[t], COL[t]
                    to_tokens(t, 1)
                    row_broadcast(n)
                    E["gm_ready"].wait(pe)
                    last_row(t, 8)
                    E["state_ready"].wait(pe)
                    half(t, 0, lambda h: zT[:, h, c:c + n], lambda h: zT[:, 4 + h, c:c + n], 8, None, mlstm=True)
                    E["rot_ready"].wait(pe)
                    for g, base in ((0, 0), (1, 4)):
                        bank = lanes[g].open(pe)
                        for h in range(4):
                            last = flip(bank[:, h * P:h * P + n], rot(base + h)[:n], n)
                        lanes[g].close(last)
                    E["qkT_dve"].wait(pe)
                    E["qkT_act"].wait(pe)
                    half(t, 1, lambda h: qT[0][:, h, :n], lambda h: kT[0][:, h, :n], 24, None)
                    finish_tile(t)
                output_projection()

            def rot(c):
                return AT[c // 4][:, c % 4, :]

            def layer_c():
                norm()
                small_projection(16, 2, 6)
                cumulate(8)
                input_projection()
                E["z_ready"].wait(pe)
                for t in range(TILES):
                    n, c = N_TOK[t], COL[t]
                    to_tokens(t, 0)
                    E["qkn_ready"].wait(pe)
                    for i, (dst, base) in enumerate(((0, 0), (1, 4), (2, 8), (3, 12))):
                        lane = lanes[i % 2]
                        bank = lane.open(pe)
                        for h in range(4):
                            last = flip(bank[:, h * P:h * P + n], TM[:n, base + h, :], n)
                        lane.close(last)
                    E["qkT_dve"].wait(pe)
                    E["qkT_act"].wait(pe)
                    last_row(t, 8)
                    for f in range(2):
                        row_broadcast(n)
                    for f in range(2):
                        bank = L0.open(pe)
                        for h in range(4):
                            last = mm(bank[:n, h * P:h * P + n], kT[f][:, h, :n], kT[f][:, h, :n])
                        L0.close(last)
                        E["a_ready"].wait(pe)
                        bank = L1.open(pe)
                        for h in range(4):
                            last = flip(bank[:n, h * P:h * P + n], tmp[:n, h, :n], n)
                        L1.close(last)
                    levels = 6 if n == 128 else 4
                    for lv in range(levels):
                        for f in range(2):
                            E["tu_ready"].wait(pe)
                            bank = L0.open(pe)
                            for h in range(4):
                                last = mm(bank[:n, h * P:h * P + n], AT[f][:n, h, :n], TI[f][:n, h, :n])
                            L0.close(last)
                        for f in range(2):
                            E["yi_ready"].wait(pe)
                            bank = L0.open(pe)
                            for h in range(4):
                                last = mm(bank[:n, h * P:h * P + n], UI[f][:n, h, :n], YI[f][:n, h, :n])
                            L0.close(last)
                            bank = L0.open(pe)
                            for h in range(4):
                                last = mm(bank[:n, h * P:h * P + n], YI[f][:n, h, :n], UI[f][:n, h, :n])
                            L0.close(last)
                    for f in range(2):
                        E["tu_ready"].wait(pe)
                    E["state_ready"].wait(pe)
                    for f in range(2):
                        half(t, f, lambda h: qT[f][:, h, :n], lambda h: kT[f][:, h, :n], 16 + 4 * f, None, delta=True)
                    finish_tile(t)
                output_projection()

            def experts(l):
                norm()
                small_projection(36, 1 + 2 * l, 4)
                E["choice_ready"].wait(pe)
                M = route[:, 0:96].rearrange("p (t e) -> p t e", e=NEXP)
                bank = L0.open(pe)
                for t in range(TILES):
                    last = mm(bank[0:NEXP, 0:1], M[:, t, :], ones[:, 0:1], t == 0, t == 2)
                L0.close(last)
                bank = L0.open(pe)
                for t in range(TILES):
                    for s in range(t + 1):
                        last = mm(bank[:, 32 * t:32 * t + 32], tri_strict if s == t else ones, M[:, s, :],
                                  s == 0, s == t)
                L0.close(last)
                E["nb_ready"].wait(pe)
                nbc, nbb = route[0:NEXP, 700:701], route[0:NEXP, 704:832]
                bank = L0.open(pe)
                L0.close(mm(bank[0:NEXP, 0:1], tri_incl[0:NEXP, 0:NEXP], nbc))
                bank = L0.open(pe)
                L0.close(mm(bank[:, 0:NEXP], nbb, tri_strict[0:NEXP, 0:NEXP]))
                E["list_ready"].wait(pe)
                bank = L0.open(pe)
                L0.close(mm(bank[0:1, 0:MAX_BLOCKS], ones[0:NEXP, 0:1], route[0:NEXP, 832:832 + MAX_BLOCKS]))
                E["blocks_ready"].wait(pe)
                m = moe[l]
                nb = nblk_reg(pe)
                for used in ("gate_used", "up_used", "down_used"):
                    pe.sem_inc(m[used], 2)

                def gather(u, count):
                    pe.wait_ge(m["onehot"], count)
                    for k in range(KT):
                        for t in range(TILES):
                            n = N_TOK[t]
                            last = mm(banks[4 + u][:, k * BLK:k * BLK + BLK], HN[:n, t, k * P:k * P + P],
                                      oh[u][0][:n, t, :], t == 0, t == 2)
                    last.then_inc(m["gathered"], 1)

                gather(0, 1)
                with pe.Fori(0, nb) as b:
                    for u in range(2):
                        i = 2 * b + u
                        pe.wait_ge(m["xg"], i + 1)
                        for s, used in ((0, "gate_used"), (1, "up_used")):
                            pe.wait_ge(m["w_in"][3 * u + s], 16 * b + 16)
                            w = W[:, 3 * u + s, :].rearrange("p (k n) -> p k n", k=KT)
                            for j in range(4):
                                for k in range(KT):
                                    last = mm(banks[6 + u][:, 256 * s + BLK * j:256 * s + BLK * j + BLK],
                                              w[:, k, j * P:j * P + P], xg[u][:, k, :], k == 0, k == KT - 1)
                            last.then_inc(m[used], 1)
                        gather(1 - u, i + 2)
                        pe.wait_ge(m["hidden"], i + 1)
                        pe.wait_ge(m["w_in"][3 * u + 2], 16 * b + 16)
                        pe.wait_ge(m["ya"], i + 1)
                        pe.wait_ge(m["yb"], i + 1)
                        w = W[:, 3 * u + 2, :].rearrange("p (k n) -> p k n", k=4)
                        for half_ in range(2):
                            for j in range(4):
                                last = mm(banks[2 * u + half_][0:BLK, :], hid[u][:, j * BLK:j * BLK + BLK],
                                          w[:, j, 512 * half_:512 * half_ + 512], j == 0, j == 3)
                        last.then_inc(m["down_used"], 1)

            const_in.wait(pe, 16)
            layer_ab()
            experts(0)
            layer_c()
            experts(1)

        @block.scalar
        def _(act):
            do = InOrder(act, order["act"])

            def norm():
                for t in range(TILES):
                    n = N_TOK[t]
                    x_ready.wait(act)
                    do(nc.scalar.activation(junk[:n, :], X[:n, t, :], ACT.Square, accum_out=sumsq[:n, t:t + 1]),
                       ss_ready)

            def take_transposed(event):
                for t in range(TILES):
                    n, c = N_TOK[t], COL[t]
                    take_one(t, event)

            def take_one(t, event):
                n, c = N_TOK[t], COL[t]
                bank = L1.take(act)
                do(nc.scalar.copy(HT[:, 4:8, c:c + n], heads4(bank[:, :])[:, :, :n]), L1.taken)
                event.mark(act.nop())

            def log_gate(w, e):
                E["gate_exp_in"].wait(act)
                do(nc.scalar.activation(t24b[:, 0:3 * w], t24a[:, 0:3 * w], ACT.Exp, scale=-1.0))
                do(nc.scalar.activation(t24b[:, 0:3 * w], t24b[:, 0:3 * w], ACT.Ln, bias=ones[:, 0:1]))
                if e:
                    do(nc.scalar.activation(t24c[:, :], beta[:, :], ACT.Exp, scale=-1.0))
                    do(nc.scalar.activation(gb1, gb1, ACT.Exp))
                E["gate_exp"].mark(act.nop())

            def to_tokens(t, groups):
                n = N_TOK[t]
                if not E["rows_clear"].seen.get(id(act)):
                    E["rows_clear"].wait(act, 16)
                if t:
                    E["tile_done"].wait(act)
                for g in groups:
                    bank = L1.take(act)
                    do(nc.scalar.copy(TM[:n, 4 * g:4 * g + 4, :], heads4(bank[:n, :])), L1.taken)
                E["tm_act"].mark(act.nop())

            def scores_T(n):
                bank = L1.take(act)
                do(nc.scalar.copy(ST[:n, :, :n], heads4(bank[:n, :])[:, :, :n]), L1.taken)
                E["st_ready"].mark(act.nop())

            def layer_ab():
                norm()
                take_transposed(ht_act)
                log_gate(4, False)
                for c in range(32):
                    bank = L1.take(act)
                    do(nc.scalar.activation(zT[:, c, :], bank[:, 0:COLS], ACT.Copy,
                                            scale=float(P) ** -0.5 if 4 <= c < 8 else 1.0), L1.taken)
                E["z_ready"].mark(act.nop())
                for t in range(TILES):
                    n = N_TOK[t]
                    to_tokens(t, (1, 3, 5, 7))
                    E["ein_ready"].wait(act)
                    do(nc.scalar.activation(eout[:n, 0:12], ein[:n, 0:12], ACT.Exp))
                    do(nc.scalar.activation(eout[:, 12:16], ein[:, 12:16], ACT.Exp), E["eout_ready"])
                    for h in range(4):
                        do(nc.scalar.activation(GAM[0][:n, h, :n], GAM[1][:n, h, :n], ACT.Exp,
                                                bias=negg[:n, h:h + 1]))
                    E["p_ready"].mark(act.nop())
                    scores_T(n)
                    bank = L1.take(act)
                    do(nc.scalar.copy(kT[0][:, :, :n], heads4(bank[:, :])[:, :, :n]), L1.taken)
                    E["qkT_act"].mark(act.nop())
                    scores_T(n)
                    E["gexp_ready"].wait(act)
                    do(nc.scalar.activation(YI[0][:n], TM[:n, 12:16, :], ACT.Exp, scale=-1.0))
                    do(nc.scalar.activation(YI[1][:n], TM[:n, 28:32, :], ACT.Exp, scale=-1.0), E["gexp_ready2"])
                    take_one(t, E["yT_act"])

            def layer_c():
                norm()
                take_transposed(ht_act)
                log_gate(8, True)
                for p in range(8):
                    for j in range(4):
                        bank = L1.take(act)
                        do(nc.scalar.copy(zT[:, 4 * p + j, :], bank[:, 0:COLS]), L1.taken)
                    if p < 6:
                        E["conv_raw"].mark(act.nop())
                        E["conv_done"].wait(act)
                        do(nc.scalar.activation(zT[:, 4 * p:4 * p + 4, PAD:COLS], convbuf, ACT.Silu), E["conv_used"])
                E["z_ready"].mark(act.nop())
                for t in range(TILES):
                    n = N_TOK[t]
                    to_tokens(t, (1, 3, 5, 7))
                    for i in range(2):
                        bank = L1.take(act)
                        dst = (qT, kT)[i][1]
                        do(nc.scalar.copy(dst[:, :, :n], heads4(bank[:, :])[:, :, :n]), L1.taken)
                    E["qkT_act"].mark(act.nop())
                    E["ein_ready"].wait(act)
                    do(nc.scalar.activation(eout[:n, 0:16], ein[:n, 0:16], ACT.Exp))
                    do(nc.scalar.activation(eout[:, 16:24], ein[:, 16:24], ACT.Exp), E["eout_ready"])
                    for f in range(2):
                        E["am_ready"].wait(act)
                        for h in range(4):
                            do(nc.scalar.activation(GAM[f][:n, h, :n], GAM[f][:n, h, :n], ACT.Exp,
                                                    bias=gm[:n, 4 * f + h:4 * f + h + 1]))
                        E["p_ready"].mark(act.nop())
                    for f in range(2):
                        bank = L1.take(act)
                        do(nc.scalar.copy(AT[f][:n, :, :n], heads4(bank[:n, :])[:, :, :n]), L1.taken)
                        E["at_ready"].mark(act.nop())
                    for f in range(2):
                        scores_T(n)
                        bank = L1.take(act)
                        do(nc.scalar.copy(YI[f][:n, :, :], heads4(bank[:n, :])), L1.taken)
                        E["vn_ready"].mark(act.nop())
                    E["gexp_ready"].wait(act)
                    do(nc.scalar.activation(AT[0][:n], TM[:n, 24:28, :], ACT.Exp, scale=-1.0))
                    do(nc.scalar.activation(AT[1][:n], TM[:n, 28:32, :], ACT.Exp, scale=-1.0), E["gexp_ready2"])
                    take_one(t, E["yT_act"])

            def experts(l):
                act.wait_ge(states_out, l + 1)
                norm()
                take_transposed(ht_act)
                E["logits_exp_in"].wait(act)
                do(nc.scalar.activation(route[:, 300:312], route[:, 300:312], ACT.Exp), E["logits_exp"])
                E["logits_exp_in"].wait(act)
                do(nc.scalar.activation(route[:, 320:323], route[:, 320:323], ACT.Exp), E["logits_exp"])
                E["blocks_ready"].wait(act)
                m = moe[l]
                nb = nblk_reg(act)
                act.sem_inc(m["ya"], 2)
                with act.Fori(0, nb) as b:
                    for u in range(2):
                        i = 2 * b + u
                        act.wait_ge(m["gate_used"], i + 3)
                        act.wait_ge(m["up_used"], i + 3)
                        nc.scalar.activation(sg[u], banks[6 + u][:, 0:256], ACT.Silu).then_inc(m["silu"], 1)
                        act.wait_ge(m["down_used"], i + 3)
                        act.wait_ge(m["stored"][u], 16 * b)
                        nc.scalar.copy(ys[u][0:BLK, 0:512], banks[2 * u][0:BLK, :]).then_inc(m["ya"], 1)
                        act.wait_ge(m["ya"], i + 3)
                        act.wait_ge(m["yb"], i + 3)
                        act.dma_start(a["block_rows"][bass.ds(BLK * i, BLK), :], ys[u][0:BLK, :]
                                      ).then_inc(m["stored"][u], 16)

            layer_ab()
            experts(0)
            layer_c()
            experts(1)
            norm()

        @block.vector
        def _(dve):
            do = InOrder(dve, order["dve"])
            v = nc.vector

            def tt(out, i0, i1, op, event=None):
                do(v.tensor_tensor(out, i0, i1, op), event)

            def ts(out, i0, s1, s2=None, op0=ALU.mult, op1=ALU.bypass, event=None):
                if s2 is None:
                    do(v.tensor_scalar(out, i0, s1, None, op0), event)
                else:
                    do(v.tensor_scalar(out, i0, s1, s2, op0, op1), event)

            def cp(out, i, event=None):
                do(v.tensor_copy(out, i), event)

            def red(out, i, op=ALU.add, event=None):
                do(v.tensor_reduce(out, i, X_AXIS, op), event)

            def signal(event):
                event.mark(dve.nop())

            def bc_last(ap, n):
                return ap.unsqueeze(len(ap.shape)).to_broadcast(list(ap.shape) + [n])

            def bc_mid(ap, n):
                return ap.unsqueeze(1).to_broadcast([ap.shape[0], n] + list(ap.shape[1:]))

            def norm(last=False):
                gain_in.wait(dve, 16)
                for t in range(TILES):
                    n = N_TOK[t]
                    rs_ready.wait(dve)
                    do(v.scalar_tensor_tensor(out=HN[:n, t, :], in0=X[:n, t, :], scalar=rstd[:n, t:t + 1],
                                              in1=gain[:n, :], op0=ALU.mult, op1=ALU.mult),
                       E["hn_out"] if last else hn_ready)
                if not last:
                    signal(gain_used)
                    for t in range(TILES):
                        take_one(t, ht_dve)

            def take_one(t, event):
                n, c = N_TOK[t], COL[t]
                bank = L0.take(dve)
                cp(HT[:, 0:4, c:c + n], heads4(bank[:, :])[:, :, :n], L0.taken)
                signal(event)

            def gates(w):
                g3 = g16[:, 0:3 * w].rearrange("p (t w) -> p t w", w=w)
                do(v.memset(g16, 0.0))
                bank = L0.take(dve)
                cp(g3[:, 0:2, :], bank[:, 0:128].rearrange("p (t w) -> p t w", w=64)[:, :, 0:w])
                cp(g3[:32, 2, :], bank[:32, 128:128 + w], L0.taken)
                signal(small_used)
                return g3

            def to_tokens(t, groups):
                n = N_TOK[t]
                for g in groups:
                    bank = L0.take(dve)
                    cp(TM[:n, 4 * g:4 * g + 4, :], heads4(bank[:n, :]), L0.taken)
                signal(E["tm_dve"])
                E["tm_act"].wait(dve)

            def diag(col, n):
                tt(tmp[:n, :, :n], bc_mid(ident[:n, :n], 4), bc_last(col, n), ALU.mult, E["diag_ready"])

            def half(t, f, gam, wq, wkk, dec, kchunk, vchunk, mlstm=False, delta=False):
                n = N_TOK[t]
                st = states[t][:, 4 * f:4 * f + 4, :]
                y = Yout[:, 4 * f:4 * f + 4, :]
                bank = L0.take(dve)
                tt(Sm[:n, :, :n], heads4(bank[:n, :])[:, :, :n], gam, ALU.mult, L0.taken)
                signal(E["s_ready"])
                if delta:
                    bank = L0.take(dve)
                    tt(tmp[:n], heads4(bank[:n, :]), bc_last(wq, P), ALU.mult, L0.taken)
                    tt(tmp[:n], TM[:n, vchunk:vchunk + 4, :], tmp[:n], ALU.subtract)
                    tt(TM[:n, vchunk:vchunk + 4, :], tmp[:n], bc_last(beta3[:n, t, 4 * f:4 * f + 4], P),
                       ALU.mult, E["r_ready"])
                tt(kw[:n], TM[:n, kchunk:kchunk + 4, :], bc_last(wkk, P), ALU.mult, E["kw_ready"])
                bank = L0.take(dve)
                tt(tmp[:n], heads4(bank[:n, :]), bc_last(wq, P), ALU.mult, L0.taken)
                if mlstm:
                    red(den[:n, :], Sm[:n, :, :n])
                    bank = L0.take(dve)
                    tt(den2[:n, :], bank[:n, 0:4], wq, ALU.mult, L0.taken)
                    tt(den[:n, :], den[:n, :], den2[:n, :], ALU.add)
                    ts(den2[:n, :], den[:n, :], -1.0)
                    tt(den[:n, :], den[:n, :], den2[:n, :], ALU.max)
                    tt(den[:n, :], den[:n, :], eout[:n, 4:8], ALU.max)
                    do(v.reciprocal(den[:n, :], den[:n, :]))
                bank = L0.take(dve)
                tt(y[:n], heads4(bank[:n, :]), tmp[:n], ALU.add, L0.taken)
                if mlstm:
                    tt(y[:n], y[:n], bc_last(den[:n, :], P), ALU.mult)
                tt(st, st, bc_last(dec, P), ALU.mult)
                bank = L0.take(dve)
                tt(st, st, heads4(bank[:, :]), ALU.add, L0.taken)
                if mlstm:
                    ns = nstate[t // 2]
                    tt(ns, ns, dec, ALU.mult)
                    bank = L0.take(dve)
                    tt(ns, ns, bank[:, 0:4], ALU.add, L0.taken)

            def head_norm(t, gates_c, scratch, exps, plain_first):
                n = N_TOK[t]
                signal(E["gexp_ready"])
                for f in range(2):
                    y = Yout[:n, 4 * f:4 * f + 4, :]
                    tt(tmp[:n], y, y, ALU.mult)
                    red(hss[:n, 4 * f:4 * f + 4], tmp[:n])
                signal(E["hss_ready"])
                E["gexp_ready2"].wait(dve)
                for f in range(2):
                    ts(exps[f][:n], exps[f][:n], 1.0, op0=ALU.add)
                    do(v.reciprocal(exps[f][:n], exps[f][:n]))
                    if not (plain_first and f == 0):
                        tt(exps[f][:n], exps[f][:n], TM[:n, gates_c[f]:gates_c[f] + 4, :], ALU.mult)
                E["hrs_ready"].wait(dve)
                for f in range(2):
                    y = Yout[:n, 4 * f:4 * f + 4, :]
                    tt(y, y, bc_last(hrs[:n, 4 * f:4 * f + 4], P), ALU.mult)
                    tt(y, y, bc_mid(hgain[:n, f if plain_first else 0, :], 4), ALU.mult)
                    tt(y, y, exps[f][:n], ALU.mult)
                signal(E["y_ready"])
                signal(E["tile_done"])
                take_one(t, E["yT_dve"])

            def output_projection():
                for p in range(2):
                    for t in range(TILES):
                        n = N_TOK[t]
                        bank = L0.take(dve)
                        tt(X[:n, t, 512 * p:512 * p + 512], X[:n, t, 512 * p:512 * p + 512], bank[:n, :],
                           ALU.add, L0.taken)
                for t in range(TILES):
                    signal(x_ready)

            lg4 = lg[:, 0:12].rearrange("p (t w) -> p t w", w=4)
            lg8 = lg.rearrange("p (t w) -> p t w", w=8)
            b4 = bcum[:, 0:12].rearrange("p (t w) -> p t w", w=4)
            b8 = bcum.rearrange("p (t w) -> p t w", w=8)
            beta3 = beta.rearrange("p (t w) -> p t w", w=8)

            def layer_ab():
                norm()
                small_in[0].wait(dve, 64)
                g3 = gates(8)
                tt(g3, g3, bc_mid(gb1, 3), ALU.add)
                ab = t24a[:, 0:12].rearrange("p (t w) -> p t w", w=4)
                ts(ab, g3[:, :, 4:8], -1.0)
                tt(ab, ab, g3[:, :, 4:8], ALU.max, E["gate_exp_in"])
                ts(lg4, g3[:, :, 4:8], 0.0, op0=ALU.min)
                E["gate_exp"].wait(dve)
                tt(lg[:, 0:12], lg[:, 0:12], t24b[:, 0:12], ALU.subtract, E["lf_ready"])
                bank = L0.take(dve)
                cp(bcum[:, 0:12], bank[:, 0:12], L0.taken)
                a3 = acol[:, 0:12].rearrange("p (t w) -> p t w", w=4)
                tt(a3, g3[:, :, 0:4], b4, ALU.subtract)
                do(v.memset(state1, 0.0))
                do(v.memset(nstate[0], 0.0))
                do(v.memset(mprev[0], 0.0))
                state_in.wait(dve, 64)
                E["rows_clear"].wait(dve, 16)
                for t in range(TILES):
                    n, g = N_TOK[t], t // 2
                    mp = mprev[g]
                    if t == 0:
                        E["z_ready"].wait(dve)
                    to_tokens(t, (2, 4, 6))
                    diag(a3[:n, t, :], n)
                    bank = L0.take(dve)
                    tt(GAM[1][:n, :, :n], heads4(bank[:n, :])[:, :, :n], bc_mid(cst("negmask")[:n, :n], 4),
                       ALU.add, L0.taken)
                    red(m1[:n, :], GAM[1][:n, :, :n], ALU.max)
                    tt(gm[:n, 0:4], m1[:n, :], mp[:n, :], ALU.max)
                    tt(gm[:n, 4:8], gm[:n, 0:4], b4[:n, t, :], ALU.add, E["gm_ready"])
                    ts(negg[:n, :], gm[:n, 0:4], -1.0)
                    bank = L0.take(dve)
                    cp(gl, bank[:, 0:8], L0.taken)
                    tt(ein[:n, 0:4], mp[:n, :], gm[:n, 0:4], ALU.subtract)
                    ts(ein[:n, 4:8], gm[:n, 4:8], -1.0)
                    tt(ein[:n, 8:12], a3[:n, t, :], gl[:n, 0:4], ALU.subtract)
                    tt(ein[:, 12:16], mp, gl[:, 0:4], ALU.subtract)
                    cp(mp, gl[:, 4:8], E["ein_ready"])
                    signal(E["state_ready"])
                    E["eout_ready"].wait(dve)
                    E["p_ready"].wait(dve)
                    half(t, 0, GAM[0][:n, :, :n], eout[:n, 0:4], eout[:n, 8:12], eout[:, 12:16], 4, 8, mlstm=True)
                    for j in range(2):
                        cos = bc_mid(rotc[:n, t, j, :], 4)
                        sin = bc_mid(rots[:n, t, j, :], 4)
                        x1, x2 = TM[:n, 16 + 4 * j:20 + 4 * j, 0:64], TM[:n, 16 + 4 * j:20 + 4 * j, 64:128]
                        o, s = AT[j], TI[0]
                        tt(o[:n, :, 0:64], x1, cos, ALU.mult)
                        tt(s[:n, :, 0:64], x2, sin, ALU.mult)
                        tt(o[:n, :, 0:64], o[:n, :, 0:64], s[:n, :, 0:64], ALU.subtract)
                        tt(o[:n, :, 64:128], x1, sin, ALU.mult)
                        tt(s[:n, :, 0:64], x2, cos, ALU.mult)
                        tt(o[:n, :, 64:128], o[:n, :, 64:128], s[:n, :, 0:64], ALU.add)
                    cp(TM[:n, 20:24, :], AT[1][:n], E["rot_ready"])
                    bank = L0.take(dve)
                    cp(qT[0][:, :, :n], heads4(bank[:, :])[:, :, :n], L0.taken)
                    signal(E["qkT_dve"])
                    r = cst("ret_k")[:n, 4 * g:4 * g + 4]
                    half(t, 1, heads4(cst("ret_decay")[:n, :])[:, :, :n], cst("ret_q")[:n, :], r,
                         cst("ret_c")[:, 4 * g:4 * g + 4], 20, 24)
                    if t >= 1:
                        signal(E["state_done"])
                    head_norm(t, (12, 28), None, YI, True)
                output_projection()

            def layer_c():
                norm()
                small_in[2].wait(dve, 96)
                g3 = gates(16)
                cp(beta3, g3[:, :, 0:8])
                x3 = g3[:, :, 8:16]
                tt(x3, x3, bc_mid(gb2, 3), ALU.add)
                ab = t24a.rearrange("p (t w) -> p t w", w=8)
                ts(ab, x3, -1.0)
                tt(ab, ab, x3, ALU.max, E["gate_exp_in"])
                ts(lg8, x3, 0.0, op0=ALU.max)
                E["gate_exp"].wait(dve)
                ts(beta, t24c, 1.0, op0=ALU.add)
                do(v.reciprocal(beta, beta))
                tt(lg, lg, t24b, ALU.add)
                ts(lg, lg, -1.0)
                tt(lg8, lg8, bc_mid(gb1, 3), ALU.mult, E["lf_ready"])
                bank = L0.take(dve)
                cp(bcum, bank[:, 0:24], L0.taken)
                ts(acol, bcum, -1.0)
                a3 = acol.rearrange("p (t w) -> p t w", w=8)
                for p in range(6):
                    E["conv_raw"].wait(dve)
                    c4 = zT[:, 4 * p:4 * p + 4, :]
                    cp(c4[:, :, COL[2] - PAD:COL[2]], cconv[:, 4 * p:4 * p + 4, 4:7])
                    cp(tails[:, 4 * p:4 * p + 4, 0:3], c4[:, :, COL[2] - 2 * PAD:COL[2] - PAD])
                    cp(tails[:, 4 * p:4 * p + 4, 3:6], c4[:, :, COLS - PAD:COLS])
                    if p:
                        E["conv_used"].wait(dve)
                    for j in range(4):
                        ch = 4 * p + j
                        o = convbuf[:, j, :]
                        ts(o, zT[:, ch, 0:COLS - PAD], cconv[:, ch, 0:1])
                        for k in range(1, 4):
                            do(v.scalar_tensor_tensor(out=o, in0=zT[:, ch, k:k + COLS - PAD],
                                                      scalar=cconv[:, ch, k:k + 1], in1=o,
                                                      op0=ALU.mult, op1=ALU.add))
                    signal(E["conv_done"])
                signal(E["tails_done"])
                E["conv_used"].wait(dve)
                do(v.memset(state1, 0.0))
                state_in.wait(dve, 16)
                for t in range(TILES):
                    n, g = N_TOK[t], t // 2
                    if t == 0:
                        E["z_ready"].wait(dve)
                    to_tokens(t, (0, 2, 4, 6))
                    for i in range(4):
                        qk = TM[:n, 4 * i:4 * i + 4, :]
                        tt(tmp[:n], qk, qk, ALU.mult)
                        red(hss[:n, 4 * i:4 * i + 4], tmp[:n])
                    signal(E["hss_ready"])
                    E["hrs_ready"].wait(dve)
                    ts(hrs[:n, 0:8], hrs[:n, 0:8], float(P) ** -0.5)
                    cp(gm[:n, :], b8[:n, t, :])
                    for i in range(4):
                        qk = TM[:n, 4 * i:4 * i + 4, :]
                        tt(qk, qk, bc_last(hrs[:n, 4 * i:4 * i + 4], P), ALU.mult)
                    signal(E["qkn_ready"])
                    for i in range(2):
                        bank = L0.take(dve)
                        cp((qT, kT)[i][0][:, :, :n], heads4(bank[:, :])[:, :, :n], L0.taken)
                    signal(E["qkT_dve"])
                    bank = L0.take(dve)
                    cp(gl, bank[:, 0:8], L0.taken)
                    cp(ein[:n, 0:8], gm[:n, :])
                    tt(ein[:n, 8:16], gl[:n, :], gm[:n, :], ALU.subtract)
                    cp(ein[:, 16:24], gl, E["ein_ready"])
                    for f in range(2):
                        diag(a3[:n, t, 4 * f:4 * f + 4], n)
                        bank = L0.take(dve)
                        tt(GAM[f][:n, :, :n], heads4(bank[:n, :])[:, :, :n], bc_mid(cst("negmask")[:n, :n], 4),
                           ALU.add, L0.taken)
                        signal(E["am_ready"])
                    E["eout_ready"].wait(dve)
                    for f in range(2):
                        E["p_ready"].wait(dve)
                        bank = L0.take(dve)
                        if f:
                            E["at_ready"].wait(dve)
                        tt(tmp[:n, :, :n], heads4(bank[:n, :])[:, :, :n], GAM[f][:n, :, :n], ALU.mult, L0.taken)
                        tt(tmp[:n, :, :n], tmp[:n, :, :n], bc_mid(cst("strict")[:n, :n], 4), ALU.mult)
                        tt(tmp[:n, :, :n], tmp[:n, :, :n], bc_last(beta3[:n, t, 4 * f:4 * f + 4], n), ALU.mult,
                           E["a_ready"])
                        tt(TI[f][:n, :, :n], tmp[:n, :, :n], bc_mid(merge[:n, 0, :n], 4), ALU.mult)
                        tt(TI[f][:n, :, :n], bc_mid(ident[:n, :n], 4), TI[f][:n, :, :n], ALU.subtract)
                    E["at_ready"].wait(dve)
                    for f in range(2):
                        tt(UI[f][:n, :, :n], AT[f][:n, :, :n], bc_mid(cst("merge1_t")[:n, :n], 4), ALU.mult)
                        tt(UI[f][:n, :, :n], bc_mid(ident[:n, :n], 4), UI[f][:n, :, :n], ALU.subtract,
                           E["tu_ready"])
                    levels = 6 if n == 128 else 4
                    for lv in range(levels):
                        for f in range(2):
                            bank = L0.take(dve)
                            tt(YI[f][:n, :, :n], heads4(bank[:n, :])[:, :, :n], bc_mid(merge[:n, lv + 1, :n], 4),
                               ALU.mult, L0.taken)
                            signal(E["yi_ready"])
                        for f in range(2):
                            for M in (TI[f], UI[f]):
                                bank = L0.take(dve)
                                tt(M[:n, :, :n], M[:n, :, :n], heads4(bank[:n, :])[:, :, :n], ALU.subtract,
                                   L0.taken)
                            signal(E["tu_ready"])
                    signal(E["state_ready"])
                    for f in range(2):
                        half(t, f, GAM[f][:n, :, :n], eout[:n, 4 * f:4 * f + 4], eout[:n, 8 + 4 * f:12 + 4 * f],
                             eout[:, 16 + 4 * f:20 + 4 * f], 8 + 4 * f, 16 + 4 * f, delta=True)
                    if t >= 1:
                        signal(E["state_done"])
                    head_norm(t, (24, 28), None, AT, False)
                output_projection()

            def experts(l):
                dve.wait_ge(states_out, l + 1)
                norm()
                small_in[1 + 2 * l].wait(dve, 64)
                r = lambda o, w: route[:, o:o + w]
                t3 = lambda ap, w: ap.rearrange("p (t w) -> p t w", w=w)
                logit = t3(r(400, 108), 36)
                do(v.memset(r(400, 108), 0.0))
                bank = L0.take(dve)
                tt(logit[:, 0:2, :], t3(bank[:, 0:128], 64)[:, :, 0:36], bc_mid(rb, 2), ALU.add)
                tt(logit[:32, 2, :], bank[:32, 128:164], rb[:32, :], ALU.add, L0.taken)
                signal(small_used)
                grp, fine = logit[:, :, 0:4], logit[:, :, 4:36]
                gmax, gsum, psel = r(510, 3), r(513, 3), r(516, 3)
                eq = t3(r(520, 24), 8)
                idx = r(544, 3)
                ohg = t3(r(548, 12), 4)
                red(gmax, grp, ALU.max)
                tt(t3(r(300, 12), 4), grp, bc_last(gmax, 4), ALU.subtract, E["logits_exp_in"])
                E["logits_exp"].wait(dve)
                red(gsum, t3(r(300, 12), 4))
                do(v.reciprocal(psel, gsum))

                def first_max(vals, top, w, out):
                    e_ = eq[:, :, 0:w]
                    tt(e_, vals, bc_last(top, w), ALU.is_equal)
                    tt(e_, e_, bc_mid(cst("iota_m99")[:, 0:w], 3), ALU.mult)
                    red(idx, e_, ALU.min)
                    tt(out, bc_mid(cst("iota_m99")[:, 0:w], 3), bc_last(idx, w), ALU.is_equal)

                first_max(grp, gmax, 4, ohg)
                tt(ohg, ohg, bc_last(cst("valid"), 4), ALU.mult)
                fs, oh1, oh2 = t3(r(560, 24), 8), t3(r(584, 24), 8), t3(r(608, 24), 8)
                wide = r(900, 96)
                wide4 = wide.rearrange("p (t g j) -> p t g j", g=NGRP, j=EPG)
                for t in range(TILES):
                    tt(wide4[:, t], fine[:, t, :].rearrange("p (g j) -> p g j", j=EPG), bc_last(ohg[:, t, :], EPG),
                       ALU.mult)
                    red(fs[:, t, :], wide4[:, t].rearrange("p g j -> p j g"))
                max1, max2 = r(632, 3), r(636, 3)
                red(max1, fs, ALU.max)
                first_max(fs, max1, 8, oh1)
                do(v.scalar_tensor_tensor(out=r(640, 24), in0=r(584, 24), scalar=-BIG, in1=r(560, 24),
                                          op0=ALU.mult, op1=ALU.add))
                rest = t3(r(640, 24), 8)
                red(max2, rest, ALU.max)
                first_max(rest, max2, 8, oh2)
                tt(r(320, 3), max2, max1, ALU.subtract, E["logits_exp_in"])
                M = r(0, 96)
                Mk = [r(100, 96), r(200, 96)]
                for k, o in enumerate((oh1, oh2)):
                    m4 = Mk[k].rearrange("p (t g j) -> p t g j", g=NGRP, j=EPG)
                    for t in range(TILES):
                        tt(m4[:, t], bc_last(ohg[:, t, :], EPG), bc_mid(o[:, t, :], NGRP), ALU.mult)
                tt(M, Mk[0], Mk[1], ALU.add, E["choice_ready"])
                E["logits_exp"].wait(dve)
                s = r(664, 3)
                ts(s, r(320, 3), 1.0, op0=ALU.add)
                do(v.reciprocal(s, s))
                tt(pw[0][:, 0:3], psel, s, ALU.mult)
                tt(pw[0][:, 3:6], pw[0][:, 0:3], r(320, 3), ALU.mult)
                bank = L0.take(dve)
                cp(r(668, 1)[0:NEXP], bank[0:NEXP, 0:1], L0.taken)
                ts(r(670, 5)[0:NEXP], cst("thresh")[0:NEXP, :], r(668, 1)[0:NEXP], op0=ALU.is_lt)
                red(r(700, 1)[0:NEXP], r(670, 5)[0:NEXP])
                ts(route[0:NEXP, 704:832], ones[0:NEXP, :], r(700, 1)[0:NEXP])
                signal(E["nb_ready"])
                bank = L0.take(dve)
                cp(wide, bank[:, 0:96], L0.taken)
                bank = L0.take(dve)
                cp(r(680, 1)[0:NEXP], bank[0:NEXP, 0:1], L0.taken)
                bank = L0.take(dve)
                ts(r(1000, 32), bank[:, 0:32], float(BLK), event=L0.taken)
                ts(route[0:NEXP, 832:832 + MAX_BLOCKS], cst("iota_list")[0:NEXP, :], r(680, 1)[0:NEXP],
                   op0=ALU.is_ge)
                cp(route[0:NEXP, 832 + MAX_BLOCKS - 1:832 + MAX_BLOCKS], r(700, 1)[0:NEXP], E["list_ready"])
                tt(t3(wide, NEXP), t3(wide, NEXP), bc_mid(r(1000, 32), 3), ALU.add)
                for k in range(2):
                    tt(r(1100, 96), Mk[k], wide, ALU.mult)
                    red(dk[:, 3 * k:3 * k + 3], t3(r(1100, 96), NEXP))
                    cp(slots_i[:, k, :], dk[:, 3 * k:3 * k + 3])
                    tt(dk[:, 3 * k:3 * k + 3], dk[:, 3 * k:3 * k + 3], cst("invalid"), ALU.add)
                bank = L0.take(dve)
                last_ = MAX_BLOCKS - 1
                ts(r(1200, MAX_BLOCKS)[0:1], bank[0:1, 0:MAX_BLOCKS], float(NEXP - 1), op0=ALU.min)
                cp(r(1300, 1)[0:1], bank[0:1, last_:last_ + 1], L0.taken)
                cp(blocks_i[:, 0:last_], r(1200, last_)[0:1])
                cp(blocks_i[:, last_:last_ + 1], r(1300, 1)[0:1], E["blocks_ready"])
                m = moe[l]
                nb = nblk_reg(dve)
                dve.sem_inc(m["yb"], 2)
                iota = bc_mid(cst("iota_blk"), 3)

                def onehot(u, count):
                    v.tensor_tensor(oh[u][0], iota, bc_last(dk[:, 0:3], BLK), ALU.is_equal).then_inc(m["step"], 1)
                    v.tensor_tensor(oh[u][1], iota, bc_last(dk[:, 3:6], BLK), ALU.is_equal).then_inc(m["step"], 1)
                    dve.wait_ge(m["step"], 3 * count + 2)
                    v.tensor_scalar(dk, dk, -float(BLK), None, ALU.add).then_inc(m["step"], 1)
                    v.tensor_tensor(oh[u][0], oh[u][0], oh[u][1], ALU.add).then_inc(m["onehot"], 1)
                    dve.wait_ge(m["step"], 3 * count + 3)

                def fetched(u, count):
                    dve.wait_ge(m["gathered"], count)
                    v.tensor_copy(xg[u].rearrange("p k s -> p (k s)"), banks[4 + u][:, :]).then_inc(m["xg"], 1)

                onehot(0, 0)
                fetched(0, 1)
                with dve.Fori(0, nb) as b:
                    for u in range(2):
                        i = 2 * b + u
                        onehot(1 - u, i + 1)
                        dve.wait_ge(m["silu"], i + 1)
                        v.tensor_tensor(hid[u], sg[u], banks[6 + u][:, 256:512], ALU.mult).then_inc(m["hidden"], 1)
                        fetched(1 - u, i + 2)
                        dve.wait_ge(m["down_used"], i + 3)
                        dve.wait_ge(m["stored"][u], 16 * b)
                        v.tensor_copy(ys[u][0:BLK, 512:1024], banks[2 * u + 1][0:BLK, :]).then_inc(m["yb"], 1)
                for t in range(TILES):
                    n = N_TOK[t]
                    dve.wait_ge(m["yg_in"][t % 2], 32 * (t // 2 + 1))
                    for k in range(2):
                        ins = v.scalar_tensor_tensor(out=X[:n, t, :], in0=yg[:n, t % 2, k, :],
                                                     scalar=pw[0][:n, 3 * k + t:3 * k + t + 1], in1=X[:n, t, :],
                                                     op0=ALU.mult, op1=ALU.add)
                        do(ins)
                    signal(x_ready)
                    dve.nop().then_inc(m["yg_used"], 1)

            do(v.memset(TM[:, 0:8, :], 0.0), E["zero_rows"])
            const_in.wait(dve, 16)
            for t in range(TILES):
                x_in[t].wait(dve, 16)
                signal(x_ready)
            do(v.memset(HT[:, :, 0:PAD], 0.0))
            do(v.memset(HT[:, :, COL[2] - PAD:COL[2]], 0.0))
            layer_ab()
            experts(0)
            layer_c()
            experts(1)
            norm(last=True)

        @block.sync
        def _(sp):
            def dma(dst, src, event):
                event.mark(sp.dma_start(dst, src), 16)

            dma(const[:], a["const"], const_in)
            for t in range(TILES):
                src = a["x_prompt"][0, 128 * t:128 * t + 128, :] if t < 2 else a["x_sample"][0]
                dma(X[:N_TOK[t], t, :], src, x_in[t])

            def pieces(w_in, w_out, cols, layer):
                for p in range(10):
                    if layer or p >= 4:
                        sp.wait_ge(*piece_done[10 * layer + p - 4])
                    src = w_in[:, cols[p]:cols[p] + 512] if p < 8 else w_out[:, 512 * (p - 8):512 * (p - 7)]
                    dma(W[:, p % 4, :].rearrange("p (k n) -> p k n", k=KT),
                        src.rearrange("(k p) n -> p k n", p=P), piece_in[p % 4])

            def experts(l):
                m = moe[l]
                E["blocks_ready"].wait(sp)
                nb = nblk_reg(sp)
                with sp.Fori(0, nb) as b:
                    for u in range(2):
                        i = 2 * b + u
                        e = sp.value_load(blocks_i[0:1, bass.ds(i, 1)], min_val=0, max_val=NEXP - 1)
                        for s, (name, used) in enumerate((("moe_w_gate", "gate_used"), ("moe_w_up", "up_used"),
                                                          ("moe_w_down", "down_used"))):
                            sp.wait_ge(m[used], i + 1)
                            kk = 8 if s < 2 else 4
                            sp.dma_start(W[:, 3 * u + s, :].rearrange("p (k n) -> p k n", k=kk),
                                         a[name][l, bass.ds(e, 1), :, :].rearrange("o (k p) n -> p (o k) n", p=P)
                                         ).then_inc(m["w_in"][3 * u + s], 16)
                return nb

            pieces(a["ab_w_in"][0], a["ab_w_out"][0],
                   [512 * i for i in range(4)] + [2056 + 512 * i for i in range(4)], 0)
            sp.wait_ge(*piece_done[9])
            nb = experts(0)
            sp.wait_ge(moe[0]["down_used"], 2 * nb + 2)
            pieces(a["c_w_in"][0], a["c_w_out"][0],
                   [512 * i for i in range(6)] + [3088, 3600], 1)
            sp.wait_ge(*piece_done[19])
            experts(1)
            for t in range(TILES):
                E["hn_out"].wait(sp)
                dst = a["y_prompt"][0, 128 * t:128 * t + 128, :] if t < 2 else a["y_sample"][0]
                dma(dst, HN[:N_TOK[t], t, :], y_written)
            sp.wait_ge(y_written.sem, 16 * 3)

        @block.gpsimd
        def _(pool):
            do = InOrder(pool, order["pool"])

            def load(dst, src, event):
                event.mark(pool.dma_start(dst, src), 16)

            def store(dst, src):
                out_written.made += 16
                pool.dma_start(dst, src).then_inc(out_written.sem, 16)

            def power(dst, src, scale, n, w, ready, done):
                ready.wait(pool)
                do(nc.gpsimd.tensor_scalar(src, src, scale, EPS, ALU.mult, ALU.add))
                do(nc.gpsimd.tensor_tensor(dst, src, cst("half_neg")[:n, 0:w], ALU.pow), done)

            def norm(k):
                for t in range(TILES):
                    n = N_TOK[t]
                    power(rstd[:n, t:t + 1], sumsq[:n, t:t + 1], 1.0 / D, n, 1, ss_ready, rs_ready)
                if k < 4:
                    gain_used.wait(pool)
                    g = (a["norm_mix"], a["norm_ffn"])[(k + 1) % 2][(k + 1) // 2] if k < 3 else a["norm_final"]
                    load(gain[:], g.partition_broadcast(P), gain_in)

            load(gain[:], a["norm_mix"][0].partition_broadcast(P), gain_in)
            load(small_w[:, :, 0:8], a["ab_w_in"][0][:, 2048:2056].rearrange("(k p) n -> p k n", p=P), small_in[0])
            load(gb1, a["ab_gate_bias"][0].partition_broadcast(P), small_in[0])
            load(hgain[:, 0, :], a["ab_norm_a"][0].partition_broadcast(P), small_in[0])
            load(hgain[:, 1, :], a["ab_norm_b"][0].partition_broadcast(P), small_in[0])
            load(mprev[1], a["state_mlstm_m"][0, 0].partition_broadcast(P), state_in)
            load(nstate[1], a["state_n_t"], state_in)
            load(state2[:, 0:4, :], a["state_mlstm_c"][0, 0].rearrange("h k v -> k h v"), state_in)
            load(state2[:, 4:8, :], a["state_ret"][0, 0].rearrange("h k v -> k h v"), state_in)
            E["zero_rows"].wait(pool)
            load(a["block_rows"][9 * BLK - BLK:MAX_BLOCKS * BLK, :].rearrange("(r p) n -> p r n", p=P),
                 TM[:, 0:8, :].rearrange("p c n -> p (c n)").unsqueeze(1).to_broadcast([P, 18, D]), E["rows_clear"])
            load(cconv[:, :, 0:4], a["conv_taps"], small_in[2])
            load(cconv[:, :, 4:7], a["conv_state"], small_in[2])
            norm(0)
            for t in range(TILES):
                n = N_TOK[t]
                power(hrs[:n, 0:8], hss[:n, 0:8], 1.0 / P, n, 8, E["hss_ready"], E["hrs_ready"])
                if t >= 1:
                    E["state_done"].wait(pool)
                    g = t - 1
                    store(a["out_c"][g].rearrange("h k v -> k h v"), states[t][:, 0:4, :])
                    store(a["out_ret"][g].rearrange("h k v -> k h v"), states[t][:, 4:8, :])
                    store(a["out_n"][g], nstate[g])
                    store(a["out_m"][g], mprev[g][0:1, :])
            pool.wait_ge(out_written.sem, 16 * 8)
            nc.gpsimd.sem_inc(states_out, 1)
            small_used.wait(pool)
            for l in range(2):
                load(small_w[:, :, 0:4], a["moe_w_grp"][l].rearrange("(k p) n -> p k n", p=P), small_in[1 + 2 * l])
                load(small_w[:, :, 4:36], a["moe_w_exp"][l].rearrange("(k p) n -> p k n", p=P), small_in[1 + 2 * l])
                load(rb[:, 0:4], a["moe_b_grp"][l].partition_broadcast(P), small_in[1 + 2 * l])
                load(rb[:, 4:36], a["moe_b_exp"][l].partition_broadcast(P), small_in[1 + 2 * l])
                norm(2 * l + 1)
                if l == 0:
                    load(state2[:, :, :], a["state_gdn"][0, 0].rearrange("h k v -> k h v"), state_in)
                    load(gb1, a["c_a_log"][0].partition_broadcast(P), small_in[2])
                    load(gb2, a["c_dt_bias"][0].partition_broadcast(P), small_in[2])
                    load(hgain[:, 0, :], a["c_norm"][0].partition_broadcast(P), small_in[2])
                    small_used.wait(pool)
                    load(small_w[:, :, 0:16], a["c_w_in"][0][:, 3072:3088].rearrange("(k p) n -> p k n", p=P),
                         small_in[2])
                m = moe[l]
                E["blocks_ready"].wait(pool)
                nb = nblk_reg(pool)
                for u in range(2):
                    pool.wait_ge(m["stored"][u], 16 * nb)
                do(pool.nop())
                for t in range(TILES):
                    n = N_TOK[t]
                    if t == 2:
                        pool.wait_ge(m["yg_used"], 1)
                    for k in range(2):
                        pool.indirect_dma_start(
                            yg[:n, t % 2, k, :], None, a["block_rows"],
                            bass.IndirectOffsetOnAxis(ap=slots_i[:n, k, t:t + 1], axis=0)
                        ).then_inc(m["yg_in"][t % 2], 16)
                if l == 0:
                    norm(2)
                    for t in range(TILES):
                        n = N_TOK[t]
                        power(hrs[:n, 0:16], hss[:n, 0:16], 1.0, n, 16, E["hss_ready"], E["hrs_ready"])
                        power(hrs[:n, 0:8], hss[:n, 0:8], 1.0 / P, n, 8, E["hss_ready"], E["hrs_ready"])
                        if t >= 1:
                            E["state_done"].wait(pool)
                            store(a["out_gdn"][t - 1].rearrange("h k v -> k h v"), states[t])
                    E["tails_done"].wait(pool)
                    store(a["out_tails"], tails[:])
                    pool.wait_ge(out_written.sem, 16 * 11)
                    nc.gpsimd.sem_inc(states_out, 1)
                    small_used.wait(pool)
            norm(4)


_OUTS = {"y_prompt": (1, 256, 1024), "y_sample": (1, 32, 1024), "out_c": (2, 4, 128, 128), "out_n": (2, 128, 4),
         "out_m": (2, 1, 4), "out_ret": (2, 4, 128, 128), "out_gdn": (2, 8, 128, 128), "out_tails": (128, 24, 6)}
_IN = ["x_prompt", "x_sample", "state_mlstm_c", "state_mlstm_m", "state_ret", "state_gdn", "norm_mix", "norm_ffn",
       "norm_final", "ab_w_in", "ab_gate_bias", "ab_w_out", "ab_norm_a", "ab_norm_b", "c_w_in", "c_a_log",
       "c_dt_bias", "c_norm", "c_w_out", "moe_w_grp", "moe_b_grp", "moe_w_exp", "moe_b_exp", "moe_w_gate",
       "moe_w_up", "moe_w_down"]


def constants():
    import numpy as np

    f = np.float32
    i = np.arange(P)
    row, col = i[:, None], i[None, :]
    c = {
        "ident": row == col, "tri_incl": row <= col, "tri_strict": row < col, "ones": np.ones((P, P)),
        "negmask": np.where(col <= row, 0.0, -BIG), "strict": col < row,
        "merge": np.concatenate([(row // (2 * s) == col // (2 * s)) & (row // s % 2 == 1) & (col // s % 2 == 0)
                                 for s in (1, 2, 4, 8, 16, 32, 64)], 1),
        "merge1_t": (row // 2 == col // 2) & (row % 2 == 0) & (col % 2 == 1),
        "iota_blk": np.tile(np.arange(BLK), (P, 1)), "iota_m99": np.tile(np.arange(8) - 99, (P, 1)),
        "valid": np.stack([i >= 0, i >= 0, i < N_TOK[2]], 1),
        "invalid": np.stack([i * 0, i * 0, np.where(i < N_TOK[2], 0, 1e6)], 1),
        "thresh": np.tile(BLK * np.arange(5), (P, 1)), "iota_list": np.tile(np.arange(MAX_BLOCKS), (P, 1)),
        "half_neg": np.full((P, 16), -0.5),
    }
    lg = np.log(f(1.0) - f(2.0) ** (f(-5.0) - np.arange(4, dtype=f))).astype(f)
    rel = (row - col).astype(f)
    c["ret_decay"] = np.concatenate([np.where(rel >= 0, np.exp(np.where(rel >= 0, rel, f(0)) * g), 0) for g in lg], 1)
    c["ret_q"] = np.exp((i[:, None] + 1).astype(f) * lg)
    c["ret_k"] = np.concatenate([np.exp(np.minimum(n - 1 - i, P)[:, None].astype(f) * lg) for n in (128, 32)], 1)
    c["ret_c"] = np.concatenate([np.tile(np.exp(f(n) * lg), (P, 1)) for n in (128, 32)], 1)
    inv = f(10000.0) ** (-np.arange(64, dtype=f) / f(64))
    cos, sin = [], []
    for t in range(TILES):
        pos = (128 * t + i).astype(f)
        ang = (pos[:, None] * inv[None, :]).astype(f)
        for scale in (f(1.0), f(P) ** f(-0.5)):
            cos.append(np.cos(ang) * scale)
            sin.append(np.sin(ang) * scale)
    c["rot_cos"], c["rot_sin"] = np.concatenate(cos, 1), np.concatenate(sin, 1)
    return np.concatenate([np.asarray(c[n], f).reshape(P, w) for n, w in _SIZES], 1)


def kernel(**inputs):
    import numpy as np
    import concourse.bacc as bacc
    from concourse.bass_utils import run_bass_kernel_spmd

    nc = bacc.Bacc("TRN2", target_bir_lowering=False, num_devices=1)
    x = {k: np.ascontiguousarray(inputs[k]) for k in _IN}
    x["const"] = constants()
    x["conv_taps"] = np.ascontiguousarray(np.asarray(inputs["c_conv_w"])[0].reshape(4, 24, P).transpose(2, 1, 0))
    x["conv_state"] = np.ascontiguousarray(
        np.asarray(inputs["state_gdn_conv"])[0, 0].reshape(3, 24, P).transpose(2, 1, 0))
    x["state_n_t"] = np.ascontiguousarray(np.asarray(inputs["state_mlstm_n"])[0, 0].T)
    arrays = {f"in_{k}": v for k, v in x.items()}
    a = {k: nc.dram_tensor(f"in_{k}", v.shape, F32, kind="ExternalInput").ap() for k, v in x.items()}
    for k, s in _OUTS.items():
        a[k] = nc.dram_tensor(k, s, F32, kind="ExternalOutput").ap()
    a["block_rows"] = nc.dram_tensor("block_rows", (MAX_BLOCKS * BLK, D), F32, kind="Internal").ap()
    trunk(nc, a)
    r = run_bass_kernel_spmd(nc, [arrays], core_ids=[0]).results[0]
    tails = r["out_tails"].transpose(2, 1, 0).reshape(2, 1, 1, 3, 3072)
    c, n, m = r["out_c"], r["out_n"].transpose(0, 2, 1), r["out_m"]
    sides = [(c[g][None, None], n[g][None, None], m[g][None], r["out_ret"][g][None, None],
              r["out_gdn"][g][None, None], tails[g]) for g in range(2)]
    return (r["y_prompt"], r["y_sample"], *sides[0], *sides[1])
```

```python
from contextlib import ExitStack

import concourse.bass as bass
from concourse import mybir

F32 = mybir.dt.float32
I32 = mybir.dt.int32
ALU = mybir.AluOpType
ACT = mybir.ActivationFunctionType
X_AXIS = mybir.AxisListType.X

P = 128
D = 1024
KT = D // P
N_TOK = [128, 128, 32]
TILES = 3
PAD = 3
COL = [PAD, PAD + 128, 2 * PAD + 256]
COLS = 2 * PAD + 256 + 32
HEADS = 8
NEXP, NGRP, EPG, F = 32, 4, 8, 512
BLK = 64
MAX_BLOCKS = 44
EPS = 1e-6
BIG = 1e30

_SIZES = [("ident", 128), ("tri_incl", 128), ("tri_strict", 128), ("ones", 128), ("negmask", 128),
          ("strict", 128), ("merge", 7 * 128), ("merge1_t", 128),
          ("ret_decay", 512), ("rot_cos", 3 * 128), ("rot_sin", 3 * 128), ("ret_q", 4), ("ret_k", 8),
          ("ret_c", 8), ("iota_pair", 2 * BLK), ("iota_m99", 8), ("valid", 3), ("invalid", 3),
          ("thresh", 5), ("iota_list", MAX_BLOCKS), ("list_first", MAX_BLOCKS), ("slot_first", NEXP), ("slot_more", NEXP), ("half_neg", 16)]
CONST = {}
_at = 0
for _n, _w in _SIZES:
    CONST[_n] = (_at, _w)
    _at += _w
CONST_COLS = _at


class Event:

    def __init__(self, sem):
        self.sem, self.made, self.seen = sem, 0, {}

    def mark(self, ins, by=1):
        self.made += by
        ins.then_inc(self.sem, by)

    def wait(self, eng, by=1):
        key = id(eng)
        self.seen[key] = self.seen.get(key, 0) + by
        eng.wait_ge(self.sem, self.seen[key])


class InOrder:

    def __init__(self, eng, event):
        self.eng, self.event = eng, event

    def __call__(self, ins, event=None):
        ev = event or self.event
        ev.mark(ins)
        self.eng.wait_ge(ev.sem, ev.made)


class Lane:

    def __init__(self, full, taken, banks):
        self.full, self.taken, self.banks = full, taken, banks
        self.filled = self.opened = 0

    def open(self, pe):
        if self.filled >= 2:
            pe.wait_ge(self.taken.sem, self.filled - 1)
        return self.banks[self.filled % 2]

    def close(self, ins):
        self.filled += 1
        self.full.mark(ins)

    def take(self, eng):
        self.full.wait(eng)
        self.opened += 1
        return self.banks[(self.opened - 1) % 2]


def trunk(nc, a):
    with ExitStack() as ctx:
        def sb(name, shape, dt=F32):
            return ctx.enter_context(nc.sbuf_tensor(name, shape, dt))

        def sem(name):
            return ctx.enter_context(nc.semaphore(name))

        def ev(name):
            return Event(sem(name))

        W = sb("W", [P, 6, 4096])
        const = sb("const", [P, CONST_COLS])
        zT = sb("zT", [P, 32, COLS])
        TM = sb("TM", [P, 32, P])
        X = sb("X", [P, TILES, D])
        HN = sb("HN", [P, TILES, D])
        HT = sb("HT", [P, KT, COLS])
        gain = sb("gain", [P, D])
        state2 = sb("state2", [P, HEADS, P])
        sm = sb("sm", [P, 436])
        small_w = sb("small_w", [P, KT, 36])
        hgain = sb("hgain", [P, 2, P])
        blocks_i = sb("blocks_i", [1, MAX_BLOCKS], I32)
        banks = [ctx.enter_context(nc.psum_tensor(f"bank{i}", [P, 512], F32)) for i in range(8)]

        def cst(name):
            o, w = CONST[name]
            return const[:, o:o + w]

        ident, ones, tri_incl, tri_strict = cst("ident"), cst("ones"), cst("tri_incl"), cst("tri_strict")
        ws = W[:, 4:6, :].rearrange("p s n -> p (s n)")
        hs = HN[:].rearrange("p t n -> p (t n)")
        zf = zT[:].rearrange("p c n -> p (c n)")

        def heads4(ap):
            return ap.rearrange("p (h n) -> p h n", n=P)

        qT = [heads4(ws[:, 512 * i:512 * i + 512]) for i in range(2)]
        kT = [heads4(ws[:, 1024 + 512 * i:1536 + 512 * i]) for i in range(2)]
        AT, TI, UI, YI = [[heads4(ws[:, 2048 + 1024 * j + 512 * i:2560 + 1024 * j + 512 * i])
                           for i in range(2)] for j in range(4)]
        GAM = [heads4(ws[:, 6144 + 512 * i:6656 + 512 * i]) for i in range(2)]
        Yout = ws[:, 7168:8192].rearrange("p (h n) -> p h n", n=P)
        state1 = hs[:, 0:1024].rearrange("p (h n) -> p h n", n=P)
        Sm, ST, kw, tmp = [heads4(hs[:, 1024 + 512 * i:1536 + 512 * i]) for i in range(4)]
        states = [state1, state1, state2[:, :, :]]
        xg = zf[:, 0:1024].rearrange("p (k u s) -> p k u s", u=2, s=BLK)
        sg = [zf[0:BLK, 1024 + F * u:1024 + F * (u + 1)] for u in range(2)]
        hid = [zf[0:BLK, 2048 + F * u:2048 + F * (u + 1)] for u in range(2)]
        hidT = [zf[:, 3072 + 256 * u:3328 + 256 * u] for u in range(2)]
        ys = [zf[:, 3584 + 512 * u:4096 + 512 * u] for u in range(2)]
        oh = [zf[:, 4608 + 384 * k:4992 + 384 * k].rearrange("p (t s) -> p t s", s=2 * BLK) for k in range(2)]
        route = zf[:, 5400:7600]
        junk = zf[:, 8384:9408]
        convbuf = [ws[:, 1200 * i:1200 * i + 4 * (COLS - PAD)].rearrange("p (c n) -> p c n", c=4) for i in range(2)]
        cconv = ws[:, 6656:6824].rearrange("p (c n) -> p c n", n=7)
        tails = ws[:, 6848:6992].rearrange("p (c n) -> p c n", n=6)
        rotc = cst("rot_cos").rearrange("p (t j n) -> p t j n", t=3, j=2)
        rots = cst("rot_sin").rearrange("p (t j n) -> p t j n", t=3, j=2)
        merge = cst("merge").rearrange("p (l n) -> p l n", n=P)
        yg = TM[:].rearrange("p c n -> p (c n)").rearrange("p (b k n) -> p b k n", b=2, k=2)

        _sm = [0]

        def small(w):
            _sm[0] += w
            return sm[:, _sm[0] - w:_sm[0]]

        sumsq, rstd = small(3), small(3)
        g16 = small(48)
        gb1, gb2 = small(8), small(8)
        lg = small(24)
        bcum = small(24)
        acol = small(24)
        t24a, t24b, t24c = small(24), small(24), small(24)
        beta = small(24)
        mprev = [small(4), small(4)]
        nstate = [small(4), small(4)]
        gm = small(8)
        gl = small(8)
        negg = small(4)
        ein, eout = small(32), small(32)
        den, den2 = small(4), small(4)
        hss, hrs = small(16), small(16)
        m1 = small(4)
        pw = [small(6)]
        dk = small(6)
        rb = small(36)
        slots_i = small(6).bitcast(I32).rearrange("p (k t) -> p k t", t=TILES)

        order = {e: ev(f"{e}_order") for e in ("dve", "act", "pool")}
        lanes = [Lane(ev("lane_dve_full"), ev("lane_dve_taken"), banks[0:2]),
                 Lane(ev("lane_act_full"), ev("lane_act_taken"), banks[2:4])]
        L0, L1 = lanes
        const_in, x_in = ev("const_in"), [ev(f"x_in{i}") for i in range(3)]
        gain0_in, gain_in, gain_used = ev("gain0_in"), ev("gain_in"), ev("gain_used")
        piece_in = [ev(f"piece_in{i}") for i in range(4)]
        scratch_free = []
        piece_done = []
        small_in = [ev(f"small_in{i}") for i in range(4)]
        small_used = ev("small_used")
        x_ready, ss_ready, rs_ready, hn_ready = ev("x_ready"), ev("ss_ready"), ev("rs_ready"), ev("hn_ready")
        ht_dve, ht_act = ev("ht_dve"), ev("ht_act")
        names = ["z_ready", "tm_dve", "tm_act", "gate_exp_in", "gate_exp", "lf_ready", "diag_ready", "gm_ready",
                 "ein_ready", "eout_ready", "rot_ready", "qkT_dve", "qkT_act", "s_ready", "st_ready", "kw_ready",
                 "state_ready", "r_ready", "vn_ready", "am_ready", "p_ready", "a_ready", "at_ready", "tu_ready",
                 "yi_ready", "hss_ready", "hrs_ready", "y_ready", "yT_dve", "yT_act", "tile_done",
                 "conv_raw", "conv_in", "conv_done", "logits_exp_in", "logits_exp", "choice_ready", "nb_ready",
                 "nbb_ready", "list_ready", "blocks_ready", "qkn_ready", "state_done", "tails_done",
                 "hn_out", "conv_used", "zero_rows", "rows_clear"]
        E = {n: ev(n) for n in names}
        state_in = ev("state_in")
        out_written, y_written = ev("out_written"), ev("y_written")
        moe = [dict(
            w_in=[sem(f"moe{l}_w_in{s}") for s in range(6)],
            gate_used=sem(f"moe{l}_gate_used"), up_used=sem(f"moe{l}_up_used"), down_used=sem(f"moe{l}_down_used"),
            onehot=sem(f"moe{l}_onehot"), gathered=sem(f"moe{l}_gathered"),
            xg_dve=sem(f"moe{l}_xg_dve"), xg_act=sem(f"moe{l}_xg_act"),
            silu=sem(f"moe{l}_silu"), hidden=sem(f"moe{l}_hidden"), flipped=sem(f"moe{l}_flipped"),
            hiddenT=sem(f"moe{l}_hiddenT"), y=[sem(f"moe{l}_y{u}") for u in range(2)],
            step=sem(f"moe{l}_step"),
            stored=[sem(f"moe{l}_stored{u}") for u in range(2)],
            yg_in=[sem(f"moe{l}_yg_in{b}") for b in range(2)], yg_used=sem(f"moe{l}_yg_used"),
        ) for l in range(2)]

        states_out = sem("states_out")

        block = ctx.enter_context(nc.Block())

        def nblk_reg(eng):
            count = eng.value_load(blocks_i[0:1, MAX_BLOCKS - 1:MAX_BLOCKS], min_val=NEXP, max_val=MAX_BLOCKS - 2)
            return eng.snap((count + 1) // 2)

        @block.tensor
        def _(pe):
            def mm(out, lhsT, rhs, start=True, stop=True):
                return nc.tensor.matmul(out, lhsT, rhs, start=start, stop=stop)

            def flip(out, src, n):
                return nc.tensor.transpose(out, src, ident[:n, :n])

            def transpose_tile(src, t, n):
                for g in range(2):
                    bank = lanes[g].open(pe)
                    for j in range(4):
                        last = flip(bank[:, j * P:j * P + n], src(4 * g + j)[:n], n)
                    lanes[g].close(last)

            def norm():
                for t in range(TILES):
                    hn_ready.wait(pe)
                    transpose_tile(lambda c: HN[:, t, c * P:c * P + P], t, N_TOK[t])
                ht_dve.wait(pe, 3)
                ht_act.wait(pe, 3)

            def small_projection(w, which, loads):
                small_in[which].wait(pe, 16 * loads)
                bank = L0.open(pe)
                for t in range(TILES):
                    n, c = N_TOK[t], COL[t]
                    for k in range(KT):
                        last = mm(bank[:n, 64 * t:64 * t + w], HT[:, k, c:c + n], small_w[:, k, 0:w],
                                  k == 0, k == KT - 1)
                L0.close(last)

            def input_projection():
                for p in range(8):
                    piece_in[p % 4].wait(pe, 16)
                    w = W[:, p % 4, :].rearrange("p (k n) -> p k n", k=KT)
                    for j in range(4):
                        bank = L1.open(pe)
                        for k in range(KT):
                            last = mm(bank[:, 0:COLS], w[:, k, j * P:j * P + P], HT[:, k, :], k == 0, k == KT - 1)
                        L1.close(last)
                    piece_done.append((L1.full.sem, L1.full.made))

            def output_projection():
                E["yT_dve"].wait(pe, 3)
                E["yT_act"].wait(pe, 3)
                for p in (8, 9):
                    piece_in[p % 4].wait(pe, 16)
                    w = W[:, p % 4, :].rearrange("p (k n) -> p k n", k=KT)
                    for t in range(TILES):
                        n, c = N_TOK[t], COL[t]
                        bank = L0.open(pe)
                        for k in range(KT):
                            last = mm(bank[:n, :], HT[:, k, c:c + n], w[:, k, :], k == 0, k == KT - 1)
                        L0.close(last)
                    piece_done.append((L0.full.sem, L0.full.made))

            def to_tokens(t, first):
                n, c = N_TOK[t], COL[t]
                for g in range(first, 8):
                    lane = lanes[g % 2]
                    bank = lane.open(pe)
                    for j in range(4):
                        last = flip(bank[:n, j * P:j * P + P], zT[:, 4 * g + j, c:c + n], P)
                    lane.close(last)
                E["tm_dve"].wait(pe)
                E["tm_act"].wait(pe)

            def row_broadcast(n):
                E["diag_ready"].wait(pe)
                bank = L0.open(pe)
                L0.close(mm(heads4(bank[:n, :])[:, :, :n], ones[:n, :n], tmp[:n, :, :n]))

            def last_row(t, w):
                n = N_TOK[t]
                sel = ident[:n, n - 1:n].to_broadcast([n, P])
                bank = L0.open(pe)
                L0.close(mm(bank[:, 0:w], sel, gm[:n, 0:w]))

            def half(t, f, q, k, vchunk, kwise, mlstm=False, delta=False):
                n = N_TOK[t]
                st = states[t]
                bank = L0.open(pe)
                for h in range(4):
                    last = mm(bank[:n, h * P:h * P + n], q(h), k(h))
                L0.close(last)
                if delta:
                    bank = L0.open(pe)
                    for h in range(4):
                        last = mm(bank[:n, h * P:h * P + P], k(h), st[:, 4 * f + h, :])
                    L0.close(last)
                E["s_ready"].wait(pe)
                bank = L1.open(pe)
                for h in range(4):
                    last = flip(bank[:n, h * P:h * P + n], Sm[:n, h, :n], n)
                L1.close(last)
                bank = L0.open(pe)
                for h in range(4):
                    last = mm(bank[:n, h * P:h * P + P], q(h), st[:, 4 * f + h, :])
                L0.close(last)
                if mlstm:
                    bank = L0.open(pe)
                    for h in range(4):
                        last = mm(bank[:n, h:h + 1], q(h), nstate[t // 2][:, h:h + 1])
                    L0.close(last)
                if delta:
                    E["r_ready"].wait(pe)
                    bank = L1.open(pe)
                    for h in range(4):
                        last = mm(bank[:n, h * P:h * P + P], UI[f][:n, h, :n], TM[:n, vchunk + h, :])
                    L1.close(last)
                    E["vn_ready"].wait(pe)
                v = (lambda h: YI[f][:n, h, :]) if delta else (lambda h: TM[:n, vchunk + h, :])
                E["st_ready"].wait(pe)
                bank = L0.open(pe)
                for h in range(4):
                    last = mm(bank[:n, h * P:h * P + P], ST[:n, h, :n], v(h))
                L0.close(last)
                E["kw_ready"].wait(pe)
                bank = L0.open(pe)
                for h in range(4):
                    last = mm(bank[:, h * P:h * P + P], kw[:n, h, :], v(h))
                L0.close(last)
                if mlstm:
                    bank = L0.open(pe)
                    for h in range(4):
                        last = mm(bank[:, h:h + 1], kw[:n, h, :], ones[:n, 0:1])
                    L0.close(last)

            def finish_tile(t):
                E["y_ready"].wait(pe)
                transpose_tile(lambda c: Yout[:, c, :], t, N_TOK[t])

            def cumulate(w):
                E["lf_ready"].wait(pe)
                bank = L0.open(pe)
                L0.close(mm(bank[:, 0:3 * w], tri_incl, lg[:, 0:3 * w]))

            def layer_ab():
                norm()
                small_projection(8, 0, 4)
                cumulate(4)
                input_projection()
                E["z_ready"].wait(pe)
                for t in range(TILES):
                    n, c = N_TOK[t], COL[t]
                    to_tokens(t, 1)
                    row_broadcast(n)
                    E["gm_ready"].wait(pe)
                    last_row(t, 8)
                    E["state_ready"].wait(pe)
                    half(t, 0, lambda h: zT[:, h, c:c + n], lambda h: zT[:, 4 + h, c:c + n], 8, None, mlstm=True)
                    E["rot_ready"].wait(pe)
                    for g, base in ((0, 0), (1, 4)):
                        bank = lanes[g].open(pe)
                        for h in range(4):
                            last = flip(bank[:, h * P:h * P + n], rot(base + h)[:n], n)
                        lanes[g].close(last)
                    E["qkT_dve"].wait(pe)
                    E["qkT_act"].wait(pe)
                    half(t, 1, lambda h: qT[0][:, h, :n], lambda h: kT[0][:, h, :n], 24, None)
                    finish_tile(t)
                scratch_free.append((L1.full.sem, L1.full.made))
                output_projection()

            def rot(c):
                return AT[c // 4][:, c % 4, :]

            def layer_c():
                norm()
                small_projection(16, 2, 6)
                cumulate(8)
                input_projection()
                E["z_ready"].wait(pe)
                for t in range(TILES):
                    n, c = N_TOK[t], COL[t]
                    to_tokens(t, 0)
                    E["qkn_ready"].wait(pe)
                    for i, (dst, base) in enumerate(((0, 0), (1, 4), (2, 8), (3, 12))):
                        lane = lanes[i % 2]
                        bank = lane.open(pe)
                        for h in range(4):
                            last = flip(bank[:, h * P:h * P + n], TM[:n, base + h, :], n)
                        lane.close(last)
                    E["qkT_dve"].wait(pe)
                    E["qkT_act"].wait(pe)
                    last_row(t, 8)
                    for f in range(2):
                        row_broadcast(n)
                    for f in range(2):
                        bank = L0.open(pe)
                        for h in range(4):
                            last = mm(bank[:n, h * P:h * P + n], kT[f][:, h, :n], kT[f][:, h, :n])
                        L0.close(last)
                        E["a_ready"].wait(pe)
                        bank = L1.open(pe)
                        for h in range(4):
                            last = flip(bank[:n, h * P:h * P + n], tmp[:n, h, :n], n)
                        L1.close(last)
                    levels = 6 if n == 128 else 4
                    for lv in range(levels):
                        for f in range(2):
                            E["tu_ready"].wait(pe)
                            bank = L0.open(pe)
                            for h in range(4):
                                last = mm(bank[:n, h * P:h * P + n], AT[f][:n, h, :n], TI[f][:n, h, :n])
                            L0.close(last)
                        for f in range(2):
                            E["yi_ready"].wait(pe)
                            bank = L0.open(pe)
                            for h in range(4):
                                last = mm(bank[:n, h * P:h * P + n], UI[f][:n, h, :n], YI[f][:n, h, :n])
                            L0.close(last)
                            bank = L0.open(pe)
                            for h in range(4):
                                last = mm(bank[:n, h * P:h * P + n], YI[f][:n, h, :n], UI[f][:n, h, :n])
                            L0.close(last)
                    for f in range(2):
                        E["tu_ready"].wait(pe)
                    E["state_ready"].wait(pe)
                    for f in range(2):
                        half(t, f, lambda h: qT[f][:, h, :n], lambda h: kT[f][:, h, :n], 16 + 4 * f, None, delta=True)
                    finish_tile(t)
                scratch_free.append((L1.full.sem, L1.full.made))
                output_projection()

            def experts(l):
                norm()
                small_projection(36, 1 + 2 * l, 4)
                E["choice_ready"].wait(pe)
                M = route[:, 0:96].rearrange("p (t e) -> p t e", e=NEXP)
                bank = L0.open(pe)
                for t in range(TILES):
                    last = mm(bank[0:NEXP, 0:1], M[:, t, :], ones[:, 0:1], t == 0, t == 2)
                L0.close(last)
                bank = L0.open(pe)
                for t in range(TILES):
                    for s in range(t + 1):
                        last = mm(bank[:, 32 * t:32 * t + 32], tri_strict if s == t else ones, M[:, s, :],
                                  s == 0, s == t)
                L0.close(last)
                E["nb_ready"].wait(pe)
                nbc, nbb = route[0:NEXP, 700:701], route[0:NEXP, 704:832]
                bank = L0.open(pe)
                L0.close(mm(bank[0:NEXP, 0:1], tri_incl[0:NEXP, 0:NEXP], nbc))
                bank = L0.open(pe)
                L0.close(mm(bank[:, 0:NEXP], nbb, tri_strict[0:NEXP, 0:NEXP]))
                E["list_ready"].wait(pe)
                bank = L0.open(pe)
                L0.close(mm(bank[0:1, 0:MAX_BLOCKS], ones[0:NEXP, 0:1], route[0:NEXP, 832:832 + MAX_BLOCKS]))
                E["blocks_ready"].wait(pe)
                m = moe[l]
                nb = nblk_reg(pe)
                for used in ("gate_used", "up_used", "down_used"):
                    pe.sem_inc(m[used], 2)

                def gather(count):
                    pe.wait_ge(m["onehot"], count)
                    for k in range(KT):
                        for t in range(TILES):
                            n = N_TOK[t]
                            last = mm(banks[k // 4][:, k % 4 * P:k % 4 * P + P], HN[:n, t, k * P:k * P + P],
                                      oh[0][:n, t, :], t == 0, t == 2)
                    last.then_inc(m["gathered"], 1)

                def gate_up(u, b):
                    pe.wait_ge(m["w_in"][3 * u], 16 * b + 16)
                    pe.wait_ge(m["w_in"][3 * u + 1], 16 * b + 16)
                    w = [W[:, 3 * u + s, :].rearrange("p (k n) -> p k n", k=KT) for s in range(2)]
                    for k in range(KT):
                        for s, used in ((0, "gate_used"), (1, "up_used")):
                            ins = mm(banks[2 + u][BLK * s:BLK * s + BLK, :], xg[:, k, u, :], w[s][:, k, :],
                                     k == 0, k == KT - 1)
                            if k == KT - 1:
                                ins.then_inc(m[used], 1)

                def flip_hidden(u, i):
                    pe.wait_ge(m["hidden"], i + 1)
                    for j in range(4):
                        last = mm(banks[4 + u][:, j * BLK:j * BLK + BLK], hid[u][:, j * P:j * P + P], ident[:BLK, :BLK])
                    last.then_inc(m["flipped"], 1)

                def down(u, b, i):
                    pe.wait_ge(m["hiddenT"], i + 1)
                    pe.wait_ge(m["w_in"][3 * u + 2], 16 * b + 16)
                    pe.wait_ge(m["y"][u], b + 1)
                    w = W[:, 3 * u + 2, :].rearrange("p (k n) -> p k n", k=4)
                    for j in range(4):
                        for h in range(2):
                            last = mm(banks[6 + u][BLK * h:BLK * h + BLK, :], hidT[u][:, j * BLK:j * BLK + BLK],
                                      w[:, j, 512 * h:512 * h + 512], j == 0, j == 3)
                    last.then_inc(m["down_used"], 1)

                gather(1)
                with pe.Fori(0, nb) as b:
                    pe.wait_ge(m["xg_dve"], b + 1)
                    pe.wait_ge(m["xg_act"], b + 1)
                    gate_up(0, b)
                    gate_up(1, b)
                    flip_hidden(0, 2 * b)
                    gather(b + 2)
                    flip_hidden(1, 2 * b + 1)
                    down(0, b, 2 * b)
                    down(1, b, 2 * b + 1)

            const_in.wait(pe, 16)
            layer_ab()
            experts(0)
            layer_c()
            experts(1)

        @block.scalar
        def _(act):
            do = InOrder(act, order["act"])

            def norm():
                for t in range(TILES):
                    n = N_TOK[t]
                    x_ready.wait(act)
                    do(nc.scalar.activation(junk[:n, :], X[:n, t, :], ACT.Square, accum_out=sumsq[:n, t:t + 1]),
                       ss_ready)

            def take_transposed(event):
                for t in range(TILES):
                    n, c = N_TOK[t], COL[t]
                    take_one(t, event)

            def take_one(t, event):
                n, c = N_TOK[t], COL[t]
                bank = L1.take(act)
                do(nc.scalar.copy(HT[:, 4:8, c:c + n], heads4(bank[:, :])[:, :, :n]), L1.taken)
                event.mark(act.nop())

            def log_gate(w, e):
                E["gate_exp_in"].wait(act)
                do(nc.scalar.activation(t24b[:, 0:3 * w], t24a[:, 0:3 * w], ACT.Exp, scale=-1.0))
                do(nc.scalar.activation(t24b[:, 0:3 * w], t24b[:, 0:3 * w], ACT.Ln, bias=ones[:, 0:1]))
                if e:
                    do(nc.scalar.activation(t24c[:, :], beta[:, :], ACT.Exp, scale=-1.0))
                    do(nc.scalar.activation(gb1, gb1, ACT.Exp))
                E["gate_exp"].mark(act.nop())

            def to_tokens(t, groups):
                n = N_TOK[t]
                if not E["rows_clear"].seen.get(id(act)):
                    E["rows_clear"].wait(act, 16)
                if t:
                    E["tile_done"].wait(act)
                for g in groups:
                    bank = L1.take(act)
                    do(nc.scalar.copy(TM[:n, 4 * g:4 * g + 4, :], heads4(bank[:n, :])), L1.taken)
                E["tm_act"].mark(act.nop())

            def scores_T(n):
                bank = L1.take(act)
                do(nc.scalar.copy(ST[:n, :, :n], heads4(bank[:n, :])[:, :, :n]), L1.taken)
                E["st_ready"].mark(act.nop())

            def layer_ab():
                norm()
                take_transposed(ht_act)
                log_gate(4, False)
                for c in range(32):
                    bank = L1.take(act)
                    func = ACT.Sigmoid if 12 <= c < 16 else ACT.Silu if c >= 28 else ACT.Copy
                    do(nc.scalar.activation(zT[:, c, :], bank[:, 0:COLS], func,
                                            scale=float(P) ** -0.5 if 4 <= c < 8 else 1.0), L1.taken)
                E["z_ready"].mark(act.nop())
                for t in range(TILES):
                    n = N_TOK[t]
                    to_tokens(t, (1, 3, 5, 7))
                    E["ein_ready"].wait(act)
                    do(nc.scalar.activation(eout[:n, 0:12], ein[:n, 0:12], ACT.Exp))
                    do(nc.scalar.activation(eout[:, 12:16], ein[:, 12:16], ACT.Exp), E["eout_ready"])
                    for h in range(4):
                        do(nc.scalar.activation(GAM[0][:n, h, :n], GAM[1][:n, h, :n], ACT.Exp,
                                                bias=negg[:n, h:h + 1]))
                    E["p_ready"].mark(act.nop())
                    scores_T(n)
                    bank = L1.take(act)
                    do(nc.scalar.copy(kT[0][:, :, :n], heads4(bank[:, :])[:, :, :n]), L1.taken)
                    E["qkT_act"].mark(act.nop())
                    scores_T(n)
                    take_one(t, E["yT_act"])

            def layer_c():
                norm()
                take_transposed(ht_act)
                log_gate(8, True)
                for p in range(8):
                    for j in range(4):
                        bank = L1.take(act)
                        do(nc.scalar.activation(zT[:, 4 * p + j, :], bank[:, 0:COLS],
                                                ACT.Copy if p < 6 else ACT.Silu), L1.taken)
                    if p < 6:
                        E["conv_raw"].mark(act.nop())
                    if 1 <= p <= 6:
                        q = p - 1
                        E["conv_done"].wait(act)
                        do(nc.scalar.activation(zT[:, 4 * q:4 * q + 4, PAD:COLS], convbuf[q % 2], ACT.Silu),
                           E["conv_used"])
                E["z_ready"].mark(act.nop())
                for t in range(TILES):
                    n = N_TOK[t]
                    to_tokens(t, (1, 3, 5, 7))
                    for i in range(2):
                        bank = L1.take(act)
                        dst = (qT, kT)[i][1]
                        do(nc.scalar.copy(dst[:, :, :n], heads4(bank[:, :])[:, :, :n]), L1.taken)
                    E["qkT_act"].mark(act.nop())
                    E["ein_ready"].wait(act)
                    do(nc.scalar.activation(eout[:n, 0:16], ein[:n, 0:16], ACT.Exp))
                    do(nc.scalar.activation(eout[:, 16:24], ein[:, 16:24], ACT.Exp), E["eout_ready"])
                    for f in range(2):
                        E["am_ready"].wait(act)
                        for h in range(4):
                            do(nc.scalar.activation(GAM[f][:n, h, :n], GAM[f][:n, h, :n], ACT.Exp,
                                                    bias=gm[:n, 4 * f + h:4 * f + h + 1]))
                        E["p_ready"].mark(act.nop())
                    for f in range(2):
                        bank = L1.take(act)
                        do(nc.scalar.copy(AT[f][:n, :, :n], heads4(bank[:n, :])[:, :, :n]), L1.taken)
                        E["at_ready"].mark(act.nop())
                    for f in range(2):
                        scores_T(n)
                        bank = L1.take(act)
                        do(nc.scalar.copy(YI[f][:n, :, :], heads4(bank[:n, :])), L1.taken)
                        E["vn_ready"].mark(act.nop())
                    take_one(t, E["yT_act"])

            def experts(l):
                act.wait_ge(states_out, l + 1)
                norm()
                take_transposed(ht_act)
                E["logits_exp_in"].wait(act)
                do(nc.scalar.activation(route[:, 300:312], route[:, 300:312], ACT.Exp), E["logits_exp"])
                E["logits_exp_in"].wait(act)
                do(nc.scalar.activation(route[:, 320:323], route[:, 320:323], ACT.Exp), E["logits_exp"])
                E["blocks_ready"].wait(act)
                m = moe[l]
                nb = nblk_reg(act)
                act.sem_inc(m["y"][0], 1)

                def fetched(count):
                    act.wait_ge(m["gathered"], count)
                    nc.scalar.copy(xg[:, 4:8].rearrange("p k u s -> p (k u s)"), banks[1][:, :]
                                   ).then_inc(m["xg_act"], 1)

                fetched(1)
                with act.Fori(0, nb) as b:
                    for u in range(2):
                        i = 2 * b + u
                        act.wait_ge(m["gate_used"], i + 3)
                        nc.scalar.activation(sg[u], banks[2 + u][0:BLK, :], ACT.Silu).then_inc(m["silu"], 1)
                    fetched(b + 2)
                    act.wait_ge(m["down_used"], 2 * b + 3)
                    act.wait_ge(m["stored"][0], 32 * b)
                    nc.scalar.copy(ys[0], banks[6][:, :]).then_inc(m["y"][0], 1)
                    for u in range(2):
                        act.wait_ge(m["y"][u], b + 2)
                        for h in range(2):
                            act.dma_start(a["block_rows"][bass.ds(BLK * (2 * b + u), BLK), 512 * h:512 * h + 512],
                                          ys[u][BLK * h:BLK * h + BLK, :]).then_inc(m["stored"][u], 16)

            layer_ab()
            experts(0)
            layer_c()
            experts(1)
            norm()

        @block.vector
        def _(dve):
            do = InOrder(dve, order["dve"])
            v = nc.vector

            def tt(out, i0, i1, op, event=None):
                do(v.tensor_tensor(out, i0, i1, op), event)

            def ts(out, i0, s1, s2=None, op0=ALU.mult, op1=ALU.bypass, event=None):
                if s2 is None:
                    do(v.tensor_scalar(out, i0, s1, None, op0), event)
                else:
                    do(v.tensor_scalar(out, i0, s1, s2, op0, op1), event)

            def cp(out, i, event=None):
                do(v.tensor_copy(out, i), event)

            def red(out, i, op=ALU.add, event=None):
                do(v.tensor_reduce(out, i, X_AXIS, op), event)

            def signal(event):
                event.mark(dve.nop())

            def bc_last(ap, n):
                return ap.unsqueeze(len(ap.shape)).to_broadcast(list(ap.shape) + [n])

            def bc_mid(ap, n):
                return ap.unsqueeze(1).to_broadcast([ap.shape[0], n] + list(ap.shape[1:]))

            def norm(last=False, first=False):
                (gain0_in if first else gain_in).wait(dve, 16)
                for t in range(TILES):
                    n = N_TOK[t]
                    rs_ready.wait(dve)
                    do(v.scalar_tensor_tensor(out=HN[:n, t, :], in0=X[:n, t, :], scalar=rstd[:n, t:t + 1],
                                              in1=gain[:n, :], op0=ALU.mult, op1=ALU.mult),
                       E["hn_out"] if last else hn_ready)
                if not last:
                    signal(gain_used)
                    for t in range(TILES):
                        take_one(t, ht_dve)

            def take_one(t, event):
                n, c = N_TOK[t], COL[t]
                bank = L0.take(dve)
                cp(HT[:, 0:4, c:c + n], heads4(bank[:, :])[:, :, :n], L0.taken)
                signal(event)

            def gates(w):
                g3 = g16[:, 0:3 * w].rearrange("p (t w) -> p t w", w=w)
                do(v.memset(g16, 0.0))
                bank = L0.take(dve)
                cp(g3[:, 0:2, :], bank[:, 0:128].rearrange("p (t w) -> p t w", w=64)[:, :, 0:w])
                cp(g3[:32, 2, :], bank[:32, 128:128 + w], L0.taken)
                signal(small_used)
                return g3

            def to_tokens(t, groups):
                n = N_TOK[t]
                for g in groups:
                    bank = L0.take(dve)
                    cp(TM[:n, 4 * g:4 * g + 4, :], heads4(bank[:n, :]), L0.taken)
                signal(E["tm_dve"])
                E["tm_act"].wait(dve)

            def diag(col, n):
                tt(tmp[:n, :, :n], bc_mid(ident[:n, :n], 4), bc_last(col, n), ALU.mult, E["diag_ready"])

            def half(t, f, gam, wq, wkk, dec, kchunk, vchunk, mlstm=False, delta=False):
                n = N_TOK[t]
                st = states[t][:, 4 * f:4 * f + 4, :]
                y = Yout[:, 4 * f:4 * f + 4, :]
                bank = L0.take(dve)
                tt(Sm[:n, :, :n], heads4(bank[:n, :])[:, :, :n], gam, ALU.mult, L0.taken)
                signal(E["s_ready"])
                if delta:
                    bank = L0.take(dve)
                    tt(tmp[:n], heads4(bank[:n, :]), bc_last(wq, P), ALU.mult, L0.taken)
                    tt(tmp[:n], TM[:n, vchunk:vchunk + 4, :], tmp[:n], ALU.subtract)
                    tt(TM[:n, vchunk:vchunk + 4, :], tmp[:n], bc_last(beta3[:n, t, 4 * f:4 * f + 4], P),
                       ALU.mult, E["r_ready"])
                tt(kw[:n], TM[:n, kchunk:kchunk + 4, :], bc_last(wkk, P), ALU.mult, E["kw_ready"])
                bank = L0.take(dve)
                tt(tmp[:n], heads4(bank[:n, :]), bc_last(wq, P), ALU.mult, L0.taken)
                if mlstm:
                    red(den[:n, :], Sm[:n, :, :n])
                    bank = L0.take(dve)
                    tt(den2[:n, :], bank[:n, 0:4], wq, ALU.mult, L0.taken)
                    tt(den[:n, :], den[:n, :], den2[:n, :], ALU.add)
                    ts(den2[:n, :], den[:n, :], -1.0)
                    tt(den[:n, :], den[:n, :], den2[:n, :], ALU.max)
                    tt(den[:n, :], den[:n, :], eout[:n, 4:8], ALU.max)
                    do(v.reciprocal(den[:n, :], den[:n, :]))
                bank = L0.take(dve)
                tt(y[:n], heads4(bank[:n, :]), tmp[:n], ALU.add, L0.taken)
                if mlstm:
                    tt(y[:n], y[:n], bc_last(den[:n, :], P), ALU.mult)
                tt(st, st, bc_last(dec, P), ALU.mult)
                bank = L0.take(dve)
                tt(st, st, heads4(bank[:, :]), ALU.add, L0.taken)
                if mlstm:
                    ns = nstate[t // 2]
                    tt(ns, ns, dec, ALU.mult)
                    bank = L0.take(dve)
                    tt(ns, ns, bank[:, 0:4], ALU.add, L0.taken)

            def head_norm(t, gates_c, two_gains):
                n = N_TOK[t]
                for f in range(2):
                    y = Yout[:n, 4 * f:4 * f + 4, :]
                    tt(tmp[:n], y, y, ALU.mult)
                    red(hss[:n, 4 * f:4 * f + 4], tmp[:n])
                signal(E["hss_ready"])
                for f in range(2):
                    g = TM[:n, gates_c[f]:gates_c[f] + 4, :]
                    tt(g, g, bc_mid(hgain[:n, f if two_gains else 0, :], 4), ALU.mult)
                E["hrs_ready"].wait(dve)
                for f in range(2):
                    y = Yout[:n, 4 * f:4 * f + 4, :]
                    g = TM[:n, gates_c[f]:gates_c[f] + 4, :]
                    tt(y, y, bc_last(hrs[:n, 4 * f:4 * f + 4], P), ALU.mult)
                    tt(y, y, g, ALU.mult)
                signal(E["y_ready"])
                signal(E["tile_done"])
                take_one(t, E["yT_dve"])

            def output_projection():
                for p in range(2):
                    for t in range(TILES):
                        n = N_TOK[t]
                        bank = L0.take(dve)
                        tt(X[:n, t, 512 * p:512 * p + 512], X[:n, t, 512 * p:512 * p + 512], bank[:n, :],
                           ALU.add, L0.taken)
                for t in range(TILES):
                    signal(x_ready)

            lg4 = lg[:, 0:12].rearrange("p (t w) -> p t w", w=4)
            lg8 = lg.rearrange("p (t w) -> p t w", w=8)
            b4 = bcum[:, 0:12].rearrange("p (t w) -> p t w", w=4)
            b8 = bcum.rearrange("p (t w) -> p t w", w=8)
            beta3 = beta.rearrange("p (t w) -> p t w", w=8)

            def layer_ab():
                norm(first=True)
                small_in[0].wait(dve, 64)
                g3 = gates(8)
                tt(g3, g3, bc_mid(gb1, 3), ALU.add)
                ab = t24a[:, 0:12].rearrange("p (t w) -> p t w", w=4)
                ts(ab, g3[:, :, 4:8], -1.0)
                tt(ab, ab, g3[:, :, 4:8], ALU.max, E["gate_exp_in"])
                ts(lg4, g3[:, :, 4:8], 0.0, op0=ALU.min)
                E["gate_exp"].wait(dve)
                tt(lg[:, 0:12], lg[:, 0:12], t24b[:, 0:12], ALU.subtract, E["lf_ready"])
                bank = L0.take(dve)
                cp(bcum[:, 0:12], bank[:, 0:12], L0.taken)
                a3 = acol[:, 0:12].rearrange("p (t w) -> p t w", w=4)
                tt(a3, g3[:, :, 0:4], b4, ALU.subtract)
                do(v.memset(state1, 0.0))
                do(v.memset(nstate[0], 0.0))
                do(v.memset(mprev[0], 0.0))
                state_in.wait(dve, 64)
                E["rows_clear"].wait(dve, 16)
                for t in range(TILES):
                    n, g = N_TOK[t], t // 2
                    mp = mprev[g]
                    if t == 0:
                        E["z_ready"].wait(dve)
                    to_tokens(t, (2, 4, 6))
                    diag(a3[:n, t, :], n)
                    bank = L0.take(dve)
                    tt(GAM[1][:n, :, :n], heads4(bank[:n, :])[:, :, :n], bc_mid(cst("negmask")[:n, :n], 4),
                       ALU.add, L0.taken)
                    red(m1[:n, :], GAM[1][:n, :, :n], ALU.max)
                    tt(gm[:n, 0:4], m1[:n, :], mp[:n, :], ALU.max)
                    tt(gm[:n, 4:8], gm[:n, 0:4], b4[:n, t, :], ALU.add, E["gm_ready"])
                    ts(negg[:n, :], gm[:n, 0:4], -1.0)
                    bank = L0.take(dve)
                    cp(gl, bank[:, 0:8], L0.taken)
                    tt(ein[:n, 0:4], mp[:n, :], gm[:n, 0:4], ALU.subtract)
                    ts(ein[:n, 4:8], gm[:n, 4:8], -1.0)
                    tt(ein[:n, 8:12], a3[:n, t, :], gl[:n, 0:4], ALU.subtract)
                    tt(ein[:, 12:16], mp, gl[:, 0:4], ALU.subtract)
                    cp(mp, gl[:, 4:8], E["ein_ready"])
                    signal(E["state_ready"])
                    E["eout_ready"].wait(dve)
                    E["p_ready"].wait(dve)
                    half(t, 0, GAM[0][:n, :, :n], eout[:n, 0:4], eout[:n, 8:12], eout[:, 12:16], 4, 8, mlstm=True)
                    for j in range(2):
                        cos = bc_mid(rotc[:n, t, j, :], 4)
                        sin = bc_mid(rots[:n, t, j, :], 4)
                        x1, x2 = TM[:n, 16 + 4 * j:20 + 4 * j, 0:64], TM[:n, 16 + 4 * j:20 + 4 * j, 64:128]
                        o, s = AT[j], TI[0]
                        tt(o[:n, :, 0:64], x1, cos, ALU.mult)
                        tt(s[:n, :, 0:64], x2, sin, ALU.mult)
                        tt(o[:n, :, 0:64], o[:n, :, 0:64], s[:n, :, 0:64], ALU.subtract)
                        tt(o[:n, :, 64:128], x1, sin, ALU.mult)
                        tt(s[:n, :, 0:64], x2, cos, ALU.mult)
                        tt(o[:n, :, 64:128], o[:n, :, 64:128], s[:n, :, 0:64], ALU.add)
                    cp(TM[:n, 20:24, :], AT[1][:n], E["rot_ready"])
                    bank = L0.take(dve)
                    cp(qT[0][:, :, :n], heads4(bank[:, :])[:, :, :n], L0.taken)
                    signal(E["qkT_dve"])
                    r = cst("ret_k")[:n, 4 * g:4 * g + 4]
                    half(t, 1, heads4(cst("ret_decay")[:n, :])[:, :, :n], cst("ret_q")[:n, :], r,
                         cst("ret_c")[:, 4 * g:4 * g + 4], 20, 24)
                    if t >= 1:
                        signal(E["state_done"])
                    head_norm(t, (12, 28), True)
                output_projection()

            def layer_c():
                norm()
                small_in[2].wait(dve, 96)
                g3 = gates(16)
                cp(beta3, g3[:, :, 0:8])
                x3 = g3[:, :, 8:16]
                tt(x3, x3, bc_mid(gb2, 3), ALU.add)
                ab = t24a.rearrange("p (t w) -> p t w", w=8)
                ts(ab, x3, -1.0)
                tt(ab, ab, x3, ALU.max, E["gate_exp_in"])
                ts(lg8, x3, 0.0, op0=ALU.max)
                E["gate_exp"].wait(dve)
                ts(beta, t24c, 1.0, op0=ALU.add)
                do(v.reciprocal(beta, beta))
                tt(lg, lg, t24b, ALU.add)
                ts(lg, lg, -1.0)
                tt(lg8, lg8, bc_mid(gb1, 3), ALU.mult, E["lf_ready"])
                bank = L0.take(dve)
                cp(bcum, bank[:, 0:24], L0.taken)
                ts(acol, bcum, -1.0)
                a3 = acol.rearrange("p (t w) -> p t w", w=8)
                for p in range(6):
                    E["conv_raw"].wait(dve)
                    c4 = zT[:, 4 * p:4 * p + 4, :]
                    cp(c4[:, :, COL[2] - PAD:COL[2]], cconv[:, 4 * p:4 * p + 4, 4:7])
                    cp(tails[:, 4 * p:4 * p + 4, 0:3], c4[:, :, COL[2] - 2 * PAD:COL[2] - PAD])
                    cp(tails[:, 4 * p:4 * p + 4, 3:6], c4[:, :, COLS - PAD:COLS])
                    if p >= 2:
                        E["conv_used"].wait(dve)
                    for k in range(4):
                        for j in range(4):
                            ch, o = 4 * p + j, convbuf[p % 2][:, j, :]
                            tap = cconv[:, ch, k:k + 1]
                            src = zT[:, ch, k:k + COLS - PAD]
                            if k == 0:
                                ins = v.tensor_scalar(o, src, tap, None, ALU.mult)
                            else:
                                ins = v.scalar_tensor_tensor(out=o, in0=src, scalar=tap, in1=o,
                                                             op0=ALU.mult, op1=ALU.add)
                            if j == 3:
                                do(ins)
                            else:
                                order["dve"].mark(ins)
                    signal(E["conv_done"])
                signal(E["tails_done"])
                E["conv_used"].wait(dve, 2)
                dve.wait_ge(out_written.sem, 16 * 9)
                do(v.memset(state1, 0.0))
                state_in.wait(dve, 16)
                for t in range(TILES):
                    n, g = N_TOK[t], t // 2
                    if t == 0:
                        E["z_ready"].wait(dve)
                    to_tokens(t, (0, 2, 4, 6))
                    for i in range(4):
                        qk = TM[:n, 4 * i:4 * i + 4, :]
                        tt(tmp[:n], qk, qk, ALU.mult)
                        red(hss[:n, 4 * i:4 * i + 4], tmp[:n])
                    signal(E["hss_ready"])
                    E["hrs_ready"].wait(dve)
                    ts(hrs[:n, 0:8], hrs[:n, 0:8], float(P) ** -0.5)
                    cp(gm[:n, :], b8[:n, t, :])
                    for i in range(4):
                        qk = TM[:n, 4 * i:4 * i + 4, :]
                        tt(qk, qk, bc_last(hrs[:n, 4 * i:4 * i + 4], P), ALU.mult)
                    signal(E["qkn_ready"])
                    for i in range(2):
                        bank = L0.take(dve)
                        cp((qT, kT)[i][0][:, :, :n], heads4(bank[:, :])[:, :, :n], L0.taken)
                    signal(E["qkT_dve"])
                    bank = L0.take(dve)
                    cp(gl, bank[:, 0:8], L0.taken)
                    cp(ein[:n, 0:8], gm[:n, :])
                    tt(ein[:n, 8:16], gl[:n, :], gm[:n, :], ALU.subtract)
                    cp(ein[:, 16:24], gl, E["ein_ready"])
                    for f in range(2):
                        diag(a3[:n, t, 4 * f:4 * f + 4], n)
                        bank = L0.take(dve)
                        tt(GAM[f][:n, :, :n], heads4(bank[:n, :])[:, :, :n], bc_mid(cst("negmask")[:n, :n], 4),
                           ALU.add, L0.taken)
                        signal(E["am_ready"])
                    E["eout_ready"].wait(dve)
                    for f in range(2):
                        E["p_ready"].wait(dve)
                        bank = L0.take(dve)
                        if f:
                            E["at_ready"].wait(dve)
                        tt(tmp[:n, :, :n], heads4(bank[:n, :])[:, :, :n], GAM[f][:n, :, :n], ALU.mult, L0.taken)
                        tt(tmp[:n, :, :n], tmp[:n, :, :n], bc_mid(cst("strict")[:n, :n], 4), ALU.mult)
                        tt(tmp[:n, :, :n], tmp[:n, :, :n], bc_last(beta3[:n, t, 4 * f:4 * f + 4], n), ALU.mult,
                           E["a_ready"])
                        tt(TI[f][:n, :, :n], tmp[:n, :, :n], bc_mid(merge[:n, 0, :n], 4), ALU.mult)
                        tt(TI[f][:n, :, :n], bc_mid(ident[:n, :n], 4), TI[f][:n, :, :n], ALU.subtract)
                    E["at_ready"].wait(dve)
                    for f in range(2):
                        tt(UI[f][:n, :, :n], AT[f][:n, :, :n], bc_mid(cst("merge1_t")[:n, :n], 4), ALU.mult)
                        tt(UI[f][:n, :, :n], bc_mid(ident[:n, :n], 4), UI[f][:n, :, :n], ALU.subtract,
                           E["tu_ready"])
                    levels = 6 if n == 128 else 4
                    for lv in range(levels):
                        for f in range(2):
                            bank = L0.take(dve)
                            tt(YI[f][:n, :, :n], heads4(bank[:n, :])[:, :, :n], bc_mid(merge[:n, lv + 1, :n], 4),
                               ALU.mult, L0.taken)
                            signal(E["yi_ready"])
                        for f in range(2):
                            for M in (TI[f], UI[f]):
                                bank = L0.take(dve)
                                tt(M[:n, :, :n], M[:n, :, :n], heads4(bank[:n, :])[:, :, :n], ALU.subtract,
                                   L0.taken)
                            signal(E["tu_ready"])
                    signal(E["state_ready"])
                    for f in range(2):
                        half(t, f, GAM[f][:n, :, :n], eout[:n, 4 * f:4 * f + 4], eout[:n, 8 + 4 * f:12 + 4 * f],
                             eout[:, 16 + 4 * f:20 + 4 * f], 8 + 4 * f, 16 + 4 * f, delta=True)
                    if t >= 1:
                        signal(E["state_done"])
                    head_norm(t, (24, 28), False)
                output_projection()

            def experts(l):
                dve.wait_ge(states_out, l + 1)
                norm()
                small_in[1 + 2 * l].wait(dve, 64)
                r = lambda o, w: route[:, o:o + w]
                t3 = lambda ap, w: ap.rearrange("p (t w) -> p t w", w=w)
                logit = t3(r(400, 108), 36)
                do(v.memset(r(400, 108), 0.0))
                bank = L0.take(dve)
                tt(logit[:, 0:2, :], t3(bank[:, 0:128], 64)[:, :, 0:36], bc_mid(rb, 2), ALU.add)
                tt(logit[:32, 2, :], bank[:32, 128:164], rb[:32, :], ALU.add, L0.taken)
                signal(small_used)
                grp, fine = logit[:, :, 0:4], logit[:, :, 4:36]
                gmax, gsum, psel = r(510, 3), r(513, 3), r(516, 3)
                eq = t3(r(520, 24), 8)
                idx = r(544, 3)
                ohg = t3(r(548, 12), 4)
                red(gmax, grp, ALU.max)
                tt(t3(r(300, 12), 4), grp, bc_last(gmax, 4), ALU.subtract, E["logits_exp_in"])
                E["logits_exp"].wait(dve)
                red(gsum, t3(r(300, 12), 4))
                do(v.reciprocal(psel, gsum))

                def first_max(vals, top, w, out):
                    e_ = eq[:, :, 0:w]
                    tt(e_, vals, bc_last(top, w), ALU.is_equal)
                    tt(e_, e_, bc_mid(cst("iota_m99")[:, 0:w], 3), ALU.mult)
                    red(idx, e_, ALU.min)
                    tt(out, bc_mid(cst("iota_m99")[:, 0:w], 3), bc_last(idx, w), ALU.is_equal)

                first_max(grp, gmax, 4, ohg)
                tt(ohg, ohg, bc_last(cst("valid"), 4), ALU.mult)
                fs, oh1, oh2 = t3(r(560, 24), 8), t3(r(584, 24), 8), t3(r(608, 24), 8)
                wide = r(900, 96)
                wide4 = wide.rearrange("p (t g j) -> p t g j", g=NGRP, j=EPG)
                for t in range(TILES):
                    tt(wide4[:, t], fine[:, t, :].rearrange("p (g j) -> p g j", j=EPG), bc_last(ohg[:, t, :], EPG),
                       ALU.mult)
                    red(fs[:, t, :], wide4[:, t].rearrange("p g j -> p j g"))
                max1, max2 = r(632, 3), r(636, 3)
                red(max1, fs, ALU.max)
                first_max(fs, max1, 8, oh1)
                do(v.scalar_tensor_tensor(out=r(640, 24), in0=r(584, 24), scalar=-BIG, in1=r(560, 24),
                                          op0=ALU.mult, op1=ALU.add))
                rest = t3(r(640, 24), 8)
                red(max2, rest, ALU.max)
                first_max(rest, max2, 8, oh2)
                tt(r(320, 3), max2, max1, ALU.subtract, E["logits_exp_in"])
                M = r(0, 96)
                Mk = [r(100, 96), r(200, 96)]
                for k, o in enumerate((oh1, oh2)):
                    m4 = Mk[k].rearrange("p (t g j) -> p t g j", g=NGRP, j=EPG)
                    for t in range(TILES):
                        tt(m4[:, t], bc_last(ohg[:, t, :], EPG), bc_mid(o[:, t, :], NGRP), ALU.mult)
                tt(M, Mk[0], Mk[1], ALU.add, E["choice_ready"])
                E["logits_exp"].wait(dve)
                s = r(664, 3)
                ts(s, r(320, 3), 1.0, op0=ALU.add)
                do(v.reciprocal(s, s))
                tt(pw[0][:, 0:3], psel, s, ALU.mult)
                tt(pw[0][:, 3:6], pw[0][:, 0:3], r(320, 3), ALU.mult)
                bank = L0.take(dve)
                cp(r(668, 1)[0:NEXP], bank[0:NEXP, 0:1], L0.taken)
                ts(r(670, 5)[0:NEXP], cst("thresh")[0:NEXP, :], r(668, 1)[0:NEXP], op0=ALU.is_lt)
                red(r(700, 1)[0:NEXP], r(670, 5)[0:NEXP])
                ts(route[0:NEXP, 704:832], ones[0:NEXP, :], r(700, 1)[0:NEXP])
                signal(E["nb_ready"])
                bank = L0.take(dve)
                cp(wide, bank[:, 0:96], L0.taken)
                bank = L0.take(dve)
                cp(r(680, 1)[0:NEXP], bank[0:NEXP, 0:1], L0.taken)
                bank = L0.take(dve)
                do(v.scalar_tensor_tensor(out=r(1000, 32), in0=bank[:, 0:32], scalar=float(BLK), in1=cst("slot_more"),
                                          op0=ALU.mult, op1=ALU.add), L0.taken)
                ts(route[0:NEXP, 832:832 + MAX_BLOCKS], cst("iota_list")[0:NEXP, :], r(680, 1)[0:NEXP],
                   op0=ALU.is_ge)
                cp(route[0:NEXP, 832 + MAX_BLOCKS - 1:832 + MAX_BLOCKS], r(700, 1)[0:NEXP], E["list_ready"])
                ts(r(1500, 96), wide, float(BLK), op0=ALU.is_ge)
                tt(t3(r(1500, 96), NEXP), t3(r(1500, 96), NEXP), bc_mid(r(1000, 32), 3), ALU.mult)
                tt(wide, wide, r(1500, 96), ALU.add)
                tt(t3(wide, NEXP), t3(wide, NEXP), bc_mid(cst("slot_first"), 3), ALU.add)
                for k in range(2):
                    tt(r(1100, 96), Mk[k], wide, ALU.mult)
                    red(dk[:, 3 * k:3 * k + 3], t3(r(1100, 96), NEXP))
                    cp(slots_i[:, k, :], dk[:, 3 * k:3 * k + 3])
                    tt(dk[:, 3 * k:3 * k + 3], dk[:, 3 * k:3 * k + 3], cst("invalid"), ALU.add)
                bank = L0.take(dve)
                last_ = MAX_BLOCKS - 1
                ts(r(1200, MAX_BLOCKS)[0:1], bank[0:1, 0:MAX_BLOCKS], float(NEXP - 1), op0=ALU.min)
                tt(r(1200, MAX_BLOCKS)[0:1], r(1200, MAX_BLOCKS)[0:1], cst("list_first")[0:1], ALU.add)
                ts(r(1300, 1)[0:1], bank[0:1, last_:last_ + 1], float(NEXP), op0=ALU.add, event=L0.taken)
                cp(blocks_i[:, 0:last_], r(1200, last_)[0:1])
                cp(blocks_i[:, last_:last_ + 1], r(1300, 1)[0:1], E["blocks_ready"])
                m = moe[l]
                nb = nblk_reg(dve)
                dve.sem_inc(m["y"][1], 1)
                iota = bc_mid(cst("iota_pair"), 3)

                def onehot(count):
                    for k in range(2):
                        v.tensor_tensor(oh[k], iota, bc_last(dk[:, 3 * k:3 * k + 3], 2 * BLK),
                                        ALU.is_equal).then_inc(m["step"], 1)
                    dve.wait_ge(m["step"], 3 * count + 2)
                    v.tensor_scalar(dk, dk, -2.0 * BLK, None, ALU.add).then_inc(m["step"], 1)
                    v.tensor_tensor(oh[0], oh[0], oh[1], ALU.add).then_inc(m["onehot"], 1)
                    dve.wait_ge(m["step"], 3 * count + 3)

                def fetched(count):
                    dve.wait_ge(m["gathered"], count)
                    v.tensor_copy(xg[:, 0:4].rearrange("p k u s -> p (k u s)"), banks[0][:, :]
                                  ).then_inc(m["xg_dve"], 1)

                def hidden(u, i):
                    dve.wait_ge(m["silu"], i + 1)
                    dve.wait_ge(m["up_used"], i + 3)
                    v.tensor_tensor(hid[u], sg[u], banks[2 + u][BLK:2 * BLK, :], ALU.mult).then_inc(m["hidden"], 1)

                def hidden_T(u, i):
                    dve.wait_ge(m["flipped"], i + 1)
                    v.tensor_copy(hidT[u], banks[4 + u][:, 0:256]).then_inc(m["hiddenT"], 1)

                onehot(0)
                fetched(1)
                with dve.Fori(0, nb) as b:
                    onehot(b + 1)
                    hidden(0, 2 * b)
                    hidden_T(0, 2 * b)
                    hidden(1, 2 * b + 1)
                    fetched(b + 2)
                    hidden_T(1, 2 * b + 1)
                    dve.wait_ge(m["down_used"], 2 * b + 4)
                    dve.wait_ge(m["stored"][1], 32 * b)
                    v.tensor_copy(ys[1], banks[7][:, :]).then_inc(m["y"][1], 1)
                for t in range(TILES):
                    n = N_TOK[t]
                    dve.wait_ge(m["yg_in"][t % 2], 32 * (t // 2 + 1))
                    for k in range(2):
                        ins = v.scalar_tensor_tensor(out=X[:n, t, :], in0=yg[:n, t % 2, k, :],
                                                     scalar=pw[0][:n, 3 * k + t:3 * k + t + 1], in1=X[:n, t, :],
                                                     op0=ALU.mult, op1=ALU.add)
                        do(ins)
                    signal(x_ready)
                    dve.nop().then_inc(m["yg_used"], 1)

            do(v.memset(TM[:, 0:8, :], 0.0), E["zero_rows"])
            const_in.wait(dve, 16)
            for t in range(TILES):
                x_in[t].wait(dve, 16)
                signal(x_ready)
            do(v.memset(HT[:, :, 0:PAD], 0.0))
            do(v.memset(HT[:, :, COL[2] - PAD:COL[2]], 0.0))
            layer_ab()
            experts(0)
            layer_c()
            experts(1)
            norm(last=True)

        @block.sync
        def _(sp):
            def dma(dst, src, event):
                event.mark(sp.dma_start(dst, src), 16)

            def row(src):
                return src.partition_broadcast(P)

            dma(gain[:], row(a["norm_mix"][0]), gain0_in)
            for t in range(TILES):
                src = a["x_prompt"][0, 128 * t:128 * t + 128, :] if t < 2 else a["x_sample"][0]
                dma(X[:N_TOK[t], t, :], src, x_in[t])
            dma(const[:], a["const"], const_in)
            dma(small_w[:, :, 0:8], a["ab_w_in"][0][:, 2048:2056].rearrange("(k p) n -> p k n", p=P), small_in[0])
            dma(gb1, row(a["ab_gate_bias"][0]), small_in[0])
            dma(hgain[:, 0, :], row(a["ab_norm_a"][0]), small_in[0])
            dma(hgain[:, 1, :], row(a["ab_norm_b"][0]), small_in[0])

            def pieces(w_in, w_out, cols, layer):
                for p in range(10):
                    if layer or p >= 4:
                        sp.wait_ge(*piece_done[10 * layer + p - 4])
                    src = w_in[:, cols[p]:cols[p] + 512] if p < 8 else w_out[:, 512 * (p - 8):512 * (p - 7)]
                    dma(W[:, p % 4, :].rearrange("p (k n) -> p k n", k=KT),
                        src.rearrange("(k p) n -> p k n", p=P), piece_in[p % 4])

            LOADS = {0: ("moe_w_gate", "gate_used", 8), 1: ("moe_w_up", "up_used", 8), 2: ("moe_w_down", "down_used", 4)}

            def expert_piece(l, u, s, e):
                name, _, kk = LOADS[s]
                sp.dma_start(W[:, 3 * u + s, :].rearrange("p (k n) -> p k n", k=kk),
                             a[name][l, bass.ds(e, 1), :, :].rearrange("o (k p) n -> p (o k) n", p=P)
                             ).then_inc(moe[l]["w_in"][3 * u + s], 16)

            def experts(l):
                m = moe[l]
                for u, s, free in ((0, 2, piece_done[10 * l + 6]), (1, 0, piece_done[10 * l + 7]),
                                   (1, 1, scratch_free[l]), (1, 2, scratch_free[l]),
                                   (0, 0, piece_done[10 * l + 8]), (0, 1, piece_done[10 * l + 9])):
                    sp.wait_ge(*free)
                    expert_piece(l, u, s, u)
                E["blocks_ready"].wait(sp)
                nb = nblk_reg(sp)
                with sp.Fori(1, nb) as b:
                    e = [sp.value_load(blocks_i[0:1, bass.ds(2 * b + u, 1)], min_val=0, max_val=NEXP - 1)
                         for u in range(2)]
                    for u, s in ((0, 0), (0, 1), (1, 0), (1, 1), (0, 2), (1, 2)):
                        sp.wait_ge(m[LOADS[s][1]], 2 * b + u + 1)
                        expert_piece(l, u, s, e[u])
                return nb

            pieces(a["ab_w_in"][0], a["ab_w_out"][0],
                   [512 * i for i in range(4)] + [2056 + 512 * i for i in range(4)], 0)
            nb = experts(0)
            sp.wait_ge(moe[0]["down_used"], 2 * nb + 2)
            pieces(a["c_w_in"][0], a["c_w_out"][0],
                   [512 * i for i in range(6)] + [3088, 3600], 1)
            experts(1)
            for t in range(TILES):
                E["hn_out"].wait(sp)
                dst = a["y_prompt"][0, 128 * t:128 * t + 128, :] if t < 2 else a["y_sample"][0]
                dma(dst, HN[:N_TOK[t], t, :], y_written)
            sp.wait_ge(y_written.sem, 16 * 3)

        @block.gpsimd
        def _(pool):
            do = InOrder(pool, order["pool"])

            def load(dst, src, event):
                event.mark(pool.dma_start(dst, src), 16)

            def store(dst, src):
                out_written.made += 16
                pool.dma_start(dst, src).then_inc(out_written.sem, 16)

            def power(dst, src, scale, n, w, ready, done):
                ready.wait(pool)
                do(nc.gpsimd.tensor_scalar(src, src, scale, EPS, ALU.mult, ALU.add))
                do(nc.gpsimd.tensor_tensor(dst, src, cst("half_neg")[:n, 0:w], ALU.pow), done)

            def norm(k):
                for t in range(TILES):
                    n = N_TOK[t]
                    power(rstd[:n, t:t + 1], sumsq[:n, t:t + 1], 1.0 / D, n, 1, ss_ready, rs_ready)
                if k < 4:
                    gain_used.wait(pool)
                    g = (a["norm_mix"], a["norm_ffn"])[(k + 1) % 2][(k + 1) // 2] if k < 3 else a["norm_final"]
                    load(gain[:], g.partition_broadcast(P), gain_in)

            load(mprev[1], a["state_mlstm_m"][0, 0].partition_broadcast(P), state_in)
            load(nstate[1], a["state_n_t"], state_in)
            load(state2[:, 0:4, :], a["state_mlstm_c"][0, 0].rearrange("h k v -> k h v"), state_in)
            load(state2[:, 4:8, :], a["state_ret"][0, 0].rearrange("h k v -> k h v"), state_in)
            norm(0)
            E["zero_rows"].wait(pool)
            load(a["block_rows"][NEXP * BLK:MAX_BLOCKS * BLK, :].rearrange("(r p) n -> p r n", p=P),
                 TM[:, 0:8, :].rearrange("p c n -> p (c n)").unsqueeze(1).to_broadcast([P, (MAX_BLOCKS - NEXP) * BLK // P, D]), E["rows_clear"])
            for t in range(TILES):
                n = N_TOK[t]
                power(hrs[:n, 0:8], hss[:n, 0:8], 1.0 / P, n, 8, E["hss_ready"], E["hrs_ready"])
                if t >= 1:
                    E["state_done"].wait(pool)
                    g = t - 1
                    store(a["out_c"][g].rearrange("h k v -> k h v"), states[t][:, 0:4, :])
                    store(a["out_ret"][g].rearrange("h k v -> k h v"), states[t][:, 4:8, :])
                    store(a["out_n"][g], nstate[g])
                    store(a["out_m"][g], mprev[g][0:1, :])
            pool.wait_ge(out_written.sem, 16 * 8)
            nc.gpsimd.sem_inc(states_out, 1)
            small_used.wait(pool)
            for l in range(2):
                load(small_w[:, :, 0:4], a["moe_w_grp"][l].rearrange("(k p) n -> p k n", p=P), small_in[1 + 2 * l])
                load(small_w[:, :, 4:36], a["moe_w_exp"][l].rearrange("(k p) n -> p k n", p=P), small_in[1 + 2 * l])
                load(rb[:, 0:4], a["moe_b_grp"][l].partition_broadcast(P), small_in[1 + 2 * l])
                load(rb[:, 4:36], a["moe_b_exp"][l].partition_broadcast(P), small_in[1 + 2 * l])
                norm(2 * l + 1)
                if l == 0:
                    load(state2[:, :, :], a["state_gdn"][0, 0].rearrange("h k v -> k h v"), state_in)
                    load(gb1, a["c_a_log"][0].partition_broadcast(P), small_in[2])
                    load(gb2, a["c_dt_bias"][0].partition_broadcast(P), small_in[2])
                    load(hgain[:, 0, :], a["c_norm"][0].partition_broadcast(P), small_in[2])
                    small_used.wait(pool)
                    load(small_w[:, :, 0:16], a["c_w_in"][0][:, 3072:3088].rearrange("(k p) n -> p k n", p=P),
                         small_in[2])
                m = moe[l]
                E["blocks_ready"].wait(pool)
                nb = nblk_reg(pool)
                for u in range(2):
                    pool.wait_ge(m["stored"][u], 32 * nb)
                do(pool.nop())
                for t in range(TILES):
                    n = N_TOK[t]
                    if t == 2:
                        pool.wait_ge(m["yg_used"], 1)
                    for k in range(2):
                        pool.indirect_dma_start(
                            yg[:n, t % 2, k, :], None, a["block_rows"],
                            bass.IndirectOffsetOnAxis(ap=slots_i[:n, k, t:t + 1], axis=0)
                        ).then_inc(m["yg_in"][t % 2], 16)
                if l == 0:
                    load(cconv[:, :, 0:4], a["conv_taps"], small_in[2])
                    load(cconv[:, :, 4:7], a["conv_state"], small_in[2])
                    norm(2)
                    E["tails_done"].wait(pool)
                    store(a["out_tails"], tails)
                    for t in range(TILES):
                        n = N_TOK[t]
                        power(hrs[:n, 0:16], hss[:n, 0:16], 1.0, n, 16, E["hss_ready"], E["hrs_ready"])
                        power(hrs[:n, 0:8], hss[:n, 0:8], 1.0 / P, n, 8, E["hss_ready"], E["hrs_ready"])
                        if t >= 1:
                            E["state_done"].wait(pool)
                            store(a["out_gdn"][t - 1].rearrange("h k v -> k h v"), states[t])
                    pool.wait_ge(out_written.sem, 16 * 11)
                    nc.gpsimd.sem_inc(states_out, 1)
                    small_used.wait(pool)
            norm(4)


_OUTS = {"y_prompt": (1, 256, 1024), "y_sample": (1, 32, 1024), "out_c": (2, 4, 128, 128), "out_n": (2, 128, 4),
         "out_m": (2, 1, 4), "out_ret": (2, 4, 128, 128), "out_gdn": (2, 8, 128, 128), "out_tails": (128, 24, 6)}
_IN = ["x_prompt", "x_sample", "state_mlstm_c", "state_mlstm_m", "state_ret", "state_gdn", "norm_mix", "norm_ffn",
       "norm_final", "ab_w_in", "ab_gate_bias", "ab_w_out", "ab_norm_a", "ab_norm_b", "c_w_in", "c_a_log",
       "c_dt_bias", "c_norm", "c_w_out", "moe_w_grp", "moe_b_grp", "moe_w_exp", "moe_b_exp", "moe_w_gate",
       "moe_w_up", "moe_w_down"]


def constants():
    import numpy as np

    f = np.float32
    i = np.arange(P)
    row, col = i[:, None], i[None, :]
    c = {
        "ident": row == col, "tri_incl": row <= col, "tri_strict": row < col, "ones": np.ones((P, P)),
        "negmask": np.where(col <= row, 0.0, -BIG), "strict": col < row,
        "merge": np.concatenate([(row // (2 * s) == col // (2 * s)) & (row // s % 2 == 1) & (col // s % 2 == 0)
                                 for s in (1, 2, 4, 8, 16, 32, 64)], 1),
        "merge1_t": (row // 2 == col // 2) & (row % 2 == 0) & (col % 2 == 1),
        "iota_pair": np.tile(np.arange(2 * BLK), (P, 1)), "iota_m99": np.tile(np.arange(8) - 99, (P, 1)),
        "valid": np.stack([i >= 0, i >= 0, i < N_TOK[2]], 1),
        "invalid": np.stack([i * 0, i * 0, np.where(i < N_TOK[2], 0, 1e6)], 1),
        "thresh": np.tile(BLK * np.arange(1, 6), (P, 1)), "iota_list": np.tile(np.arange(MAX_BLOCKS) - NEXP, (P, 1)),
        "list_first": np.tile(np.where(np.arange(MAX_BLOCKS) < NEXP, np.arange(MAX_BLOCKS), 0), (P, 1)),
        "slot_first": np.tile(BLK * np.arange(NEXP), (P, 1)),
        "slot_more": np.tile(BLK * (NEXP - 1 - np.arange(NEXP)), (P, 1)),
        "half_neg": np.full((P, 16), -0.5),
    }
    lg = np.log(f(1.0) - f(2.0) ** (f(-5.0) - np.arange(4, dtype=f))).astype(f)
    rel = (row - col).astype(f)
    c["ret_decay"] = np.concatenate([np.where(rel >= 0, np.exp(np.where(rel >= 0, rel, f(0)) * g), 0) for g in lg], 1)
    c["ret_q"] = np.exp((i[:, None] + 1).astype(f) * lg)
    c["ret_k"] = np.concatenate([np.exp(np.minimum(n - 1 - i, P)[:, None].astype(f) * lg) for n in (128, 32)], 1)
    c["ret_c"] = np.concatenate([np.tile(np.exp(f(n) * lg), (P, 1)) for n in (128, 32)], 1)
    inv = f(10000.0) ** (-np.arange(64, dtype=f) / f(64))
    cos, sin = [], []
    for t in range(TILES):
        pos = (128 * t + i).astype(f)
        ang = (pos[:, None] * inv[None, :]).astype(f)
        for scale in (f(1.0), f(P) ** f(-0.5)):
            cos.append(np.cos(ang) * scale)
            sin.append(np.sin(ang) * scale)
    c["rot_cos"], c["rot_sin"] = np.concatenate(cos, 1), np.concatenate(sin, 1)
    return np.concatenate([np.asarray(c[n], f).reshape(P, w) for n, w in _SIZES], 1)


def kernel(**inputs):
    import numpy as np
    import concourse.bacc as bacc
    from concourse.bass_utils import run_bass_kernel_spmd

    nc = bacc.Bacc("TRN2", target_bir_lowering=False, num_devices=1)
    x = {k: np.ascontiguousarray(inputs[k]) for k in _IN}
    x["const"] = constants()
    x["conv_taps"] = np.ascontiguousarray(np.asarray(inputs["c_conv_w"])[0].reshape(4, 24, P).transpose(2, 1, 0))
    x["conv_state"] = np.ascontiguousarray(
        np.asarray(inputs["state_gdn_conv"])[0, 0].reshape(3, 24, P).transpose(2, 1, 0))
    x["state_n_t"] = np.ascontiguousarray(np.asarray(inputs["state_mlstm_n"])[0, 0].T)
    arrays = {f"in_{k}": v for k, v in x.items()}
    a = {k: nc.dram_tensor(f"in_{k}", v.shape, F32, kind="ExternalInput").ap() for k, v in x.items()}
    for k, s in _OUTS.items():
        a[k] = nc.dram_tensor(k, s, F32, kind="ExternalOutput").ap()
    a["block_rows"] = nc.dram_tensor("block_rows", (MAX_BLOCKS * BLK, D), F32, kind="Internal").ap()
    trunk(nc, a)
    r = run_bass_kernel_spmd(nc, [arrays], core_ids=[0]).results[0]
    tails = r["out_tails"].transpose(2, 1, 0).reshape(2, 1, 1, 3, 3072)
    c, n, m = r["out_c"], r["out_n"].transpose(0, 2, 1), r["out_m"]
    sides = [(c[g][None, None], n[g][None, None], m[g][None], r["out_ret"][g][None, None],
              r["out_gdn"][g][None, None], tails[g]) for g in range(2)]
    return (r["y_prompt"], r["y_sample"], *sides[0], *sides[1])
```

```python
from contextlib import ExitStack

import concourse.bass as bass
from concourse import mybir

F32 = mybir.dt.float32
I32 = mybir.dt.int32
ALU = mybir.AluOpType
ACT = mybir.ActivationFunctionType
X_AXIS = mybir.AxisListType.X

P = 128
D = 1024
KT = D // P
N_TOK = [128, 128, 32]
TILES = 3
N_ALL = sum(N_TOK)
PAD = 3
COL = [PAD, PAD + 128, 2 * PAD + 256]
COLS = 2 * PAD + 256 + 32
HEADS = 8
NEXP, NGRP, EPG, F = 32, 4, 8, 512
BLK = 64
MAX_BLOCKS = 44
EPS = 1e-6
BIG = 1e30

_SIZES = [("ident", 128), ("tri_incl", 128), ("ones", 128), ("half_neg", 16), ("tri_strict", 128), ("negmask", 128),
          ("merge", 7 * 128), ("merge1_t", 128),
          ("ret_decay", 512), ("rot_cos", 3 * 128), ("rot_sin", 3 * 128), ("ret_q", 4), ("ret_k", 8),
          ("ret_c", 8), ("iota_pair", 2 * BLK), ("iota_m99", 8), ("valid", 3), ("invalid", 3),
          ("thresh", 5), ("iota_list", MAX_BLOCKS), ("list_first", MAX_BLOCKS), ("slot_first", NEXP), ("slot_more", NEXP),
          ("slot", 1)]
CONST = {}
_at = 0
for _n, _w in _SIZES:
    CONST[_n] = (_at, _w)
    _at += _w
CONST_COLS = _at
CONST_HEAD = CONST["tri_strict"][0]


BESIDE = [[range(16, 17), range(17, 18), range(18, 19), range(19, 22)],
          [range(22, 23), range(23, 24), range(0), range(24, 26)],
          [range(26, 27), range(0), range(0), range(27, 28)]]

SCATTERS = 5


class Event:

    def __init__(self, sem):
        self.sem, self.made, self.seen = sem, 0, {}

    def mark(self, ins, by=1):
        self.made += by
        ins.then_inc(self.sem, by)

    def wait(self, eng, by=1):
        key = id(eng)
        self.seen[key] = self.seen.get(key, 0) + by
        eng.wait_ge(self.sem, self.seen[key])


class InOrder:

    def __init__(self, eng, event):
        self.eng, self.event = eng, event

    def __call__(self, ins, event=None):
        ev = event or self.event
        ev.mark(ins)
        self.eng.wait_ge(ev.sem, ev.made)


class Lane:

    def __init__(self, full, taken, banks):
        self.full, self.taken, self.banks = full, taken, banks
        self.filled = self.opened = 0

    def open(self, pe):
        if self.filled >= 2:
            pe.wait_ge(self.taken.sem, self.filled - 1)
        return self.banks[self.filled % 2]

    def close(self, ins):
        self.filled += 1
        self.full.mark(ins)

    def take(self, eng):
        self.full.wait(eng)
        self.opened += 1
        return self.banks[(self.opened - 1) % 2]


def trunk(nc, a):
    with ExitStack() as ctx:
        def sb(name, shape, dt=F32):
            return ctx.enter_context(nc.sbuf_tensor(name, shape, dt))

        def sem(name):
            return ctx.enter_context(nc.semaphore(name))

        def ev(name):
            return Event(sem(name))

        W = sb("W", [P, 6, 4096])
        const = sb("const", [P, CONST_COLS])
        zT = sb("zT", [P, 32, COLS])
        TM = sb("TM", [P, 32, P])
        X = sb("X", [P, TILES, D])
        HN = sb("HN", [P, TILES, D])
        HT = sb("HT", [P, KT, COLS])
        gain = sb("gain", [P, D])
        state2 = sb("state2", [P, HEADS, P])
        sm = sb("sm", [P, 436])
        small_w = sb("small_w", [P, KT, 36])
        hgain = sb("hgain", [P, 2, P])
        blocks_i = sb("blocks_i", [1, MAX_BLOCKS], I32)
        banks = [ctx.enter_context(nc.psum_tensor(f"bank{i}", [P, 512], F32)) for i in range(8)]

        def cst(name):
            o, w = CONST[name]
            return const[:, o:o + w]

        ident, ones, tri_incl, tri_strict = cst("ident"), cst("ones"), cst("tri_incl"), cst("tri_strict")
        ws = W[:, 4:6, :].rearrange("p s n -> p (s n)")
        hs = HN[:].rearrange("p t n -> p (t n)")
        zf = zT[:].rearrange("p c n -> p (c n)")

        def heads4(ap):
            return ap.rearrange("p (h n) -> p h n", n=P)

        qT = [heads4(ws[:, 512 * i:512 * i + 512]) for i in range(2)]
        kT = [heads4(ws[:, 1024 + 512 * i:1536 + 512 * i]) for i in range(2)]
        AT, TI, UI, YI = [[heads4(ws[:, 2048 + 1024 * j + 512 * i:2560 + 1024 * j + 512 * i])
                           for i in range(2)] for j in range(4)]
        GAM = [heads4(ws[:, 6144 + 512 * i:6656 + 512 * i]) for i in range(2)]
        Yout = ws[:, 7168:8192].rearrange("p (h n) -> p h n", n=P)
        state1 = hs[:, 0:1024].rearrange("p (h n) -> p h n", n=P)
        Sm, ST, kw, tmp = [heads4(hs[:, 1024 + 512 * i:1536 + 512 * i]) for i in range(4)]
        states = [state1, state1, state2[:, :, :]]
        xg = zf[:, 0:1024].rearrange("p (k u s) -> p k u s", u=2, s=BLK)
        sg = [zf[0:BLK, 1024 + F * u:1024 + F * (u + 1)] for u in range(2)]
        hid = [zf[0:BLK, 2048 + F * u:2048 + F * (u + 1)] for u in range(2)]
        hidT = [zf[:, 3072 + 256 * u:3328 + 256 * u] for u in range(2)]
        ys = [zf[:, 3584 + 512 * h:4096 + 512 * h] for h in range(2)]
        oh = [zf[:, 4608 + 384 * k:4992 + 384 * k].rearrange("p (t s) -> p t s", s=2 * BLK) for k in range(2)]
        route = zf[:, 5400:7600]
        rows = zf[:, 7600:7600 + 4 * N_ALL].rearrange("p (j n) -> p j n", n=N_ALL)
        share = [zf[:, 7600 + (4 + k) * N_ALL:7600 + (5 + k) * N_ALL] for k in range(2)]
        small_T = zT[:, 31, :]
        junk = zf[:, 8384:9408]
        convbuf = [ws[:, 1200 * i:1200 * i + 4 * (COLS - PAD)].rearrange("p (c n) -> p c n", c=4) for i in range(2)]
        cconv = ws[:, 6656:6824].rearrange("p (c n) -> p c n", n=7)
        tails = ws[:, 6848:6992].rearrange("p (c n) -> p c n", n=6)
        rotc = cst("rot_cos").rearrange("p (t j n) -> p t j n", t=3, j=2)
        rots = cst("rot_sin").rearrange("p (t j n) -> p t j n", t=3, j=2)
        merge = cst("merge").rearrange("p (l n) -> p l n", n=P)

        _sm = [0]

        def small(w):
            _sm[0] += w
            return sm[:, _sm[0] - w:_sm[0]]

        sumsq, rstd = small(3), small(3)
        g16 = small(48)
        gb1, gb2 = small(8), small(8)
        lg = small(24)
        bcum = small(24)
        acol = small(24)
        t24a, t24b, t24c = small(24), small(24), small(24)
        beta = small(24)
        mprev = [small(4), small(4)]
        nstate = [small(4), small(4)]
        gm = small(8)
        gl = small(8)
        negg = small(4)
        ein, eout = small(32), small(32)
        den, den2 = small(4), small(4)
        hss, hrs = small(16), small(16)
        m1 = small(4)
        pw = [small(6)]
        dk = small(6)
        rb = small(36)
        slot_at = small(1)

        order = {e: ev(f"{e}_order") for e in ("dve", "act", "pool")}
        background = Lane(ev("background_full"), ev("background_taken"), banks[4:6])
        lanes = [Lane(ev("lane_dve_full"), ev("lane_dve_taken"), banks[0:2]),
                 Lane(ev("lane_act_full"), ev("lane_act_taken"), banks[2:4])]
        L0, L1 = lanes
        const_head_in, const_in, x_in = ev("const_head_in"), ev("const_in"), [ev(f"x_in{i}") for i in range(3)]
        gain0_in, gain_in, gain_used = ev("gain0_in"), ev("gain_in"), ev("gain_used")
        piece_in = [ev(f"piece_in{i}") for i in range(4)]
        scratch_free = []
        piece_done = []
        small_in = [ev(f"small_in{i}") for i in range(4)]
        small_used, hgain_in = ev("small_used"), ev("hgain_in")
        x_ready, ss_ready, rs_ready, hn_ready = ev("x_ready"), ev("ss_ready"), ev("rs_ready"), ev("hn_ready")
        ht_dve, ht_act = ev("ht_dve"), ev("ht_act")
        names = ["z_ready", "tm_dve", "tm_act", "gate_exp_in", "gate_exp", "lf_ready", "diag_ready", "gm_ready",
                 "ein_ready", "eout_ready", "rot_ready", "qkT_dve", "qkT_act", "s_ready", "st_ready", "kw_ready",
                 "state_ready", "r_ready", "vn_ready", "p_ready", "a_ready", "at_ready", "tu_ready",
                 "yi_ready", "hss_dve", "hrs_ready", "y_ready", "yT_act", "tile_done",
                 "conv_raw", "conv_done", "logits_exp_in", "logits_exp", "choice_ready", "nb_ready",
                 "list_ready", "blocks_ready", "qkn_ready", "state_done", "tails_done",
                 "hn_out", "conv_used", "out_ready", "small_ready", "rows_diag", "rows_wide",
                 "hss_act", "y_done", "gates_ready", "out_taken"]
        E = {n: ev(n) for n in names}
        state_in = ev("state_in")
        out_written, y_written = ev("out_written"), ev("y_written")
        moe = [dict(
            w_in=[sem(f"moe{l}_w_in{s}") for s in range(6)],
            gate_used=sem(f"moe{l}_gate_used"), up_used=sem(f"moe{l}_up_used"), down_used=sem(f"moe{l}_down_used"),
            onehot=sem(f"moe{l}_onehot"), gathered=sem(f"moe{l}_gathered"),
            xg_dve=sem(f"moe{l}_xg_dve"), xg_act=sem(f"moe{l}_xg_act"),
            silu=sem(f"moe{l}_silu"), hidden=sem(f"moe{l}_hidden"), flipped=sem(f"moe{l}_flipped"),
            hiddenT=sem(f"moe{l}_hiddenT"), half_down=sem(f"moe{l}_half_down"),
            y=[sem(f"moe{l}_y{h}") for h in range(2)],
            step=sem(f"moe{l}_step"), share_step=sem(f"moe{l}_share_step"), share=sem(f"moe{l}_share"),
            quarter=sem(f"moe{l}_quarter"), scattered=sem(f"moe{l}_scattered"), added=sem(f"moe{l}_added"),
        ) for l in range(2)]

        states_out = sem("states_out")

        block = ctx.enter_context(nc.Block())

        def nblk_reg(eng):
            count = eng.value_load(blocks_i[0:1, MAX_BLOCKS - 1:MAX_BLOCKS], min_val=NEXP, max_val=MAX_BLOCKS - 2)
            return eng.snap((count + 1) // 2)

        @block.tensor
        def _(pe):
            def mm(out, lhsT, rhs, start=True, stop=True):
                return nc.tensor.matmul(out, lhsT, rhs, start=start, stop=stop)

            def flip(out, src, n):
                return nc.tensor.transpose(out, src, ident[:n, :n])

            def transpose_tile(src, t, n):
                for g in range(2):
                    bank = lanes[g].open(pe)
                    for j in range(4):
                        last = flip(bank[:, j * P:j * P + n], src(4 * g + j)[:n], n)
                    lanes[g].close(last)

            def norm():
                for t in range(TILES):
                    hn_ready.wait(pe)
                    transpose_tile(lambda c: HN[:, t, c * P:c * P + P], t, N_TOK[t])
                ht_dve.wait(pe, 3)
                ht_act.wait(pe, 3)

            def small_projection(w, which, loads, beside=range(0)):
                small_in[which].wait(pe, 16 * loads)
                bank = L0.open(pe)
                for k in range(KT):
                    last = mm(bank[:w, 0:COLS], small_w[:, k, 0:w], HT[:, k, :], k == 0, k == KT - 1)
                L0.close(last)
                for c in beside:
                    project(c, L1)
                E["small_ready"].wait(pe)
                bank = L0.open(pe)
                for t in range(TILES):
                    n, c = N_TOK[t], COL[t]
                    last = flip(bank[:n, 64 * t:64 * t + w], small_T[:w, c:c + n], w)
                L0.close(last)

            def project(c, lane):
                p = c // 4
                if c % 4 == 0:
                    piece_in[p % 4].wait(pe, 16)
                w = W[:, p % 4, :].rearrange("p (k n) -> p k n", k=KT)
                bank = lane.open(pe)
                for k in range(KT):
                    last = mm(bank[:, 0:COLS], w[:, k, c % 4 * P:c % 4 * P + P], HT[:, k, :], k == 0, k == KT - 1)
                lane.close(last)
                if c % 4 == 3:
                    piece_done.append((lane.full.sem, lane.full.made))

            def project_gates(t, p, steps, bank):
                if t == 0 and steps[0] == 0:
                    piece_in[p % 4].wait(pe, 16)
                if steps[0] == 0:
                    bank = background.open(pe)
                n, c = N_TOK[t], COL[t]
                w = W[:, p % 4, :].rearrange("p (k n) -> p k n", k=KT)
                for k in steps:
                    if t < 2:
                        last = mm(bank[:n, :], HT[:, k, c:c + n], w[:, k, :], k == 0, k == KT - 1)
                    else:
                        for q in range(4):
                            last = mm(bank[32 * q:32 * q + n, 0:P], HT[:, k, c:c + n], w[:, k, P * q:P * q + P],
                                      k == 0, k == KT - 1)
                if steps[-1] == KT - 1:
                    background.close(last)
                    if t == 2:
                        piece_done.append((background.full.sem, background.full.made))
                return bank

            def y_transposed():
                E["yT_act"].wait(pe, 2)

            def output_part(t, k):
                if k == 0:
                    y_transposed()
                    if t == 0:
                        for p in range(2):
                            piece_in[p].wait(pe, 16)
                    else:
                        E["out_taken"].wait(pe)
                n, c = N_TOK[t], COL[t]
                for p in range(2):
                    w = W[:, p, :].rearrange("p (k n) -> p k n", k=KT)
                    last = mm(banks[6 + p][:n, :], zT[:, k, c:c + n], w[:, k, :], k == 0, k == KT - 1)
                if k == KT - 1:
                    E["out_ready"].mark(last)

            def output_sample():
                y_transposed()
                n, c = N_TOK[2], COL[2]
                bank = L0.open(pe)
                for k in range(KT):
                    for q in range(4):
                        w = W[:, q // 2, :].rearrange("p (k n) -> p k n", k=KT)
                        last = mm(bank[32 * q:32 * q + n, 0:256], zT[:, k, c:c + n],
                                  w[:, k, 256 * (q % 2):256 * (q % 2) + 256], k == 0, k == KT - 1)
                L0.close(last)
                for p in range(2):
                    piece_done.append((L0.full.sem, L0.full.made))

            def to_tokens(t, groups):
                n, c = N_TOK[t], COL[t]
                for g in groups:
                    lane = lanes[g % 2]
                    bank = lane.open(pe)
                    for j in range(4):
                        last = flip(bank[:n, j * P:j * P + P], zT[:, 4 * g + j, c:c + n], P)
                    lane.close(last)
                E["tm_dve"].wait(pe)
                E["tm_act"].wait(pe)

            def row_broadcast(n, lane=L0, masked=False, src=tmp):
                E["diag_ready"].wait(pe)
                bank = lane.open(pe)
                last = mm(heads4(bank[:n, :])[:, :, :n], ones[:n, :n], src[:n, :, :n], True, not masked)
                if masked:
                    negmask4 = cst("negmask")[:n, :n].unsqueeze(1).to_broadcast([n, 4, n])
                    last = mm(heads4(bank[:n, :])[:, :, :n], ident[:n, :n], negmask4, False, True)
                lane.close(last)

            def last_row(t, w):
                n = N_TOK[t]
                sel = ident[:n, n - 1:n].to_broadcast([n, P])
                bank = L0.open(pe)
                L0.close(mm(bank[:, 0:w], sel, gm[:n, 0:w]))

            def half(t, f, q, k, vchunk, mlstm=False, delta=False, beside=range(0)):
                n = N_TOK[t]
                st = states[t]
                bank = L0.open(pe)
                for h in range(4):
                    last = mm(bank[:n, h * P:h * P + n], q(h), k(h))
                L0.close(last)
                if delta:
                    bank = L0.open(pe)
                    for h in range(4):
                        last = mm(bank[:n, h * P:h * P + P], k(h), st[:, 4 * f + h, :])
                    L0.close(last)
                for c in beside:
                    project(c, background)
                E["s_ready"].wait(pe)
                bank = L1.open(pe)
                for h in range(4):
                    last = flip(bank[:n, h * P:h * P + n], Sm[:n, h, :n], n)
                L1.close(last)
                bank = L0.open(pe)
                for h in range(4):
                    last = mm(bank[:n, h * P:h * P + P], q(h), st[:, 4 * f + h, :])
                L0.close(last)
                if mlstm:
                    bank = L0.open(pe)
                    for h in range(4):
                        last = mm(bank[:n, h:h + 1], q(h), nstate[t // 2][:, h:h + 1])
                    L0.close(last)
                if delta:
                    E["r_ready"].wait(pe)
                    bank = L1.open(pe)
                    for h in range(4):
                        last = mm(bank[:n, h * P:h * P + P], UI[f][:n, h, :n], TM[:n, vchunk + h, :])
                    L1.close(last)
                    E["vn_ready"].wait(pe)
                v = (lambda h: YI[f][:n, h, :]) if delta else (lambda h: TM[:n, vchunk + h, :])
                E["st_ready"].wait(pe)
                bank = L0.open(pe)
                for h in range(4):
                    last = mm(bank[:n, h * P:h * P + P], ST[:n, h, :n], v(h))
                L0.close(last)
                E["kw_ready"].wait(pe)
                bank = L0.open(pe)
                for h in range(4):
                    last = mm(bank[:, h * P:h * P + P], kw[:n, h, :], v(h))
                L0.close(last)
                if mlstm:
                    bank = L0.open(pe)
                    for h in range(4):
                        last = mm(bank[:, h:h + 1], kw[:n, h, :], ones[:n, 0:1])
                    L0.close(last)

            def finish_half(t, f):
                E["y_ready"].wait(pe)
                n = N_TOK[t]
                bank = L1.open(pe)
                for h in range(4):
                    last = flip(bank[:, h * P:h * P + n], Yout[:n, 4 * f + h, :], n)
                L1.close(last)

            def cumulate(w):
                E["lf_ready"].wait(pe)
                bank = L0.open(pe)
                L0.close(mm(bank[:, 0:3 * w], tri_incl, lg[:, 0:3 * w]))

            def layer_ab():
                norm()
                small_projection(8, 0, 2, beside=range(1))
                for c in range(1, 16):
                    project(c, L1)
                    if c == 4:
                        cumulate(4)
                const_in.wait(pe, 16)
                E["z_ready"].wait(pe)
                for t in range(TILES):
                    n, c = N_TOK[t], COL[t]
                    beside = BESIDE[t]
                    to_tokens(t, (1, 2, 3))
                    row_broadcast(n)
                    for ch in beside[0]:
                        project(ch, background)
                    E["gm_ready"].wait(pe)
                    last_row(t, 8)
                    for ch in beside[1]:
                        project(ch, background)
                    E["state_ready"].wait(pe)
                    half(t, 0, lambda h: zT[:, h, c:c + n], lambda h: zT[:, 4 + h, c:c + n], 8, mlstm=True,
                         beside=beside[2])
                    for ch in beside[3]:
                        project(ch, background)
                    finish_half(t, 0)
                E["z_ready"].wait(pe)
                for t in range(TILES):
                    n, c = N_TOK[t], COL[t]
                    to_tokens(t, (4, 5, 6))
                    if t:
                        for k in range(4):
                            output_part(t - 1, k)
                    else:
                        for ch in (28, 29):
                            project(ch, background)
                    E["rot_ready"].wait(pe)
                    for g, base in ((0, 0), (1, 4)):
                        bank = lanes[g].open(pe)
                        for h in range(4):
                            last = flip(bank[:, h * P:h * P + n], rot(base + h)[:n], n)
                        lanes[g].close(last)
                    E["qkT_dve"].wait(pe)
                    E["qkT_act"].wait(pe)
                    half(t, 1, lambda h: qT[0][:, h, :n], lambda h: kT[0][:, h, :n], 24)
                    if not t:
                        for ch in (30, 31):
                            project(ch, background)
                        E["z_ready"].wait(pe)
                    to_tokens(t, (7,))
                    if t:
                        for k in range(4, 8):
                            output_part(t - 1, k)
                    finish_half(t, 1)
                scratch_free.append((L1.full.sem, L1.full.made))
                output_sample()

            def rot(c):
                return AT[c // 4][:, c % 4, :]

            def layer_c():
                norm()
                small_projection(16, 2, 6, beside=range(1))
                for c in range(1, 24):
                    project(c, L1)
                    if c == 4:
                        cumulate(8)
                E["z_ready"].wait(pe)
                for t in range(TILES):
                    n, c = N_TOK[t], COL[t]
                    to_tokens(t, range(6))
                    if t:
                        for k in range(5):
                            output_part(t - 1, k)
                    else:
                        project_gates(t, 6, range(KT), None)
                    for i, base in enumerate((0, 4, 8, 12)):
                        E["qkn_ready"].wait(pe)
                        lane = lanes[i % 2]
                        bank = lane.open(pe)
                        for h in range(4):
                            last = flip(bank[:, h * P:h * P + n], TM[:n, base + h, :], n)
                        lane.close(last)
                    E["qkT_dve"].wait(pe)
                    E["qkT_act"].wait(pe)
                    last_row(t, 8)
                    for f in range(2):
                        row_broadcast(n, L1, masked=True, src=(tmp, Sm)[f])
                    gates = None
                    for f in range(2):
                        bank = L0.open(pe)
                        for h in range(4):
                            last = mm(bank[:n, h * P:h * P + n], kT[f][:, h, :n], kT[f][:, h, :n])
                        L0.close(last)
                        if t < 2:
                            gates = project_gates(t, 7 - t, range(4 * f, 4 * f + 4), gates)
                        else:
                            project_gates(t, 6 + f, range(KT), None)
                        E["a_ready"].wait(pe)
                        bank = L1.open(pe)
                        for h in range(4):
                            last = flip(bank[:n, h * P:h * P + n], tmp[:n, h, :n], n)
                        L1.close(last)
                    levels = 6 if n == 128 else 4
                    for lv in range(levels):
                        for f in range(2):
                            E["tu_ready"].wait(pe)
                            bank = L0.open(pe)
                            for h in range(4):
                                last = mm(bank[:n, h * P:h * P + n], AT[f][:n, h, :n], TI[f][:n, h, :n])
                            L0.close(last)
                        for f in range(2):
                            E["yi_ready"].wait(pe)
                            if lv < levels - 1:
                                bank = L0.open(pe)
                                for h in range(4):
                                    last = mm(bank[:n, h * P:h * P + n], UI[f][:n, h, :n], YI[f][:n, h, :n])
                                L0.close(last)
                            bank = L0.open(pe)
                            for h in range(4):
                                last = mm(bank[:n, h * P:h * P + n], YI[f][:n, h, :n], UI[f][:n, h, :n])
                            L0.close(last)
                    for f in range(2):
                        E["tu_ready"].wait(pe)
                    E["state_ready"].wait(pe)
                    for f in range(2):
                        if t == 1:
                            gates = project_gates(t, 7, range(4 * f, 4 * f + 4), gates)
                        half(t, f, lambda h: qT[f][:, h, :n], lambda h: kT[f][:, h, :n], 16 + 4 * f, delta=True)
                    if t:
                        for k in range(5, 8):
                            output_part(t - 1, k)
                    for f in range(2):
                        finish_half(t, f)
                scratch_free.append((L1.full.sem, L1.full.made))
                output_sample()

            def experts(l):
                norm()
                small_projection(36, 1 + 2 * l, 4)
                E["choice_ready"].wait(pe)
                M = route[:, 0:96].rearrange("p (t e) -> p t e", e=NEXP)
                bank = L0.open(pe)
                for t in range(TILES):
                    last = mm(bank[0:NEXP, 0:1], M[:, t, :], ones[:, 0:1], t == 0, t == 2)
                L0.close(last)
                bank = L0.open(pe)
                for t in range(TILES):
                    for s in range(t + 1):
                        last = mm(bank[:, 32 * t:32 * t + 32], tri_strict if s == t else ones, M[:, s, :],
                                  s == 0, s == t)
                L0.close(last)
                E["nb_ready"].wait(pe)
                nbc, nbb = route[0:NEXP, 700:701], route[0:NEXP, 704:832]
                bank = L0.open(pe)
                L0.close(mm(bank[0:NEXP, 0:1], tri_incl[0:NEXP, 0:NEXP], nbc))
                bank = L0.open(pe)
                L0.close(mm(bank[:, 0:NEXP], nbb, tri_strict[0:NEXP, 0:NEXP]))
                E["list_ready"].wait(pe)
                bank = L0.open(pe)
                L0.close(mm(bank[0:1, 0:MAX_BLOCKS], ones[0:NEXP, 0:1], route[0:NEXP, 832:832 + MAX_BLOCKS]))
                E["blocks_ready"].wait(pe)
                m = moe[l]
                nb = nblk_reg(pe)
                for used in ("gate_used", "up_used", "down_used"):
                    pe.sem_inc(m[used], 2)

                def gather(count):
                    pe.wait_ge(m["onehot"], count)
                    for k in range(KT):
                        for t in range(TILES):
                            n = N_TOK[t]
                            last = mm(banks[k // 4][:, k % 4 * P:k % 4 * P + P], HN[:n, t, k * P:k * P + P],
                                      oh[0][:n, t, :], t == 0, t == 2)
                    last.then_inc(m["gathered"], 1)

                def gate_up(u, b):
                    pe.wait_ge(m["w_in"][3 * u], 16 * b + 16)
                    pe.wait_ge(m["w_in"][3 * u + 1], 16 * b + 16)
                    w = [W[:, 3 * u + s, :].rearrange("p (k n) -> p k n", k=KT) for s in range(2)]
                    for k in range(KT):
                        for s, used in ((0, "gate_used"), (1, "up_used")):
                            ins = mm(banks[2 + u][BLK * s:BLK * s + BLK, :], xg[:, k, u, :], w[s][:, k, :],
                                     k == 0, k == KT - 1)
                            if k == KT - 1:
                                ins.then_inc(m[used], 1)

                def flip_hidden(u, i):
                    pe.wait_ge(m["hidden"], i + 1)
                    for j in range(4):
                        last = mm(banks[4 + u][:, j * BLK:j * BLK + BLK], hid[u][:, j * P:j * P + P], ident[:BLK, :BLK])
                    last.then_inc(m["flipped"], 1)

                def down(b):
                    pe.wait_ge(m["hiddenT"], 2 * b + 2)
                    for u in range(2):
                        pe.wait_ge(m["w_in"][3 * u + 2], 16 * b + 16)
                    pe.wait_ge(m["added"], SCATTERS * b)
                    for h in range(2):
                        for j in range(4):
                            for u in range(2):
                                w = W[:, 3 * u + 2, :].rearrange("p (k n) -> p k n", k=4)
                                last = mm(banks[6 + h][BLK * u:BLK * u + BLK, :], hidT[u][:, j * BLK:j * BLK + BLK],
                                          w[:, j, 512 * h:512 * h + 512], j == 0, j == 3)
                        last.then_inc(m["down_used"] if h else m["half_down"], 2 if h else 1)

                def scatter(b):
                    pe.wait_ge(m["share"], b + 1)
                    for i in range(4):
                        t, h = i % 2, i // 2
                        if t == 0:
                            pe.wait_ge(m["y"][h], b + 1)
                        mm(banks[4 + i][:, :], share[0][:, P * t:P * t + P], ys[h]).then_inc(m["scattered"], 1)
                    pe.wait_ge(m["added"], SCATTERS * b + 1)
                    for q in range(4):
                        last = mm(banks[4][32 * q:32 * q + 32, 0:256], share[0][:, 2 * P:N_ALL],
                                  ys[q // 2][:, 256 * (q % 2):256 * (q % 2) + 256])
                    last.then_inc(m["scattered"], 1)

                gather(1)
                for t in range(TILES):
                    n = N_TOK[t]
                    E["rows_diag"].wait(pe)
                    E["rows_wide"].mark(mm(banks[5 + t][:, 0:4 * n].rearrange("p (j n) -> p j n", j=4), ones[:n, :],
                                           TM[:n, 4 * t:4 * t + 4, 0:n]))
                with pe.Fori(0, nb) as b:
                    pe.wait_ge(m["xg_dve"], b + 1)
                    pe.wait_ge(m["xg_act"], b + 1)
                    gate_up(0, b)
                    gate_up(1, b)
                    flip_hidden(0, 2 * b)
                    gather(b + 2)
                    flip_hidden(1, 2 * b + 1)
                    down(b)
                    scatter(b)

            const_head_in.wait(pe, 16)
            layer_ab()
            experts(0)
            layer_c()
            experts(1)

        @block.scalar
        def _(act):
            do = InOrder(act, order["act"])

            def norm():
                for t in range(TILES):
                    n = N_TOK[t]
                    x_ready.wait(act)
                    do(nc.scalar.activation(junk[:n, :], X[:n, t, :], ACT.Square, accum_out=sumsq[:n, t:t + 1]),
                       ss_ready)

            def take_transposed(event):
                for t in range(TILES):
                    n, c = N_TOK[t], COL[t]
                    take_one(t, event)

            def take_one(t, event):
                n, c = N_TOK[t], COL[t]
                bank = L1.take(act)
                do(nc.scalar.copy(HT[:, 4:8, c:c + n], heads4(bank[:, :])[:, :, :n]), L1.taken)
                event.mark(act.nop())

            def log_gate(w, e):
                E["gate_exp_in"].wait(act)
                do(nc.scalar.activation(t24b[:, 0:3 * w], t24a[:, 0:3 * w], ACT.Exp, scale=-1.0))
                do(nc.scalar.activation(t24b[:, 0:3 * w], t24b[:, 0:3 * w], ACT.Ln, bias=ones[:, 0:1]))
                if e:
                    do(nc.scalar.activation(t24c[:, :], beta[:, :], ACT.Exp, scale=-1.0))
                    do(nc.scalar.activation(gb1, gb1, ACT.Exp))
                E["gate_exp"].mark(act.nop())

            def to_tokens(t, groups, free=True):
                n = N_TOK[t]
                if not free:
                    E["tile_done"].wait(act)
                for g in groups:
                    bank = L1.take(act)
                    do(nc.scalar.copy(TM[:n, 4 * g:4 * g + 4, :], heads4(bank[:n, :])), L1.taken)
                E["tm_act"].mark(act.nop())

            def projected(c, lane, func=ACT.Copy, scale=1.0):
                bank = lane.take(act)
                do(nc.scalar.activation(zT[:, c, :], bank[:, 0:COLS], func, scale=scale), lane.taken)

            def take_gates(t, p):
                n, first = N_TOK[t], 24 + 4 * (p - 6)
                bank = background.take(act)
                if t < 2:
                    do(nc.scalar.activation(TM[:n, first:first + 4, :], heads4(bank[:n, :]), ACT.Silu),
                       background.taken)
                else:
                    for q in range(4):
                        do(nc.scalar.activation(TM[:n, first + q, :], bank[32 * q:32 * q + n, 0:P], ACT.Silu),
                           background.taken if q == 3 else None)
                E["gates_ready"].mark(act.nop())

            def y_T(t, f):
                n, c = N_TOK[t], COL[t]
                bank = L1.take(act)
                do(nc.scalar.copy(zT[:, 4 * f:4 * f + 4, c:c + n], heads4(bank[:, :])[:, :, :n]), L1.taken)
                E["yT_act"].mark(act.nop())

            def square_sums(src, scratch, out, event):
                for h in range(4):
                    ins = nc.scalar.activation(scratch[:, h], src[:, h], ACT.Square, accum_out=out[:, h:h + 1])
                    if h == 3:
                        do(ins, event)
                    else:
                        order["act"].mark(ins)

            def y_squares(n, f, scratch):
                E["y_done"].wait(act)
                square_sums(Yout[:n, 4 * f:4 * f + 4, :], scratch[:n], hss[:n, 4 * f:4 * f + 4], E["hss_act"])

            def scores_T(n):
                bank = L1.take(act)
                do(nc.scalar.copy(ST[:n, :, :n], heads4(bank[:n, :])[:, :, :n]), L1.taken)
                E["st_ready"].mark(act.nop())

            def layer_ab():
                norm()
                take_transposed(ht_act)
                log_gate(4, False)
                for c in range(16):
                    projected(c, L1, ACT.Sigmoid if c >= 12 else ACT.Copy, float(P) ** -0.5 if 4 <= c < 8 else 1.0)
                E["z_ready"].mark(act.nop())

                def beside(chunks):
                    for c in chunks:
                        projected(c, background)

                for t in range(TILES):
                    n = N_TOK[t]
                    to_tokens(t, (1, 3), free=t == 0)
                    beside(BESIDE[t][0])
                    E["ein_ready"].wait(act)
                    do(nc.scalar.activation(eout[:n, 0:12], ein[:n, 0:12], ACT.Exp))
                    do(nc.scalar.activation(eout[:, 12:16], ein[:, 12:16], ACT.Exp), E["eout_ready"])
                    for h in range(4):
                        do(nc.scalar.activation(GAM[0][:n, h, :n], GAM[1][:n, h, :n], ACT.Exp,
                                                bias=negg[:n, h:h + 1]))
                    E["p_ready"].mark(act.nop())
                    beside(BESIDE[t][1])
                    beside(BESIDE[t][2])
                    scores_T(n)
                    y_squares(n, 0, GAM[0])
                    beside(BESIDE[t][3])
                    y_T(t, 0)
                E["z_ready"].mark(act.nop())
                for t in range(TILES):
                    n = N_TOK[t]
                    to_tokens(t, (5,), free=False)
                    if not t:
                        for c in (28, 29):
                            projected(c, background, ACT.Silu)
                    bank = L1.take(act)
                    do(nc.scalar.copy(kT[0][:, :, :n], heads4(bank[:, :])[:, :, :n]), L1.taken)
                    E["qkT_act"].mark(act.nop())
                    scores_T(n)
                    y_squares(n, 1, GAM[0])
                    if not t:
                        for c in (30, 31):
                            projected(c, background, ACT.Silu)
                        E["z_ready"].mark(act.nop())
                    to_tokens(t, (7,))
                    y_T(t, 1)

            def layer_c():
                norm()
                take_transposed(ht_act)
                log_gate(8, True)
                for p in range(7):
                    if p < 6:
                        for c in range(4 * p, 4 * p + 4):
                            projected(c, L1)
                        E["conv_raw"].mark(act.nop())
                    if p >= 1:
                        q = p - 1
                        E["conv_done"].wait(act)
                        do(nc.scalar.activation(zT[:, 4 * q:4 * q + 4, PAD:COLS], convbuf[q % 2], ACT.Silu),
                           E["conv_used"])
                E["z_ready"].mark(act.nop())
                for t in range(TILES):
                    n = N_TOK[t]
                    to_tokens(t, (1, 3, 5), free=t == 0)
                    for g in range(2):
                        square_sums(TM[:n, 8 * g + 4:8 * g + 8, :], GAM[0][:n], hss[:n, 8 * g + 4:8 * g + 8],
                                    E["hss_act"])
                    if t == 0:
                        take_gates(t, 6)
                    for i in range(2):
                        bank = L1.take(act)
                        dst = (qT, kT)[i][1]
                        do(nc.scalar.copy(dst[:, :, :n], heads4(bank[:, :])[:, :, :n]), L1.taken)
                    E["qkT_act"].mark(act.nop())
                    E["ein_ready"].wait(act)
                    do(nc.scalar.activation(eout[:n, 0:16], ein[:n, 0:16], ACT.Exp))
                    do(nc.scalar.activation(eout[:, 16:24], ein[:, 16:24], ACT.Exp), E["eout_ready"])
                    for f in range(2):
                        bank = L1.take(act)
                        for h in range(4):
                            do(nc.scalar.activation(GAM[f][:n, h, :n], heads4(bank[:n, :])[:, h, :n], ACT.Exp,
                                                    bias=gm[:n, 4 * f + h:4 * f + h + 1]),
                               L1.taken if h == 3 else None)
                        E["p_ready"].mark(act.nop())
                    for f in range(2):
                        if f:
                            for p in ((7,), (6,), (6, 7))[t]:
                                take_gates(t, p)
                        bank = L1.take(act)
                        do(nc.scalar.copy(AT[f][:n, :, :n], heads4(bank[:n, :])[:, :, :n]), L1.taken)
                        E["at_ready"].mark(act.nop())
                    for f in range(2):
                        if t == 1 and f:
                            take_gates(t, 7)
                        scores_T(n)
                        bank = L1.take(act)
                        do(nc.scalar.copy(YI[f][:n, :, :], heads4(bank[:n, :])), L1.taken)
                        E["vn_ready"].mark(act.nop())
                        y_squares(n, f, GAM[f])
                    for f in range(2):
                        y_T(t, f)

            def experts(l):
                act.wait_ge(states_out, l + 1)
                norm()
                take_transposed(ht_act)
                E["logits_exp_in"].wait(act)
                do(nc.scalar.activation(route[:, 300:312], route[:, 300:312], ACT.Exp), E["logits_exp"])
                E["logits_exp_in"].wait(act)
                do(nc.scalar.activation(route[:, 320:323], route[:, 320:323], ACT.Exp), E["logits_exp"])
                E["blocks_ready"].wait(act)
                m = moe[l]
                nb = nblk_reg(act)

                def fetched(count):
                    act.wait_ge(m["gathered"], count)
                    nc.scalar.copy(xg[:, 4:8].rearrange("p k u s -> p (k u s)"), banks[1][:, :]
                                   ).then_inc(m["xg_act"], 1)

                fetched(1)
                with act.Fori(0, nb) as b:
                    for u in range(2):
                        i = 2 * b + u
                        act.wait_ge(m["gate_used"], i + 3)
                        nc.scalar.activation(sg[u], banks[2 + u][0:BLK, :], ACT.Silu).then_inc(m["silu"], 1)
                    fetched(b + 2)
                    act.wait_ge(m["half_down"], b + 1)
                    act.wait_ge(m["scattered"], SCATTERS * b)
                    nc.scalar.copy(ys[0], banks[6][:, :]).then_inc(m["y"][0], 1)

            layer_ab()
            experts(0)
            layer_c()
            experts(1)
            norm()

        @block.vector
        def _(dve):
            do = InOrder(dve, order["dve"])
            v = nc.vector

            def tt(out, i0, i1, op, event=None):
                do(v.tensor_tensor(out, i0, i1, op), event)

            def ts(out, i0, s1, s2=None, op0=ALU.mult, op1=ALU.bypass, event=None):
                if s2 is None:
                    do(v.tensor_scalar(out, i0, s1, None, op0), event)
                else:
                    do(v.tensor_scalar(out, i0, s1, s2, op0, op1), event)

            def cp(out, i, event=None):
                do(v.tensor_copy(out, i), event)

            def red(out, i, op=ALU.add, event=None):
                do(v.tensor_reduce(out, i, X_AXIS, op), event)

            def signal(event):
                event.mark(dve.nop())

            def by_head(out, i0, col, i1, op0, op1, event=None):
                for h in range(4):
                    ins = v.scalar_tensor_tensor(out=out[:, h], in0=i0[:, h], scalar=col[:, h:h + 1], in1=i1[:, h],
                                                 op0=op0, op1=op1)
                    if h == 3:
                        do(ins, event)
                    else:
                        order["dve"].mark(ins)

            def bc_last(ap, n):
                return ap.unsqueeze(len(ap.shape)).to_broadcast(list(ap.shape) + [n])

            def bc_mid(ap, n):
                return ap.unsqueeze(1).to_broadcast([ap.shape[0], n] + list(ap.shape[1:]))

            def norm(last=False, first=False):
                (gain0_in if first else gain_in).wait(dve, 16)
                for t in range(TILES):
                    n = N_TOK[t]
                    rs_ready.wait(dve)
                    do(v.scalar_tensor_tensor(out=HN[:n, t, :], in0=X[:n, t, :], scalar=rstd[:n, t:t + 1],
                                              in1=gain[:n, :], op0=ALU.mult, op1=ALU.mult),
                       E["hn_out"] if last else hn_ready)
                if not last:
                    signal(gain_used)
                    for t in range(TILES):
                        take_one(t, ht_dve)

            def take_one(t, event):
                n, c = N_TOK[t], COL[t]
                bank = L0.take(dve)
                cp(HT[:, 0:4, c:c + n], heads4(bank[:, :])[:, :, :n], L0.taken)
                signal(event)

            def small_product(w):
                bank = L0.take(dve)
                cp(small_T[:w, :], bank[:w, 0:COLS], L0.taken)
                signal(E["small_ready"])

            def gates(w):
                g3 = g16[:, 0:3 * w].rearrange("p (t w) -> p t w", w=w)
                do(v.memset(g16, 0.0))
                small_product(w)
                bank = L0.take(dve)
                cp(g3[:, 0:2, :], bank[:, 0:128].rearrange("p (t w) -> p t w", w=64)[:, :, 0:w])
                cp(g3[:32, 2, :], bank[:32, 128:128 + w], L0.taken)
                signal(small_used)
                return g3

            def to_tokens(t, groups):
                n = N_TOK[t]
                for g in groups:
                    bank = L0.take(dve)
                    cp(TM[:n, 4 * g:4 * g + 4, :], heads4(bank[:n, :]), L0.taken)
                signal(E["tm_dve"])
                E["tm_act"].wait(dve)

            def diag(col, n):
                tt(tmp[:n, :, :n], bc_mid(ident[:n, :n], 4), bc_last(col, n), ALU.mult, E["diag_ready"])

            def half(t, f, gam, wq, wkk, dec, kchunk, vchunk, mlstm=False, delta=False):
                n = N_TOK[t]
                st = states[t][:, 4 * f:4 * f + 4, :]
                y = Yout[:, 4 * f:4 * f + 4, :]
                bank = L0.take(dve)
                tt(Sm[:n, :, :n], heads4(bank[:n, :])[:, :, :n], gam, ALU.mult, L0.taken)
                signal(E["s_ready"])
                if delta:
                    bank = L0.take(dve)
                    by_head(tmp[:n], heads4(bank[:n, :]), wq, TM[:n, vchunk:vchunk + 4, :], ALU.mult, ALU.subtract,
                            L0.taken)
                    tt(TM[:n, vchunk:vchunk + 4, :], tmp[:n], bc_last(negbeta3[:n, t, 4 * f:4 * f + 4], P),
                       ALU.mult, E["r_ready"])
                tt(kw[:n], TM[:n, kchunk:kchunk + 4, :], bc_last(wkk, P), ALU.mult, E["kw_ready"])
                bank = L0.take(dve)
                tt(tmp[:n], heads4(bank[:n, :]), bc_last(wq, P), ALU.mult, L0.taken)
                if mlstm:
                    red(den[:n, :], Sm[:n, :, :n])
                    bank = L0.take(dve)
                    tt(den2[:n, :], bank[:n, 0:4], wq, ALU.mult, L0.taken)
                    tt(den[:n, :], den[:n, :], den2[:n, :], ALU.add)
                    ts(den2[:n, :], den[:n, :], -1.0)
                    tt(den[:n, :], den[:n, :], den2[:n, :], ALU.max)
                    tt(den[:n, :], den[:n, :], eout[:n, 4:8], ALU.max)
                    do(v.reciprocal(den[:n, :], den[:n, :]))
                bank = L0.take(dve)
                tt(y[:n], heads4(bank[:n, :]), tmp[:n], ALU.add, L0.taken)
                if mlstm:
                    tt(y[:n], y[:n], bc_last(den[:n, :], P), ALU.mult)
                signal(E["y_done"])
                bank = L0.take(dve)
                by_head(st, st, dec, heads4(bank[:, :]), ALU.mult, ALU.add, L0.taken)
                if mlstm:
                    ns = nstate[t // 2]
                    tt(ns, ns, dec, ALU.mult)
                    bank = L0.take(dve)
                    tt(ns, ns, bank[:, 0:4], ALU.add, L0.taken)

            def head_norm(t, halves, gates_c, gain_row):
                n = N_TOK[t]
                for f in halves:
                    g = TM[:n, gates_c[f]:gates_c[f] + 4, :]
                    tt(g, g, bc_mid(hgain[:n, gain_row, :], 4), ALU.mult)
                for f in halves:
                    y = Yout[:n, 4 * f:4 * f + 4, :]
                    g = TM[:n, gates_c[f]:gates_c[f] + 4, :]
                    E["hrs_ready"].wait(dve)
                    by_head(y, y, hrs[:n, 4 * f:4 * f + 4], g, ALU.mult, ALU.mult)
                    signal(E["y_ready"])

            def add_output(t):
                E["out_ready"].wait(dve)
                for p in range(2):
                    x = X[:, t, 512 * p:512 * p + 512]
                    tt(x, x, banks[6 + p][:, :], ALU.add)
                if t == 0:
                    signal(E["out_taken"])
                signal(x_ready)

            def add_output_sample():
                n = N_TOK[2]
                bank = L0.take(dve)
                for q in range(4):
                    tt(X[:n, 2, 256 * q:256 * q + 256], X[:n, 2, 256 * q:256 * q + 256],
                       bank[32 * q:32 * q + n, 0:256], ALU.add, L0.taken if q == 3 else None)
                signal(x_ready)

            lg4 = lg[:, 0:12].rearrange("p (t w) -> p t w", w=4)
            lg8 = lg.rearrange("p (t w) -> p t w", w=8)
            b4 = bcum[:, 0:12].rearrange("p (t w) -> p t w", w=4)
            b8 = bcum.rearrange("p (t w) -> p t w", w=8)
            beta3 = beta.rearrange("p (t w) -> p t w", w=8)
            negbeta3 = t24c.rearrange("p (t w) -> p t w", w=8)

            def layer_ab():
                norm(first=True)
                small_in[0].wait(dve, 32)
                g3 = gates(8)
                tt(g3, g3, bc_mid(gb1, 3), ALU.add)
                ab = t24a[:, 0:12].rearrange("p (t w) -> p t w", w=4)
                ts(ab, g3[:, :, 4:8], -1.0)
                tt(ab, ab, g3[:, :, 4:8], ALU.max, E["gate_exp_in"])
                ts(lg4, g3[:, :, 4:8], 0.0, op0=ALU.min)
                E["gate_exp"].wait(dve)
                tt(lg[:, 0:12], lg[:, 0:12], t24b[:, 0:12], ALU.subtract, E["lf_ready"])
                bank = L0.take(dve)
                cp(bcum[:, 0:12], bank[:, 0:12], L0.taken)
                a3 = acol[:, 0:12].rearrange("p (t w) -> p t w", w=4)
                tt(a3, g3[:, :, 0:4], b4, ALU.subtract)
                do(v.memset(state1, 0.0))
                do(v.memset(nstate[0], 0.0))
                do(v.memset(mprev[0], 0.0))
                state_in.wait(dve, 64)
                hgain_in.wait(dve, 32)
                const_in.wait(dve, 16)
                E["z_ready"].wait(dve)
                for t in range(TILES):
                    n, g = N_TOK[t], t // 2
                    mp = mprev[g]
                    to_tokens(t, (2,))
                    diag(a3[:n, t, :], n)
                    bank = L0.take(dve)
                    tt(GAM[1][:n, :, :n], heads4(bank[:n, :])[:, :, :n], bc_mid(cst("negmask")[:n, :n], 4),
                       ALU.add, L0.taken)
                    red(m1[:n, :], GAM[1][:n, :, :n], ALU.max)
                    tt(gm[:n, 0:4], m1[:n, :], mp[:n, :], ALU.max)
                    tt(gm[:n, 4:8], gm[:n, 0:4], b4[:n, t, :], ALU.add, E["gm_ready"])
                    ts(negg[:n, :], gm[:n, 0:4], -1.0)
                    bank = L0.take(dve)
                    cp(gl, bank[:, 0:8], L0.taken)
                    tt(ein[:n, 0:4], mp[:n, :], gm[:n, 0:4], ALU.subtract)
                    ts(ein[:n, 4:8], gm[:n, 4:8], -1.0)
                    tt(ein[:n, 8:12], a3[:n, t, :], gl[:n, 0:4], ALU.subtract)
                    tt(ein[:, 12:16], mp, gl[:, 0:4], ALU.subtract)
                    cp(mp, gl[:, 4:8], E["ein_ready"])
                    signal(E["state_ready"])
                    E["eout_ready"].wait(dve)
                    E["p_ready"].wait(dve)
                    half(t, 0, GAM[0][:n, :, :n], eout[:n, 0:4], eout[:n, 8:12], eout[:, 12:16], 4, 8, mlstm=True)
                    if t >= 1:
                        signal(E["state_done"])
                    head_norm(t, (0,), (12, 28), 0)
                    signal(E["tile_done"])
                E["z_ready"].wait(dve)
                for t in range(TILES):
                    n, g = N_TOK[t], t // 2
                    to_tokens(t, (4, 6))
                    for j in range(2):
                        cos = bc_mid(rotc[:n, t, j, :], 4)
                        sin = bc_mid(rots[:n, t, j, :], 4)
                        x1, x2 = TM[:n, 16 + 4 * j:20 + 4 * j, 0:64], TM[:n, 16 + 4 * j:20 + 4 * j, 64:128]
                        o, s = AT[j], TI[0]
                        tt(o[:n, :, 0:64], x1, cos, ALU.mult)
                        tt(s[:n, :, 0:64], x2, sin, ALU.mult)
                        tt(o[:n, :, 0:64], o[:n, :, 0:64], s[:n, :, 0:64], ALU.subtract)
                        tt(o[:n, :, 64:128], x1, sin, ALU.mult)
                        tt(s[:n, :, 0:64], x2, cos, ALU.mult)
                        tt(o[:n, :, 64:128], o[:n, :, 64:128], s[:n, :, 0:64], ALU.add)
                    cp(TM[:n, 20:24, :], AT[1][:n], E["rot_ready"])
                    bank = L0.take(dve)
                    cp(qT[0][:, :, :n], heads4(bank[:, :])[:, :, :n], L0.taken)
                    signal(E["qkT_dve"])
                    r = cst("ret_k")[:n, 4 * g:4 * g + 4]
                    half(t, 1, heads4(cst("ret_decay")[:n, :])[:, :, :n], cst("ret_q")[:n, :], r,
                         cst("ret_c")[:, 4 * g:4 * g + 4], 20, 24)
                    if t >= 1:
                        signal(E["state_done"])
                    to_tokens(t, ())
                    head_norm(t, (1,), (12, 28), 1)
                    signal(E["tile_done"])
                    if t:
                        add_output(t - 1)
                add_output_sample()

            def layer_c():
                norm()
                small_in[2].wait(dve, 96)
                g3 = gates(16)
                cp(beta3, g3[:, :, 0:8])
                x3 = g3[:, :, 8:16]
                tt(x3, x3, bc_mid(gb2, 3), ALU.add)
                ab = t24a.rearrange("p (t w) -> p t w", w=8)
                ts(ab, x3, -1.0)
                tt(ab, ab, x3, ALU.max, E["gate_exp_in"])
                ts(lg8, x3, 0.0, op0=ALU.max)
                E["gate_exp"].wait(dve)
                ts(beta, t24c, 1.0, op0=ALU.add)
                do(v.reciprocal(beta, beta))
                ts(t24c, beta, -1.0)
                tt(lg, lg, t24b, ALU.add)
                ts(lg, lg, -1.0)
                tt(lg8, lg8, bc_mid(gb1, 3), ALU.mult, E["lf_ready"])
                bank = L0.take(dve)
                cp(bcum, bank[:, 0:24], L0.taken)
                ts(acol, bcum, -1.0)
                a3 = acol.rearrange("p (t w) -> p t w", w=8)
                for p in range(6):
                    E["conv_raw"].wait(dve)
                    c4 = zT[:, 4 * p:4 * p + 4, :]
                    cp(c4[:, :, COL[2] - PAD:COL[2]], cconv[:, 4 * p:4 * p + 4, 4:7])
                    cp(tails[:, 4 * p:4 * p + 4, 0:3], c4[:, :, COL[2] - 2 * PAD:COL[2] - PAD])
                    cp(tails[:, 4 * p:4 * p + 4, 3:6], c4[:, :, COLS - PAD:COLS])
                    if p >= 2:
                        E["conv_used"].wait(dve)
                    for k in range(4):
                        for j in range(4):
                            ch, o = 4 * p + j, convbuf[p % 2][:, j, :]
                            tap = cconv[:, ch, k:k + 1]
                            src = zT[:, ch, k:k + COLS - PAD]
                            if k == 0:
                                ins = v.tensor_scalar(o, src, tap, None, ALU.mult)
                            else:
                                ins = v.scalar_tensor_tensor(out=o, in0=src, scalar=tap, in1=o,
                                                             op0=ALU.mult, op1=ALU.add)
                            if j == 3:
                                do(ins)
                            else:
                                order["dve"].mark(ins)
                    signal(E["conv_done"])
                signal(E["tails_done"])
                E["conv_used"].wait(dve, 2)
                dve.wait_ge(out_written.sem, 16 * 9)
                do(v.memset(state1, 0.0))
                state_in.wait(dve, 16)
                for t in range(TILES):
                    n, g = N_TOK[t], t // 2
                    if t == 0:
                        E["z_ready"].wait(dve)
                    to_tokens(t, (0, 2, 4))
                    for g in range(2):
                        qk = TM[:n, 8 * g:8 * g + 4, :]
                        tt(tmp[:n], qk, qk, ALU.mult)
                        red(hss[:n, 8 * g:8 * g + 4], tmp[:n], event=E["hss_dve"])
                    cp(gm[:n, :], b8[:n, t, :])
                    for g in range(2):
                        E["hrs_ready"].wait(dve)
                        if g == 0:
                            ts(hrs[:n, 0:8], hrs[:n, 0:8], float(P) ** -0.5)
                        for i in (2 * g, 2 * g + 1):
                            qk = TM[:n, 4 * i:4 * i + 4, :]
                            tt(qk, qk, bc_last(hrs[:n, 4 * i:4 * i + 4], P), ALU.mult)
                            signal(E["qkn_ready"])
                    for i in range(2):
                        bank = L0.take(dve)
                        cp((qT, kT)[i][0][:, :, :n], heads4(bank[:, :])[:, :, :n], L0.taken)
                    signal(E["qkT_dve"])
                    bank = L0.take(dve)
                    cp(gl, bank[:, 0:8], L0.taken)
                    cp(ein[:n, 0:8], gm[:n, :])
                    tt(ein[:n, 8:16], gl[:n, :], gm[:n, :], ALU.subtract)
                    cp(ein[:, 16:24], gl, E["ein_ready"])
                    for f in range(2):
                        tt((tmp, Sm)[f][:n, :, :n], bc_mid(ident[:n, :n], 4), bc_last(a3[:n, t, 4 * f:4 * f + 4], n),
                           ALU.mult, E["diag_ready"])
                    E["eout_ready"].wait(dve)
                    for f in range(2):
                        E["p_ready"].wait(dve)
                        bank = L0.take(dve)
                        if f:
                            E["at_ready"].wait(dve)
                        by_head(tmp[:n, :, :n], heads4(bank[:n, :])[:, :, :n], beta3[:n, t, 4 * f:4 * f + 4],
                                GAM[f][:n, :, :n], ALU.mult, ALU.mult, L0.taken)
                        signal(E["a_ready"])
                        tt(TI[f][:n, :, :n], tmp[:n, :, :n], bc_mid(merge[:n, 0, :n], 4), ALU.mult)
                        tt(TI[f][:n, :, :n], bc_mid(ident[:n, :n], 4), TI[f][:n, :, :n], ALU.subtract)
                    E["at_ready"].wait(dve)
                    for f in range(2):
                        tt(UI[f][:n, :, :n], AT[f][:n, :, :n], bc_mid(cst("merge1_t")[:n, :n], 4), ALU.mult)
                        tt(UI[f][:n, :, :n], bc_mid(ident[:n, :n], 4), UI[f][:n, :, :n], ALU.subtract,
                           E["tu_ready"])
                    levels = 6 if n == 128 else 4
                    for lv in range(levels):
                        for f in range(2):
                            bank = L0.take(dve)
                            tt(YI[f][:n, :, :n], heads4(bank[:n, :])[:, :, :n], bc_mid(merge[:n, lv + 1, :n], 4),
                               ALU.mult, L0.taken)
                            signal(E["yi_ready"])
                        for f in range(2):
                            for M in (TI[f], UI[f]) if lv < levels - 1 else (UI[f],):
                                bank = L0.take(dve)
                                tt(M[:n, :, :n], M[:n, :, :n], heads4(bank[:n, :])[:, :, :n], ALU.subtract,
                                   L0.taken)
                            signal(E["tu_ready"])
                    signal(E["state_ready"])
                    for f in range(2):
                        half(t, f, GAM[f][:n, :, :n], eout[:n, 4 * f:4 * f + 4], eout[:n, 8 + 4 * f:12 + 4 * f],
                             eout[:, 16 + 4 * f:20 + 4 * f], 8 + 4 * f, 16 + 4 * f, delta=True)
                    E["gates_ready"].wait(dve, 2)
                    if t >= 1:
                        signal(E["state_done"])
                    head_norm(t, (0, 1), (24, 28), 0)
                    signal(E["tile_done"])
                    if t:
                        add_output(t - 1)
                add_output_sample()

            def experts(l):
                dve.wait_ge(states_out, l + 1)
                norm()
                small_in[1 + 2 * l].wait(dve, 64)
                r = lambda o, w: route[:, o:o + w]
                t3 = lambda ap, w: ap.rearrange("p (t w) -> p t w", w=w)
                logit = t3(r(400, 108), 36)
                do(v.memset(r(400, 108), 0.0))
                small_product(36)
                bank = L0.take(dve)
                tt(logit[:, 0:2, :], t3(bank[:, 0:128], 64)[:, :, 0:36], bc_mid(rb, 2), ALU.add)
                tt(logit[:32, 2, :], bank[:32, 128:164], rb[:32, :], ALU.add, L0.taken)
                signal(small_used)
                grp, fine = logit[:, :, 0:4], logit[:, :, 4:36]
                gmax, gsum, psel = r(510, 3), r(513, 3), r(516, 3)
                eq = t3(r(520, 24), 8)
                idx = r(544, 3)
                ohg = t3(r(548, 12), 4)
                red(gmax, grp, ALU.max)
                tt(t3(r(300, 12), 4), grp, bc_last(gmax, 4), ALU.subtract, E["logits_exp_in"])
                E["logits_exp"].wait(dve)
                red(gsum, t3(r(300, 12), 4))
                do(v.reciprocal(psel, gsum))

                def first_max(vals, top, w, out):
                    e_ = eq[:, :, 0:w]
                    tt(e_, vals, bc_last(top, w), ALU.is_equal)
                    tt(e_, e_, bc_mid(cst("iota_m99")[:, 0:w], 3), ALU.mult)
                    red(idx, e_, ALU.min)
                    tt(out, bc_mid(cst("iota_m99")[:, 0:w], 3), bc_last(idx, w), ALU.is_equal)

                first_max(grp, gmax, 4, ohg)
                tt(ohg, ohg, bc_last(cst("valid"), 4), ALU.mult)
                fs, oh1, oh2 = t3(r(560, 24), 8), t3(r(584, 24), 8), t3(r(608, 24), 8)
                wide = r(900, 96)
                wide4 = wide.rearrange("p (t g j) -> p t g j", g=NGRP, j=EPG)
                tt(wide4, fine.rearrange("p t (g j) -> p t g j", j=EPG), bc_last(ohg, EPG), ALU.mult)
                red(fs, wide4.rearrange("p t g j -> p t j g"))
                max1, max2 = r(632, 3), r(636, 3)
                red(max1, fs, ALU.max)
                first_max(fs, max1, 8, oh1)
                do(v.scalar_tensor_tensor(out=r(640, 24), in0=r(584, 24), scalar=-BIG, in1=r(560, 24),
                                          op0=ALU.mult, op1=ALU.add))
                rest = t3(r(640, 24), 8)
                red(max2, rest, ALU.max)
                first_max(rest, max2, 8, oh2)
                tt(r(320, 3), max2, max1, ALU.subtract, E["logits_exp_in"])
                M = r(0, 96)
                Mk = [r(100, 96), r(200, 96)]
                for k, o in enumerate((oh1, oh2)):
                    m4 = Mk[k].rearrange("p (t g j) -> p t g j", g=NGRP, j=EPG)
                    tt(m4, bc_last(ohg, EPG), o.unsqueeze(2).to_broadcast([P, TILES, NGRP, EPG]), ALU.mult)
                tt(M, Mk[0], Mk[1], ALU.add, E["choice_ready"])
                E["logits_exp"].wait(dve)
                s = r(664, 3)
                ts(s, r(320, 3), 1.0, op0=ALU.add)
                do(v.reciprocal(s, s))
                tt(pw[0][:, 0:3], psel, s, ALU.mult)
                tt(pw[0][:, 3:6], pw[0][:, 0:3], r(320, 3), ALU.mult)
                bank = L0.take(dve)
                cp(r(668, 1)[0:NEXP], bank[0:NEXP, 0:1], L0.taken)
                ts(r(670, 5)[0:NEXP], cst("thresh")[0:NEXP, :], r(668, 1)[0:NEXP], op0=ALU.is_lt)
                red(r(700, 1)[0:NEXP], r(670, 5)[0:NEXP])
                ts(route[0:NEXP, 704:832], ones[0:NEXP, :], r(700, 1)[0:NEXP])
                signal(E["nb_ready"])
                bank = L0.take(dve)
                cp(wide, bank[:, 0:96], L0.taken)
                bank = L0.take(dve)
                cp(r(680, 1)[0:NEXP], bank[0:NEXP, 0:1], L0.taken)
                bank = L0.take(dve)
                do(v.scalar_tensor_tensor(out=r(1000, 32), in0=bank[:, 0:32], scalar=float(BLK), in1=cst("slot_more"),
                                          op0=ALU.mult, op1=ALU.add), L0.taken)
                ts(route[0:NEXP, 832:832 + MAX_BLOCKS], cst("iota_list")[0:NEXP, :], r(680, 1)[0:NEXP],
                   op0=ALU.is_ge)
                cp(route[0:NEXP, 832 + MAX_BLOCKS - 1:832 + MAX_BLOCKS], r(700, 1)[0:NEXP], E["list_ready"])
                ts(r(1500, 96), wide, float(BLK), op0=ALU.is_ge)
                tt(t3(r(1500, 96), NEXP), t3(r(1500, 96), NEXP), bc_mid(r(1000, 32), 3), ALU.mult)
                tt(wide, wide, r(1500, 96), ALU.add)
                tt(t3(wide, NEXP), t3(wide, NEXP), bc_mid(cst("slot_first"), 3), ALU.add)
                for k in range(2):
                    tt(r(1100, 96), Mk[k], wide, ALU.mult)
                    red(dk[:, 3 * k:3 * k + 3], t3(r(1100, 96), NEXP))
                    tt(dk[:, 3 * k:3 * k + 3], dk[:, 3 * k:3 * k + 3], cst("invalid"), ALU.add)
                bank = L0.take(dve)
                last_ = MAX_BLOCKS - 1
                ts(r(1200, MAX_BLOCKS)[0:1], bank[0:1, 0:MAX_BLOCKS], float(NEXP - 1), op0=ALU.min)
                tt(r(1200, MAX_BLOCKS)[0:1], r(1200, MAX_BLOCKS)[0:1], cst("list_first")[0:1], ALU.add)
                ts(r(1300, 1)[0:1], bank[0:1, last_:last_ + 1], float(NEXP), op0=ALU.add, event=L0.taken)
                cp(blocks_i[:, 0:last_], r(1200, last_)[0:1])
                cp(blocks_i[:, last_:last_ + 1], r(1300, 1)[0:1], E["blocks_ready"])
                m = moe[l]
                nb = nblk_reg(dve)
                iota = bc_mid(cst("iota_pair"), 3)

                def onehot(count):
                    for k in range(2):
                        v.tensor_tensor(oh[k], iota, bc_last(dk[:, 3 * k:3 * k + 3], 2 * BLK),
                                        ALU.is_equal).then_inc(m["step"], 1)
                    dve.wait_ge(m["step"], 3 * count + 2)
                    v.tensor_scalar(dk, dk, -2.0 * BLK, None, ALU.add).then_inc(m["step"], 1)
                    v.tensor_tensor(oh[0], oh[0], oh[1], ALU.add).then_inc(m["onehot"], 1)
                    dve.wait_ge(m["step"], 3 * count + 3)

                def fetched(count):
                    dve.wait_ge(m["gathered"], count)
                    v.tensor_copy(xg[:, 0:4].rearrange("p k u s -> p (k u s)"), banks[0][:, :]
                                  ).then_inc(m["xg_dve"], 1)

                def hidden(u, i):
                    dve.wait_ge(m["silu"], i + 1)
                    dve.wait_ge(m["up_used"], i + 3)
                    v.tensor_tensor(hid[u], sg[u], banks[2 + u][BLK:2 * BLK, :], ALU.mult).then_inc(m["hidden"], 1)

                def hidden_T(u, i):
                    dve.wait_ge(m["flipped"], i + 1)
                    v.tensor_copy(hidT[u], banks[4 + u][:, 0:256]).then_inc(m["hiddenT"], 1)

                def shares(b):
                    for k in range(2):
                        v.scalar_tensor_tensor(out=share[k], in0=rows[:, k, :], scalar=slot_at, in1=rows[:, 2 + k, :],
                                               op0=ALU.is_equal, op1=ALU.mult).then_inc(m["share_step"], 1)
                    dve.wait_ge(m["share_step"], 3 * b + 2)
                    v.tensor_scalar(slot_at, slot_at, 2.0 * BLK, None, ALU.add).then_inc(m["share_step"], 1)
                    v.tensor_tensor(share[0], share[0], share[1], ALU.add).then_inc(m["share"], 1)
                    dve.wait_ge(m["share_step"], 3 * b + 3)

                ident_k = bc_mid(ident, 2)
                pw3, dk3 = [ap.rearrange("p (k t) -> p k t", t=TILES) for ap in (pw[0], dk)]
                onehot(0)
                cp(slot_at, cst("slot"))
                for t in range(TILES):
                    n = N_TOK[t]
                    tt(TM[:n, 4 * t:4 * t + 2, 0:n], ident_k[:n, :, :n], bc_last(dk3[:n, :, t], n), ALU.mult)
                    tt(TM[:n, 4 * t + 2:4 * t + 4, 0:n], ident_k[:n, :, :n], bc_last(pw3[:n, :, t], n), ALU.mult,
                       E["rows_diag"])
                fetched(1)
                for t in range(TILES):
                    n = N_TOK[t]
                    E["rows_wide"].wait(dve)
                    cp(rows[:, :, P * t:P * t + n], banks[5 + t][:, 0:4 * n].rearrange("p (j n) -> p j n", j=4))
                with dve.Fori(0, nb) as b:
                    onehot(b + 1)
                    shares(b)
                    hidden(0, 2 * b)
                    hidden_T(0, 2 * b)
                    hidden(1, 2 * b + 1)
                    fetched(b + 2)
                    hidden_T(1, 2 * b + 1)
                    dve.wait_ge(m["down_used"], 2 * b + 4)
                    v.tensor_copy(ys[1], banks[7][:, :]).then_inc(m["y"][1], 1)
                    dve.wait_ge(m["added"], SCATTERS * b)
                    for i in range(4):
                        t, h = i % 2, i // 2
                        x = X[:, t, 512 * h:512 * h + 512]
                        dve.wait_ge(m["scattered"], SCATTERS * b + i + 1)
                        v.tensor_tensor(x, x, banks[4 + i][:, :], ALU.add).then_inc(m["added"], 1)
                    dve.wait_ge(m["scattered"], SCATTERS * b + 5)
                    for q in range(4):
                        x = X[:32, 2, 256 * q:256 * q + 256]
                        ins = v.tensor_tensor(x, x, banks[4][32 * q:32 * q + 32, 0:256], ALU.add)
                        ins.then_inc(m["added"] if q == 3 else m["quarter"], 1)
                    dve.wait_ge(m["quarter"], 3 * b + 3)
                dve.wait_ge(m["added"], nb * SCATTERS)
                for t in range(TILES):
                    signal(x_ready)

            for t in range(TILES):
                x_in[t].wait(dve, 16)
                signal(x_ready)
            do(v.memset(HT[:, :, 0:PAD], 0.0))
            do(v.memset(HT[:, :, COL[2] - PAD:COL[2]], 0.0))
            layer_ab()
            experts(0)
            layer_c()
            experts(1)
            norm(last=True)

        @block.sync
        def _(sp):
            def dma(dst, src, event):
                event.mark(sp.dma_start(dst, src), 16)

            def row(src):
                return src.partition_broadcast(P)

            dma(const[:, 0:CONST_HEAD], a["const"][:, 0:CONST_HEAD], const_head_in)
            for t in range(TILES):
                if t == 1:
                    dma(gain[:], row(a["norm_mix"][0]), gain0_in)
                src = a["x_prompt"][0, 128 * t:128 * t + 128, :] if t < 2 else a["x_sample"][0]
                dma(X[:N_TOK[t], t, :], src, x_in[t])
            dma(small_w[:, :, 0:8], a["ab_w_in"][0][:, 2048:2056].rearrange("(k p) n -> p k n", p=P), small_in[0])
            dma(gb1, row(a["ab_gate_bias"][0]), small_in[0])

            def pieces(w_in, w_out, cols, layer):
                for p in range(10):
                    if layer and p < 4:
                        m = moe[0]
                        if p == 0:
                            sp.wait_ge(m["gate_used"], 2 * nb + 1)
                        elif p == 1:
                            sp.wait_ge(m["up_used"], 2 * nb + 1)
                        else:
                            sp.wait_ge(m["down_used"], 2 * nb + 2)
                    elif p >= 4:
                        sp.wait_ge(*piece_done[10 * layer + p - 4])
                    src = w_in[:, cols[p]:cols[p] + 512] if p < 8 else w_out[:, 512 * (p - 8):512 * (p - 7)]
                    dma(W[:, p % 4, :].rearrange("p (k n) -> p k n", k=KT),
                        src.rearrange("(k p) n -> p k n", p=P), piece_in[p % 4])
                    if not layer and p == 0:
                        dma(const[:, CONST_HEAD:], a["const"][:, CONST_HEAD:], const_in)
                        dma(hgain[:, 0, :], row(a["ab_norm_a"][0]), hgain_in)
                        dma(hgain[:, 1, :], row(a["ab_norm_b"][0]), hgain_in)

            LOADS = {0: ("moe_w_gate", "gate_used", 8), 1: ("moe_w_up", "up_used", 8),
                     2: ("moe_w_down", "down_used", 4)}

            def expert_piece(l, u, s, e):
                name, _, kk = LOADS[s]
                sp.dma_start(W[:, 3 * u + s, :].rearrange("p (k n) -> p k n", k=kk),
                             a[name][l, bass.ds(e, 1), :, :].rearrange("o (k p) n -> p (o k) n", p=P)
                             ).then_inc(moe[l]["w_in"][3 * u + s], 16)

            def experts(l):
                m = moe[l]
                for u, s, free in ((0, 2, piece_done[10 * l + 6]), (1, 0, piece_done[10 * l + 7]),
                                   (1, 1, scratch_free[l]), (1, 2, scratch_free[l]),
                                   (0, 0, piece_done[10 * l + 8]), (0, 1, piece_done[10 * l + 9])):
                    sp.wait_ge(*free)
                    expert_piece(l, u, s, u)
                E["blocks_ready"].wait(sp)
                nb = nblk_reg(sp)
                with sp.Fori(1, nb) as b:
                    e = [sp.value_load(blocks_i[0:1, bass.ds(2 * b + u, 1)], min_val=0, max_val=NEXP - 1)
                         for u in range(2)]
                    for u, s in ((0, 0), (0, 1), (1, 0), (1, 1), (0, 2), (1, 2)):
                        sp.wait_ge(m[LOADS[s][1]], 2 * b + u + 1)
                        expert_piece(l, u, s, e[u])
                return nb

            pieces(a["ab_w_in"][0], a["ab_w_out"][0],
                   [512 * i for i in range(4)] + [2056 + 512 * i for i in range(4)], 0)
            nb = experts(0)
            pieces(a["c_w_in"][0], a["c_w_out"][0],
                   [512 * i for i in range(6)] + [3088, 3600], 1)
            experts(1)
            for t in range(TILES):
                E["hn_out"].wait(sp)
                dst = a["y_prompt"][0, 128 * t:128 * t + 128, :] if t < 2 else a["y_sample"][0]
                dma(dst, HN[:N_TOK[t], t, :], y_written)
            sp.wait_ge(y_written.sem, 16 * 3)

        @block.gpsimd
        def _(pool):
            do = InOrder(pool, order["pool"])

            def load(dst, src, event):
                event.mark(pool.dma_start(dst, src), 16)

            def store(dst, src):
                out_written.made += 16
                pool.dma_start(dst, src).then_inc(out_written.sem, 16)

            def power(dst, src, scale, n, w, ready, done):
                ready.wait(pool)
                do(nc.gpsimd.tensor_scalar(src, src, scale, EPS, ALU.mult, ALU.add))
                do(nc.gpsimd.tensor_tensor(dst, src, cst("half_neg")[:n, 0:w], ALU.pow), done)

            def norm(k):
                for t in range(TILES):
                    n = N_TOK[t]
                    power(rstd[:n, t:t + 1], sumsq[:n, t:t + 1], 1.0 / D, n, 1, ss_ready, rs_ready)
                if k < 4:
                    gain_used.wait(pool)
                    g = (a["norm_mix"], a["norm_ffn"])[(k + 1) % 2][(k + 1) // 2] if k < 3 else a["norm_final"]
                    load(gain[:], g.partition_broadcast(P), gain_in)

            def router_weights(l):
                small_used.wait(pool)
                load(small_w[:, :, 0:4], a["moe_w_grp"][l].rearrange("(k p) n -> p k n", p=P), small_in[1 + 2 * l])
                load(small_w[:, :, 4:36], a["moe_w_exp"][l].rearrange("(k p) n -> p k n", p=P), small_in[1 + 2 * l])
                load(rb[:, 0:4], a["moe_b_grp"][l].partition_broadcast(P), small_in[1 + 2 * l])
                load(rb[:, 4:36], a["moe_b_exp"][l].partition_broadcast(P), small_in[1 + 2 * l])

            load(mprev[1], a["state_mlstm_m"][0, 0].partition_broadcast(P), state_in)
            load(nstate[1], a["state_n_t"], state_in)
            load(state2[:, 0:4, :], a["state_mlstm_c"][0, 0].rearrange("h k v -> k h v"), state_in)
            load(state2[:, 4:8, :], a["state_ret"][0, 0].rearrange("h k v -> k h v"), state_in)
            const_head_in.wait(pool, 16)
            norm(0)
            router_weights(0)
            for f in range(2):
                for t in range(TILES):
                    n, h = N_TOK[t], slice(4 * f, 4 * f + 4)
                    power(hrs[:n, h], hss[:n, h], 1.0 / P, n, 4, E["hss_act"], E["hrs_ready"])
                    if t >= 1:
                        E["state_done"].wait(pool)
                        g = t - 1
                        store(a["out_ret" if f else "out_c"][g].rearrange("h k v -> k h v"), states[t][:, h, :])
                        if not f:
                            store(a["out_n"][g], nstate[g])
                            store(a["out_m"][g], mprev[g][0:1, :])
            pool.wait_ge(out_written.sem, 16 * 8)
            nc.gpsimd.sem_inc(states_out, 1)
            for l in range(2):
                norm(2 * l + 1)
                if l == 0:
                    load(state2[:, :, :], a["state_gdn"][0, 0].rearrange("h k v -> k h v"), state_in)
                    load(gb1, a["c_a_log"][0].partition_broadcast(P), small_in[2])
                    load(gb2, a["c_dt_bias"][0].partition_broadcast(P), small_in[2])
                    load(hgain[:, 0, :], a["c_norm"][0].partition_broadcast(P), small_in[2])
                    small_used.wait(pool)
                    load(small_w[:, :, 0:16], a["c_w_in"][0][:, 3072:3088].rearrange("(k p) n -> p k n", p=P),
                         small_in[2])
                if l == 0:
                    E["blocks_ready"].wait(pool)
                    nb = nblk_reg(pool)
                    pool.wait_ge(moe[l]["down_used"], 2 * nb + 2)
                    do(pool.nop())
                    load(cconv[:, :, 0:4], a["conv_taps"], small_in[2])
                    load(cconv[:, :, 4:7], a["conv_state"], small_in[2])
                    norm(2)
                    router_weights(1)
                    E["tails_done"].wait(pool)
                    store(a["out_tails"], tails)
                    for t in range(TILES):
                        n = N_TOK[t]
                        for h in (slice(0, 8), slice(8, 16)):
                            E["hss_act"].wait(pool)
                            power(hrs[:n, h], hss[:n, h], 1.0, n, 8, E["hss_dve"], E["hrs_ready"])
                        for h in (slice(0, 4), slice(4, 8)):
                            power(hrs[:n, h], hss[:n, h], 1.0 / P, n, 4, E["hss_act"], E["hrs_ready"])
                        if t >= 1:
                            E["state_done"].wait(pool)
                            store(a["out_gdn"][t - 1].rearrange("h k v -> k h v"), states[t])
                    pool.wait_ge(out_written.sem, 16 * 11)
                    nc.gpsimd.sem_inc(states_out, 1)
            norm(4)


_OUTS = {"y_prompt": (1, 256, 1024), "y_sample": (1, 32, 1024), "out_c": (2, 4, 128, 128), "out_n": (2, 128, 4),
         "out_m": (2, 1, 4), "out_ret": (2, 4, 128, 128), "out_gdn": (2, 8, 128, 128), "out_tails": (128, 24, 6)}
_IN = ["x_prompt", "x_sample", "state_mlstm_c", "state_mlstm_m", "state_ret", "state_gdn", "norm_mix", "norm_ffn",
       "norm_final", "ab_w_in", "ab_gate_bias", "ab_w_out", "ab_norm_a", "ab_norm_b", "c_w_in", "c_a_log",
       "c_dt_bias", "c_norm", "c_w_out", "moe_w_grp", "moe_b_grp", "moe_w_exp", "moe_b_exp", "moe_w_gate",
       "moe_w_up", "moe_w_down"]


def constants():
    import numpy as np

    f = np.float32
    i = np.arange(P)
    row, col = i[:, None], i[None, :]
    c = {
        "ident": row == col, "tri_incl": row <= col, "tri_strict": row < col, "ones": np.ones((P, P)),
        "negmask": np.where(col <= row, 0.0, -BIG),
        "merge": np.concatenate([(row // (2 * s) == col // (2 * s)) & (row // s % 2 == 1) & (col // s % 2 == 0)
                                 for s in (1, 2, 4, 8, 16, 32, 64)], 1),
        "merge1_t": (row // 2 == col // 2) & (row % 2 == 0) & (col % 2 == 1),
        "iota_pair": np.tile(np.arange(2 * BLK), (P, 1)), "iota_m99": np.tile(np.arange(8) - 99, (P, 1)),
        "valid": np.stack([i >= 0, i >= 0, i < N_TOK[2]], 1),
        "invalid": np.stack([i * 0, i * 0, np.where(i < N_TOK[2], 0, 1e6)], 1),
        "thresh": np.tile(BLK * np.arange(1, 6), (P, 1)), "iota_list": np.tile(np.arange(MAX_BLOCKS) - NEXP, (P, 1)),
        "list_first": np.tile(np.where(np.arange(MAX_BLOCKS) < NEXP, np.arange(MAX_BLOCKS), 0), (P, 1)),
        "slot_first": np.tile(BLK * np.arange(NEXP), (P, 1)),
        "slot": i[:, None] - 2 * BLK,
        "slot_more": np.tile(BLK * (NEXP - 1 - np.arange(NEXP)), (P, 1)),
        "half_neg": np.full((P, 16), -0.5),
    }
    lg = np.log(f(1.0) - f(2.0) ** (f(-5.0) - np.arange(4, dtype=f))).astype(f)
    rel = (row - col).astype(f)
    c["ret_decay"] = np.concatenate([np.where(rel >= 0, np.exp(np.where(rel >= 0, rel, f(0)) * g), 0) for g in lg], 1)
    c["ret_q"] = np.exp((i[:, None] + 1).astype(f) * lg)
    c["ret_k"] = np.concatenate([np.exp(np.minimum(n - 1 - i, P)[:, None].astype(f) * lg) for n in (128, 32)], 1)
    c["ret_c"] = np.concatenate([np.tile(np.exp(f(n) * lg), (P, 1)) for n in (128, 32)], 1)
    inv = f(10000.0) ** (-np.arange(64, dtype=f) / f(64))
    cos, sin = [], []
    for t in range(TILES):
        pos = (128 * t + i).astype(f)
        ang = (pos[:, None] * inv[None, :]).astype(f)
        for scale in (f(1.0), f(P) ** f(-0.5)):
            cos.append(np.cos(ang) * scale)
            sin.append(np.sin(ang) * scale)
    c["rot_cos"], c["rot_sin"] = np.concatenate(cos, 1), np.concatenate(sin, 1)
    return np.concatenate([np.asarray(c[n], f).reshape(P, w) for n, w in _SIZES], 1)


def kernel(**inputs):
    import numpy as np
    import concourse.bacc as bacc
    from concourse.bass_utils import run_bass_kernel_spmd

    nc = bacc.Bacc("TRN2", target_bir_lowering=False, num_devices=1)
    x = {k: np.ascontiguousarray(inputs[k]) for k in _IN}
    x["const"] = constants()
    x["conv_taps"] = np.ascontiguousarray(np.asarray(inputs["c_conv_w"])[0].reshape(4, 24, P).transpose(2, 1, 0))
    x["conv_state"] = np.ascontiguousarray(
        np.asarray(inputs["state_gdn_conv"])[0, 0].reshape(3, 24, P).transpose(2, 1, 0))
    x["state_n_t"] = np.ascontiguousarray(np.asarray(inputs["state_mlstm_n"])[0, 0].T)
    arrays = {f"in_{k}": v for k, v in x.items()}
    a = {k: nc.dram_tensor(f"in_{k}", v.shape, F32, kind="ExternalInput").ap() for k, v in x.items()}
    for k, s in _OUTS.items():
        a[k] = nc.dram_tensor(k, s, F32, kind="ExternalOutput").ap()
    trunk(nc, a)
    r = run_bass_kernel_spmd(nc, [arrays], core_ids=[0]).results[0]
    tails = r["out_tails"].transpose(2, 1, 0).reshape(2, 1, 1, 3, 3072)
    c, n, m = r["out_c"], r["out_n"].transpose(0, 2, 1), r["out_m"]
    sides = [(c[g][None, None], n[g][None, None], m[g][None], r["out_ret"][g][None, None],
              r["out_gdn"][g][None, None], tails[g]) for g in range(2)]
    return (r["y_prompt"], r["y_sample"], *sides[0], *sides[1])
```
